# Optimizing a Trainium2 kernel written in Bass

```python
import math
import jax, jax.numpy as jnp
from jax import lax
import numpy as np

D_MODEL = 1024
BATCH = 1
SEQ = 512
DEPTH = 1

CHUNK = 64
SB_BLOCK = 128
SB_HEADS = 8
SB_HEAD_DIM = 64
SB_WIDTH = SB_HEADS * SB_HEAD_DIM
RET_HEADS = 8
RET_QK_DIM = 64
RET_V_DIM = 128
RET_QK_WIDTH = RET_HEADS * RET_QK_DIM
RET_V_WIDTH = RET_HEADS * RET_V_DIM
IN_COLS = 3 * SB_WIDTH + 2 * RET_QK_WIDTH + 2 * RET_V_WIDTH
N_BRANCHES = 2
ROPE_BASE = 10000.0
N_GROUPS = 4
EXPERTS_PER_GROUP = 4
N_EXPERTS = N_GROUPS * EXPERTS_PER_GROUP
TOP_K_IN_GROUP = 2
D_FF_EXPERT = 512
EPS = 1e-6


def rms_norm(x, g):
    xf = x.astype(jnp.float32)
    y = xf * lax.rsqrt(jnp.mean(xf * xf, axis=-1, keepdims=True) + EPS)
    return (y * g.astype(jnp.float32)).astype(x.dtype)

def to_heads(t, n_heads):
    b, s, _ = t.shape
    return t.reshape(b, s, n_heads, -1).transpose(0, 2, 1, 3)

def from_heads(t):
    b, h, s, d = t.shape
    return t.transpose(0, 2, 1, 3).reshape(b, s, h * d)

def rotary(x, positions):
    half = x.shape[-1] // 2
    inv_freq = ROPE_BASE ** (-jnp.arange(half, dtype=jnp.float32) / half)
    ang = positions.astype(jnp.float32)[:, None] * inv_freq[None, :]
    cos, sin = jnp.cos(ang), jnp.sin(ang)
    x1, x2 = x[..., :half], x[..., half:]
    return jnp.concatenate([x1 * cos - x2 * sin, x2 * cos + x1 * sin], axis=-1)

def stick_breaking_attention(q, k, v):
    s_len, d = q.shape[2], q.shape[3]
    scale = 1.0 / math.sqrt(d)
    outs = []
    for blk in range(s_len // SB_BLOCK):
        q0 = blk * SB_BLOCK
        k_end = q0 + SB_BLOCK
        qb = q[:, :, q0:k_end]
        kb = k[:, :, :k_end]
        vb = v[:, :, :k_end]
        z = jnp.einsum('bhqd,bhkd->bhqk', qb, kb) * scale
        t_idx = q0 + jnp.arange(SB_BLOCK)[:, None]
        s_idx = jnp.arange(k_end)[None, :]
        mask = s_idx < t_idx
        log_keep = jnp.where(mask, jax.nn.log_sigmoid(-z), 0.0)
        suffix = lax.cumsum(log_keep, axis=3, reverse=True) - log_keep
        weights = jnp.where(mask, jnp.exp(jax.nn.log_sigmoid(z) + suffix), 0.0)
        outs.append(jnp.einsum('bhqk,bhkd->bhqd', weights, vb))
    return jnp.concatenate(outs, axis=2)

def retention_chunkwise(q, k, v):
    b, h, s_len, dk = q.shape
    dv = v.shape[-1]
    nc = s_len // CHUNK
    log_gamma = jnp.log(1.0 - 2.0 ** (-5.0 - jnp.arange(h, dtype=jnp.float32)))
    idx = jnp.arange(CHUNK, dtype=jnp.float32)
    dist = jnp.abs(idx[:, None] - idx[None, :])
    d_intra = jnp.exp(log_gamma[:, None, None] * dist)
    qc = q.reshape(b, h, nc, CHUNK, dk)
    kc = k.reshape(b, h, nc, CHUNK, dk)
    vc = v.reshape(b, h, nc, CHUNK, dv)
    scores = jnp.einsum('bhncd,bhnmd->bhncm', qc, kc) * d_intra[None, :, None]
    intra = jnp.einsum('bhncm,bhnme->bhnce', scores, vc)
    k_decay = jnp.exp(log_gamma[:, None] * (CHUNK - 1 - idx)[None, :])
    kv = jnp.einsum('bhnmd,bhnme->bhnde', kc * k_decay[None, :, None, :, None], vc)
    chunk_decay = jnp.exp(log_gamma * CHUNK)[None, :, None, None]

    def step(state, kv_n):
        return state * chunk_decay + kv_n, state

    init = jnp.zeros((b, h, dk, dv), jnp.float32)
    _, prev = lax.scan(step, init, jnp.moveaxis(kv, 2, 0))
    prev = jnp.moveaxis(prev, 0, 2)
    q_decay = jnp.exp(log_gamma[:, None] * (idx + 1.0)[None, :])
    cross = jnp.einsum('bhncd,bhnde->bhnce', qc * q_decay[None, :, None, :, None], prev)
    return (intra + cross).reshape(b, h, s_len, dv)

def hierarchical_moe(xn, w_group_router, b_group_router, w_expert_router, b_expert_router,
                     w_exp_gate, w_exp_up, w_exp_down):
    b, s_len, d = xn.shape
    xt = xn.reshape(b * s_len, d)
    n_tok = xt.shape[0]
    group_logits = (xt @ w_group_router + b_group_router).astype(jnp.float32)
    group_probs = jax.nn.softmax(group_logits, axis=-1)
    p_group, g_sel = lax.top_k(group_probs, 1)
    expert_logits = (xt @ w_expert_router + b_expert_router).astype(jnp.float32)
    expert_logits = expert_logits.reshape(n_tok, N_GROUPS, EXPERTS_PER_GROUP)
    in_group = jnp.take_along_axis(expert_logits, g_sel[:, :, None], axis=1)[:, 0]
    top_vals, top_idx = lax.top_k(in_group, TOP_K_IN_GROUP)
    gate = jax.nn.softmax(top_vals, axis=-1) * p_group
    expert_id = g_sel * EXPERTS_PER_GROUP + top_idx
    combine = jnp.sum(jax.nn.one_hot(expert_id, N_EXPERTS, dtype=jnp.float32) * gate[..., None], axis=1)
    combine = combine.astype(xt.dtype)
    y = jnp.zeros_like(xt)
    for e in range(N_EXPERTS):
        hidden = jax.nn.silu(xt @ w_exp_gate[e]) * (xt @ w_exp_up[e])
        y = y + combine[:, e:e + 1] * (hidden @ w_exp_down[e])
    return y.reshape(b, s_len, d)

def first_inputs(seed: int = 0) -> dict:
    key = jax.random.key(seed)
    ks = jax.random.split(key, 20)
    f32 = jnp.float32

    def w(k, shape, fan_in):
        return jax.random.normal(k, shape, f32) * (fan_in ** -0.5)

    def gain(k, shape):
        return 1.0 + 0.02 * jax.random.normal(k, shape, f32)

    L = DEPTH
    return {
        "x": jax.random.normal(ks[0], (BATCH, SEQ, D_MODEL), f32),
        "norm_mix_g": gain(ks[1], (L, D_MODEL)),
        "w_in": w(ks[2], (L, D_MODEL, IN_COLS), D_MODEL),
        "w_gate": w(ks[3], (L, D_MODEL, N_BRANCHES * D_MODEL), D_MODEL),
        "b_gate": 0.02 * jax.random.normal(ks[4], (L, N_BRANCHES * D_MODEL), f32),
        "w_sb_out": w(ks[5], (L, SB_WIDTH, D_MODEL), SB_WIDTH),
        "w_ret_out": w(ks[6], (L, RET_V_WIDTH, D_MODEL), RET_V_WIDTH),
        "ret_norm_g": gain(ks[7], (L, RET_V_WIDTH)),
        "w_out": w(ks[8], (L, D_MODEL, D_MODEL), D_MODEL),
        "norm_ffn_g": gain(ks[9], (L, D_MODEL)),
        "w_group_router": w(ks[10], (L, D_MODEL, N_GROUPS), D_MODEL),
        "b_group_router": 0.01 * jax.random.normal(ks[11], (L, N_GROUPS), f32),
        "w_expert_router": w(ks[12], (L, D_MODEL, N_EXPERTS), D_MODEL),
        "b_expert_router": 0.01 * jax.random.normal(ks[13], (L, N_EXPERTS), f32),
        "w_exp_gate": w(ks[14], (L, N_EXPERTS, D_MODEL, D_FF_EXPERT), D_MODEL),
        "w_exp_up": w(ks[15], (L, N_EXPERTS, D_MODEL, D_FF_EXPERT), D_MODEL),
        "w_exp_down": w(ks[16], (L, N_EXPERTS, D_FF_EXPERT, D_MODEL), D_FF_EXPERT),
        "norm_final_g": gain(ks[17], (D_MODEL,)),
    }

def first_block(x, norm_mix_g, w_in, w_gate, b_gate, w_sb_out, w_ret_out, ret_norm_g, w_out,
              norm_ffn_g, w_group_router, b_group_router, w_expert_router, b_expert_router,
              w_exp_gate, w_exp_up, w_exp_down, norm_final_g):
    h = x
    s_len = x.shape[1]
    positions = jnp.arange(s_len, dtype=jnp.int32)
    split_sizes = [SB_WIDTH, SB_WIDTH, SB_WIDTH, RET_QK_WIDTH, RET_QK_WIDTH, RET_V_WIDTH, RET_V_WIDTH]
    split_at = [int(i) for i in np.cumsum(split_sizes)[:-1]]
    for layer in range(DEPTH):
        xn = rms_norm(h, norm_mix_g[layer])
        proj = xn @ w_in[layer]
        sb_q, sb_k, sb_v, r_q, r_k, r_v, r_g = jnp.split(proj, split_at, axis=-1)
        y_sb = stick_breaking_attention(to_heads(sb_q, SB_HEADS).astype(jnp.float32),
                                        to_heads(sb_k, SB_HEADS).astype(jnp.float32),
                                        to_heads(sb_v, SB_HEADS).astype(jnp.float32))
        y_sb = from_heads(y_sb).astype(x.dtype) @ w_sb_out[layer]
        rq = rotary(to_heads(r_q, RET_HEADS).astype(jnp.float32), positions)
        rk = rotary(to_heads(r_k, RET_HEADS).astype(jnp.float32), positions) * (RET_QK_DIM ** -0.5)
        rv = to_heads(r_v, RET_HEADS).astype(jnp.float32)
        y_ret = retention_chunkwise(rq, rk, rv)
        y_ret = y_ret * lax.rsqrt(jnp.mean(y_ret * y_ret, axis=-1, keepdims=True) + EPS)
        y_ret = from_heads(y_ret) * ret_norm_g[layer].astype(jnp.float32)
        y_ret = (jax.nn.silu(r_g.astype(jnp.float32)) * y_ret).astype(x.dtype) @ w_ret_out[layer]
        gates = jax.nn.sigmoid(xn @ w_gate[layer] + b_gate[layer])
        g_sb, g_ret = jnp.split(gates, N_BRANCHES, axis=-1)
        h = h + (g_sb * y_sb + g_ret * y_ret) @ w_out[layer]
        hn = rms_norm(h, norm_ffn_g[layer])
        h = h + hierarchical_moe(hn, w_group_router[layer], b_group_router[layer],
                                 w_expert_router[layer], b_expert_router[layer],
                                 w_exp_gate[layer], w_exp_up[layer], w_exp_down[layer])
    return rms_norm(h, norm_final_g)


HEAD_DIM = 64
MIX_WIDTH = D_MODEL
N_HEADS_A = (MIX_WIDTH // 2) // HEAD_DIM
N_HEADS_B = (MIX_WIDTH // 2) // HEAD_DIM
D_NOPE = HEAD_DIM
D_ROPE = HEAD_DIM // 2
KV_RANK = 2 * HEAD_DIM
V_DIM = HEAD_DIM
IDX_HEADS = 8
IDX_DIM = HEAD_DIM
TOPK_MAX = 256
Q_BLOCK = 128
DILATED_PATTERNS = ((128, 1), (512, 4), (2048, 16))
CROSS_HEADS = 4
CROSS_HEAD_DIM = D_MODEL // CROSS_HEADS
MEM_TOKENS = 256
D_FF = 4 * D_MODEL
ROPE_THETA = 10000.0
NORM_EPS = 1e-6

IN_SIZES = (N_HEADS_A * D_NOPE,
            N_HEADS_A * D_ROPE,
            KV_RANK,
            D_ROPE,
            IDX_HEADS * IDX_DIM,
            IDX_DIM,
            IDX_HEADS,
            3 * N_HEADS_B * HEAD_DIM)
IN_COLS_2 = 512 + 256 + 128 + 32 + 512 + 64 + 8 + 1536 if D_MODEL == 1024 else int(np.sum(IN_SIZES))


def rmsnorm(x, g):
    xf = x.astype(jnp.float32)
    y = xf * lax.rsqrt(jnp.mean(xf * xf, axis=-1, keepdims=True) + NORM_EPS)
    return (y * g.astype(jnp.float32)).astype(x.dtype)

def rope(x):
    S, d = x.shape[1], x.shape[-1]
    inv = ROPE_THETA ** (-jnp.arange(0, d, 2, dtype=jnp.float32) / d)
    ang = jnp.arange(S, dtype=jnp.float32)[:, None] * inv[None, :]
    cos = jnp.cos(ang)[None, :, None, :].astype(x.dtype)
    sin = jnp.sin(ang)[None, :, None, :].astype(x.dtype)
    x1, x2 = jnp.split(x, 2, axis=-1)
    return jnp.concatenate([x1 * cos - x2 * sin, x2 * cos + x1 * sin], axis=-1)

def dsa_sparse_attention(q_nope, q_rope, c_kv, k_rope, q_idx, k_idx, w_idx, w_uk, w_uv):
    B, S = q_nope.shape[0], q_nope.shape[1]
    topk = min(TOPK_MAX, S // 4)
    nb = S // Q_BLOCK
    scale = (D_NOPE + D_ROPE) ** -0.5
    q_lat = jnp.einsum('bshn,hnc->bshc', q_nope, w_uk)
    w_eff = w_idx.astype(jnp.float32) * (IDX_HEADS ** -0.5) * (IDX_DIM ** -0.5)
    key_pos = jnp.arange(S)
    gather = jax.vmap(lambda table, ix: table[ix])

    def to_blocks(a):
        return jnp.moveaxis(a.reshape((B, nb, Q_BLOCK) + a.shape[2:]), 1, 0)

    def block(args):
        ql, qr, qi, wi, blk = args
        q_pos = blk * Q_BLOCK + jnp.arange(Q_BLOCK)
        causal = key_pos[None, :] <= q_pos[:, None]
        logits = jnp.einsum('bqhd,bsd->bhqs', qi, k_idx).astype(jnp.float32)
        index = jnp.einsum('bhqs,bqh->bqs', jax.nn.relu(logits), wi)
        index = jnp.where(causal[None], index, -jnp.inf)
        _, sel = lax.top_k(index, topk)
        valid = sel <= q_pos[None, :, None]
        c_sel = gather(c_kv, sel)
        r_sel = gather(k_rope, sel)
        s = (jnp.einsum('bqhc,bqkc->bhqk', ql, c_sel)
             + jnp.einsum('bqhr,bqkr->bhqk', qr, r_sel)).astype(jnp.float32) * scale
        s = jnp.where(valid[:, None], s, -jnp.inf)
        p = jax.nn.softmax(s, axis=-1).astype(c_sel.dtype)
        return jnp.einsum('bhqk,bqkc->bqhc', p, c_sel)

    o_lat = lax.map(block, (to_blocks(q_lat), to_blocks(q_rope), to_blocks(q_idx),
                            to_blocks(w_eff), jnp.arange(nb)))
    o_lat = jnp.moveaxis(o_lat, 0, 1).reshape(B, S, N_HEADS_A, KV_RANK)
    return jnp.einsum('bshc,hcv->bshv', o_lat, w_uv)

def dilated_pattern(q, k, v, window, dilation):
    B, H, S, d = q.shape
    n = S // dilation
    w_sub = window // dilation
    nb = -(-n // Q_BLOCK)
    pad = nb * Q_BLOCK - n

    def split(a):
        a = a.reshape(B, H, n, dilation, d).transpose(0, 1, 3, 2, 4)
        a = jnp.pad(a, ((0, 0), (0, 0), (0, 0), (0, pad), (0, 0)))
        return a.reshape(B, H, dilation, nb, Q_BLOCK, d)

    def with_prev(a):
        prev = jnp.concatenate([jnp.zeros_like(a[:, :, :, :1]), a[:, :, :, :-1]], axis=3)
        return jnp.concatenate([prev, a], axis=4)

    qb = split(q)
    kk = with_prev(split(k))
    vv = with_prev(split(v))
    s = jnp.einsum('bhrnqd,bhrnkd->bhrnqk', qb, kk).astype(jnp.float32) * (d ** -0.5)
    rel = (jnp.arange(Q_BLOCK)[:, None] + Q_BLOCK) - jnp.arange(2 * Q_BLOCK)[None, :]
    band = (rel >= 0) & (rel <= w_sub)
    has_prev = (jnp.arange(nb)[:, None, None] > 0) | (jnp.arange(2 * Q_BLOCK)[None, None, :] >= Q_BLOCK)
    mask = band[None] & has_prev
    s = jnp.where(mask, s, -jnp.inf)
    lse = jax.nn.logsumexp(s, axis=-1)
    p = jnp.exp(s - lse[..., None]).astype(v.dtype)
    o = jnp.einsum('bhrnqk,bhrnkd->bhrnqd', p, vv)

    def merge(a, tail):
        a = a.reshape((B, H, dilation, nb * Q_BLOCK) + tail)[:, :, :, :n]
        return jnp.swapaxes(a, 2, 3).reshape((B, H, S) + tail)

    return merge(o, (d,)), merge(lse, ())

def dilated_attention(q, k, v):
    outs, lses = [], []
    for window, dilation in DILATED_PATTERNS:
        o, l = dilated_pattern(q, k, v, window, dilation)
        outs.append(o)
        lses.append(l)
    alpha = jax.nn.softmax(jnp.stack(lses, axis=0), axis=0).astype(q.dtype)
    return jnp.sum(alpha[..., None] * jnp.stack(outs, axis=0), axis=0)

def second_inputs(seed: int = 0) -> dict:
    key = jax.random.key(seed)
    ks = jax.random.split(key, 20)
    f32 = jnp.float32

    def w(k, shape, fan_in):
        return jax.random.normal(k, shape, f32) * (fan_in ** -0.5)

    def gain(k, shape):
        return 1.0 + 0.02 * jax.random.normal(k, shape, f32)

    L = DEPTH
    return {
        "x": jax.random.normal(ks[0], (BATCH, SEQ, D_MODEL), f32),
        "mem": jax.random.normal(ks[1], (BATCH, MEM_TOKENS, D_MODEL), f32),
        "norm_mix_g": gain(ks[2], (L, D_MODEL)),
        "w_in": w(ks[3], (L, D_MODEL, IN_COLS_2), D_MODEL),
        "kv_norm_g": gain(ks[4], (L, KV_RANK)),
        "w_uk": w(ks[5], (L, N_HEADS_A, D_NOPE, KV_RANK), D_NOPE),
        "w_uv": w(ks[6], (L, N_HEADS_A, KV_RANK, V_DIM), KV_RANK),
        "w_out": w(ks[7], (L, N_HEADS_A * V_DIM + N_HEADS_B * HEAD_DIM, D_MODEL), MIX_WIDTH),
        "norm_cross_g": gain(ks[8], (L, D_MODEL)),
        "norm_mem_g": gain(ks[9], (L, D_MODEL)),
        "w_q_cross": w(ks[10], (L, D_MODEL, CROSS_HEADS * CROSS_HEAD_DIM), D_MODEL),
        "w_kv_cross": w(ks[11], (L, D_MODEL, 2 * CROSS_HEADS * CROSS_HEAD_DIM), D_MODEL),
        "w_o_cross": w(ks[12], (L, CROSS_HEADS * CROSS_HEAD_DIM, D_MODEL), CROSS_HEADS * CROSS_HEAD_DIM),
        "norm_mlp_g": gain(ks[13], (L, D_MODEL)),
        "w_up": w(ks[14], (L, D_MODEL, D_FF), D_MODEL),
        "w_down": w(ks[15], (L, D_FF, D_MODEL), D_FF),
        "norm_final_g": gain(ks[16], (D_MODEL,)),
    }

def second_block(x, mem, norm_mix_g, w_in, kv_norm_g, w_uk, w_uv, w_out, norm_cross_g, norm_mem_g,
              w_q_cross, w_kv_cross, w_o_cross, norm_mlp_g, w_up, w_down, norm_final_g):
    B, S, _ = x.shape
    M = mem.shape[1]
    split_at = [int(c) for c in np.cumsum(IN_SIZES)[:-1]]
    for l in range(DEPTH):
        h = rmsnorm(x, norm_mix_g[l])
        proj = h @ w_in[l]
        p_qn, p_qr, p_ckv, p_kr, p_qi, p_ki, p_wi, p_qkv = jnp.split(proj, split_at, axis=-1)
        q_nope = p_qn.reshape(B, S, N_HEADS_A, D_NOPE)
        q_rope = rope(p_qr.reshape(B, S, N_HEADS_A, D_ROPE))
        c_kv = rmsnorm(p_ckv, kv_norm_g[l])
        k_rope = rope(p_kr[:, :, None, :])[:, :, 0]
        q_idx = rope(p_qi.reshape(B, S, IDX_HEADS, IDX_DIM))
        k_idx = rope(p_ki[:, :, None, :])[:, :, 0]
        o_a = dsa_sparse_attention(q_nope, q_rope, c_kv, k_rope, q_idx, k_idx, p_wi, w_uk[l], w_uv[l])
        qkv = p_qkv.reshape(B, S, 3, N_HEADS_B, HEAD_DIM)
        q_b = rope(qkv[:, :, 0]).transpose(0, 2, 1, 3)
        k_b = rope(qkv[:, :, 1]).transpose(0, 2, 1, 3)
        v_b = qkv[:, :, 2].transpose(0, 2, 1, 3)
        o_b = dilated_attention(q_b, k_b, v_b).transpose(0, 2, 1, 3)
        heads = jnp.concatenate([o_a.reshape(B, S, N_HEADS_A * V_DIM),
                                 o_b.reshape(B, S, N_HEADS_B * HEAD_DIM)], axis=-1)
        x = x + heads @ w_out[l]
        hc = rmsnorm(x, norm_cross_g[l])
        m = rmsnorm(mem, norm_mem_g[l])
        qc = (hc @ w_q_cross[l]).reshape(B, S, CROSS_HEADS, CROSS_HEAD_DIM)
        kvc = (m @ w_kv_cross[l]).reshape(B, M, 2, CROSS_HEADS, CROSS_HEAD_DIM)
        sc = jnp.einsum('bshd,bmhd->bhsm', qc, kvc[:, :, 0]).astype(jnp.float32) * (CROSS_HEAD_DIM ** -0.5)
        pc = jax.nn.softmax(sc, axis=-1).astype(x.dtype)
        oc = jnp.einsum('bhsm,bmhd->bshd', pc, kvc[:, :, 1]).reshape(B, S, CROSS_HEADS * CROSS_HEAD_DIM)
        x = x + oc @ w_o_cross[l]
        hm = rmsnorm(x, norm_mlp_g[l])
        x = x + jnp.square(jax.nn.relu(hm @ w_up[l])) @ w_down[l]
    return rmsnorm(x, norm_final_g)


def setup_inputs(seed=0):
    out = dict(first_inputs(seed))
    for name, value in second_inputs(seed + 1).items():
        if name != "x":
            out[name + "_2"] = value
    return out


def reference(
    x, norm_mix_g, w_in, w_gate, b_gate, w_sb_out, w_ret_out, ret_norm_g, w_out, norm_ffn_g,
    w_group_router, b_group_router, w_expert_router, b_expert_router, w_exp_gate, w_exp_up,
    w_exp_down, norm_final_g, mem_2, norm_mix_g_2, w_in_2, kv_norm_g_2, w_uk_2, w_uv_2, w_out_2,
    norm_cross_g_2, norm_mem_g_2, w_q_cross_2, w_kv_cross_2, w_o_cross_2, norm_mlp_g_2, w_up_2,
    w_down_2, norm_final_g_2,
):
    x = first_block(
        x, norm_mix_g, w_in, w_gate, b_gate, w_sb_out, w_ret_out, ret_norm_g, w_out, norm_ffn_g,
        w_group_router, b_group_router, w_expert_router, b_expert_router, w_exp_gate, w_exp_up,
        w_exp_down, norm_final_g,
    )
    return second_block(
        x, mem_2, norm_mix_g_2, w_in_2, kv_norm_g_2, w_uk_2, w_uv_2, w_out_2, norm_cross_g_2,
        norm_mem_g_2, w_q_cross_2, w_kv_cross_2, w_o_cross_2, norm_mlp_g_2, w_up_2, w_down_2,
        norm_final_g_2,
    )


_drawn_inputs = setup_inputs


def setup_inputs(seed=0):
    import zlib

    import numpy as np

    out = dict(_drawn_inputs(seed))
    spreads = {}
    factors = {'b_gate': 3.686,
     'ret_norm_g': 3.066,
     'b_group_router': 3.861,
     'b_expert_router': 4.508,
     'norm_mix_g_2': 3.004,
     'kv_norm_g_2': 8.0,
     'norm_cross_g_2': 8.0,
     'norm_mem_g_2': 8.0,
     'norm_mlp_g_2': 9.664,
     'norm_final_g_2': 7.425}
    for name, (base, spread) in spreads.items():
        noise = np.random.default_rng([zlib.crc32(name.encode()), seed]).standard_normal(out[name].shape)
        drawn = base * np.exp(spread * noise) if base else spread * noise
        out[name] = __import__('jax').numpy.asarray(drawn.astype(out[name].dtype))
    for name, factor in factors.items():
        out[name] = (out[name] * factor).astype(out[name].dtype)
    return out
```

```python
import numpy as np

import concourse.bass as bass
from concourse import mybir

F32 = mybir.dt.float32
FR = mybir.dt.float32r
I32 = mybir.dt.int32
U32 = mybir.dt.uint32
ACT = mybir.ActivationFunctionType
ALU = mybir.AluOpType
AX = mybir.AxisListType

P = 128
D = 1024
S = 512
KT = D // P
TB = S // P
HEADS = 8
HD = 64
RV = 128
NG, NE = 4, 16
NR = NG + NE
FF = 512
MEM = 256
CH_HEADS, CH_DIM = 4, 256
TOPK = min(256, S // 4)
FREQ = HD // 2
FREQ_R = 16
EPS = 1e-6
BIG = 1e30
CHUNK_COLS = 2048
RING = 2
MOE_RING = 12
PAIRS = NE // 2

SEG = {512: 0, 384: 512, 128: 896, 256: 1024}
SPAN = 1280

COLS = {}
_at = 0
for _name, _n in [("mix", KT), ("bgate", 2 * KT), ("ret", KT), ("ffn", KT), ("end1", KT), ("mix2", KT), ("kv", 1),
                  ("cross", KT), ("mem", KT), ("mlp", KT), ("final", KT), ("eps", 1)]:
    COLS[_name] = _at
    _at += _n
N_COLS = _at

LAYERS = [("sb_q", 2), ("sb_k", 2), ("sb_v", 2), ("gate_sb", 4), ("sb_out", 2),
          ("ret_q", 2), ("ret_k", 2), ("ret_v", 4), ("ret_g", 4), ("gate_ret", 4), ("ret_out", 4), ("out", 4),
          ("q_idx", 2), ("k_idx", 1), ("ckv_wi", 1), ("q_nope", 2), ("q_rope", 2), ("k_rope", 1),
          ("q_b", 2), ("k_b", 2), ("v_b", 2), ("out2", 4), ("k_mem", 4), ("v_mem", 4), ("q_cross", 4),
          ("o_cross", 4), ("up0", 4), ("up1", 4), ("down0", 4), ("up2", 4), ("down1", 4), ("up3", 4), ("down2", 4),
          ("down3", 4)]
TILES_OF = {"sb_v": 8, "sb_out": 8, "ret_v": 16, "v_b": 8, "v_mem": 8}
FIRST_CHUNK, FIRST_TILE = {}, {}
_c = _t = 0
for _name, _n in LAYERS:
    FIRST_CHUNK[_name], FIRST_TILE[_name] = _c, _t
    _c += _n
    _t += TILES_OF.get(_name, 2 * _n)
N_CHUNKS = _c
N_OF = dict(LAYERS)


def build(nc, d):
    BASE = 16512

    def at(name, kb, shape, dt=F32):
        return nc.alloc_sbuf_tensor_at(name, shape, dt, offset=BASE + int(kb * 1024))

    def sem(name):
        return nc.alloc_semaphore(name)

    raw = [at(f"raw{b}", 8 * b, [P, CHUNK_COLS]) for b in range(RING)]
    w_hi = [at(f"w_hi{b}", 16 + 8 * b, [P, CHUNK_COLS], FR) for b in range(RING)]
    w_lo = [at(f"w_lo{b}", 32 + 8 * b, [P, CHUNK_COLS], FR) for b in range(RING)]
    x_hi = at("x_hi", 48, [P, KT, S], FR)
    x_lo = at("x_lo", 64, [P, KT, S], FR)
    y_hi = at("y_hi", 80, [P, KT, S], FR)
    y_lo = at("y_lo", 96, [P, KT, S], FR)
    res = at("res", 112, [P, KT, S])
    ident = at("ident", 128, [P, P])
    neg_tri = at("neg_tri", 128.5, [P, P])
    neg_ones = at("neg_ones", 129, [P, P])
    ones = at("ones", 129.5, [P, P])
    before = at("before", 130, [P, P])
    cos64 = at("cos64", 130.5, [P, S])
    sin64 = at("sin64", 132.5, [P, S])
    cos32 = at("cos32", 134.5, [P, S])
    sin32 = at("sin32", 136.5, [P, S])
    cols = at("cols", 138.5, [P, N_COLS])

    def col(name, i=0):
        return cols[:, COLS[name] + i:COLS[name] + i + 1]

    psum = nc.alloc_psum_tensor("psum", [P, 8, 512], F32)
    flat = psum[:, :, :].rearrange("p b n -> p (b n)")

    raw_landed = [sem(f"raw_landed{b}") for b in range(RING)]
    hi_ready = sem("hi_ready")
    lo_ready = sem("lo_ready")
    tile_done = sem("tile_done")
    bank_free = sem("bank_free")
    consts_landed = sem("consts_landed")

    def load_chunk(sp, c, i=0):
        if isinstance(c, int) and c >= N_CHUNKS:
            return
        if c >= RING:
            sp.wait_ge(lo_ready, c - 1 + RING * i)
        sp.dma_start(raw[c % RING][:, :], d["w_dense"][c + RING * i]).then_inc(raw_landed[c % RING], 16)

    def split_hi(act, c, tiles_before, i=0, ti=0):
        if c >= N_CHUNKS:
            return
        if c >= RING:
            act.wait_ge(tile_done, tiles_before + ti)
        act.wait_ge(raw_landed[c % RING], 16 * (c // RING + 1) + 16 * i)
        act.activation(w_hi[c % RING][:, :], raw[c % RING][:, :], ACT.Copy).then_inc(hi_ready, 1)

    def split_lo(pool, c, i=0):
        if c >= N_CHUNKS:
            return
        pool.wait_ge(hi_ready, c + 1 + RING * i)
        pool.tensor_tensor(w_lo[c % RING][:, :], raw[c % RING][:, :], w_hi[c % RING][:, :].bitcast(F32),
                           ALU.subtract).then_inc(lo_ready, 1)

    def loop(eng, n, body):
        if n == 1:
            body(0)
        else:
            with eng.Fori(0, n) as i:
                body(i)

    def turns(name):
        n = N_OF[name]
        return (n // 2, 2) if n % 2 == 0 else (1, 1)

    def per_chunk(name):
        return TILES_OF.get(name, 2 * N_OF[name]) // N_OF[name]

    def dense_sync(sp, name):
        n, k = turns(name)
        c0 = FIRST_CHUNK[name]
        loop(sp, n, lambda i: [load_chunk(sp, c0 + 4 + b, i) for b in range(k)])

    def dense_pool(pool, name, after=None):
        n, k = turns(name)
        c0 = FIRST_CHUNK[name]

        def body(i):
            for b in range(k):
                if after:
                    after(pool, i, b)
                split_lo(pool, c0 + 2 + b, i)
        loop(pool, n, body)

    def dense_act(act, name, evac=None):
        n, k = turns(name)
        c0, t0, per = FIRST_CHUNK[name], FIRST_TILE[name], per_chunk(name)

        def body(i):
            for b in range(k):
                for m in range(per if evac else 0):
                    j = per * b + m
                    act.wait_ge(tile_done, t0 + 1 + j + k * per * i)
                    act.wait_ge(consts_landed, N_CONSTS)
                    evac(act, i, j, (t0 + j) % 4)
                split_hi(act, c0 + 2 + b, t0 + per * (b + 1), i, k * per * i)
        loop(act, n, body)

    def dense_vector(dve, name, evac):
        n, k = turns(name)
        t0, per = FIRST_TILE[name], per_chunk(name)
        assert n == 1 or (k * per) % 4 == 0

        def body(i):
            for j in range(k * per):
                evac(dve, i, j, (t0 + j) % 4)
        loop(dve, n, body)

    def three_pass(pe, out, lh, ll, rh, rl, first, last):
        pe.matmul(out, lh, rh, start=first, stop=False)
        pe.matmul(out, lh, rl, start=False, stop=False)
        return pe.matmul(out, ll, rh, start=False, stop=last)

    def dense_pe(pe, name, ah, al, n_tok=S, kts=KT, token_major=False, drain=True, between=None):
        n, k = turns(name)
        c0, t0, per = FIRST_CHUNK[name], FIRST_TILE[name], per_chunk(name)
        if drain and t0:
            pe.wait_ge(bank_free, t0 + 4)

        def body(i):
            for b in range(k):
                slot = (c0 + b) % RING
                wh = w_hi[slot][:, :].rearrange("p (m k n) -> p m k n", k=kts, n=P)
                wl = w_lo[slot][:, :].rearrange("p (m k n) -> p m k n", k=kts, n=P)
                pe.wait_ge(lo_ready, c0 + b + 1 + k * i)
                for m in range(per):
                    j = per * b + m
                    bank = (t0 + j) % 4
                    pe.wait_ge(bank_free, t0 + j + 1 + k * per * i)
                    for kt in range(kts):
                        if token_major:
                            mm = three_pass(pe, psum[:, bank, 0:2 * P], ah[:, kt, m * P:(m + 1) * P],
                                            al[:, kt, m * P:(m + 1) * P], wh[:, :, kt, :], wl[:, :, kt, :],
                                            kt == 0, kt == kts - 1)
                        else:
                            mm = three_pass(pe, psum[:, bank, 0:n_tok], wh[:, m, kt, :], wl[:, m, kt, :],
                                            ah[:, kt, 0:n_tok], al[:, kt, 0:n_tok], kt == 0, kt == kts - 1)
                    mm.then_inc(tile_done, 1)
        if between:
            body(0)
            between()
            body(1)
        else:
            loop(pe, n, body)

    n_squared, n_added, n_summed, n_rooted, n_inverted, n_scaled, n_high, n_low = (
        sem("norm_" + x) for x in ("squared", "added", "summed", "rooted", "inverted", "scaled", "high", "low"))
    norms = {"all": 0, "split": 0}

    class Norm:

        def __init__(self, tag, x, gain, temps_kb, n_tok=S, hi=None, lo=None, out=None, bank=0):
            self.x, self.gain, self.n, self.hi, self.lo, self.out, self.bank = x, gain, n_tok, hi, lo, out, bank
            self.u, self.s = norms["all"], KT * norms["split"]
            norms["all"] += 1
            norms["split"] += hi is not None
            self.sq = [at(f"{tag}_sq{b}", temps_kb + 2 * b, [P, n_tok]) for b in range(2)]
            self.sum = at(f"{tag}_sum", temps_kb + 4, [P, n_tok])
            self.rms = at(f"{tag}_rms", temps_kb + 6, [P, n_tok])
            self.rstd = at(f"{tag}_rstd", temps_kb + 8, [P, n_tok])
            self.y = [at(f"{tag}_y{b}", temps_kb + 10 + 2 * b, [P, n_tok]) for b in range(3)] if hi is not None else None

        def wait_scaled(self, eng, n):
            eng.wait_ge(n_scaled, KT * self.u + n)

        def wait_split(self, eng, n=KT):
            eng.wait_ge(n_low, self.s + n)

        def act(self, act, arrived):
            sq0, add0 = KT * self.u, (KT - 1) * self.u
            for kt in range(KT):
                arrived(act, kt)
                if kt >= 2:
                    act.wait_ge(n_added, add0 + kt - 1)
                act.activation(self.sq[kt % 2][:, :], self.x[:, kt, :], ACT.Square).then_inc(n_squared, 1)
            act.wait_ge(n_summed, self.u + 1)
            act.activation(self.rms[:, :], psum[:, self.bank, 0:self.n], ACT.Sqrt, scale=1.0 / D, bias=col("eps"))\
               .then_inc(n_rooted, 1)
            if self.hi is not None:
                for kt in range(KT):
                    act.wait_ge(n_scaled, sq0 + kt + 1)
                    act.activation(self.hi[:, kt, :], self.y[kt % 3][:, :], ACT.Copy).then_inc(n_high, 1)

        def vector(self, dve, arrived):
            sq0, add0 = KT * self.u, (KT - 1) * self.u
            arrived(dve, KT - 1)
            for kt in range(1, KT):
                dve.wait_ge(n_squared, sq0 + kt + 1)
                if kt == 1:
                    dve.tensor_tensor(self.sum[:, :], self.sq[0][:, :], self.sq[1][:, :], ALU.add).then_inc(n_added, 1)
                else:
                    dve.wait_ge(n_added, add0 + kt - 1)
                    dve.tensor_tensor(self.sum[:, :], self.sum[:, :], self.sq[kt % 2][:, :], ALU.add)\
                       .then_inc(n_added, 1)
            dve.wait_ge(n_rooted, self.u + 1)
            dve.reciprocal(self.rstd[:, :], self.rms[:, :]).then_inc(n_inverted, 1)
            dve.wait_ge(n_inverted, self.u + 1)

            def low(kt):
                dve.wait_ge(n_high, self.s + kt + 1)
                dve.tensor_tensor(self.lo[:, kt, :], self.y[kt % 3][:, :], self.hi[:, kt, :].bitcast(F32),
                                  ALU.subtract).then_inc(n_low, 1)
            for kt in range(KT):
                if self.hi is not None and kt >= 3:
                    dve.wait_ge(n_low, self.s + kt - 2)
                y = self.y[kt % 3][:, :] if self.hi is not None else self.out[:, kt, :]
                dve.scalar_tensor_tensor(out=y, in0=self.x[:, kt, :], scalar=col(self.gain, kt), in1=self.rstd[:, :],
                                         op0=ALU.mult, op1=ALU.mult).then_inc(n_scaled, 1)
                if self.hi is not None and kt >= 1:
                    low(kt - 1)
            if self.hi is not None:
                low(KT - 1)

        def pe(self, pe):
            pe.wait_ge(n_added, (KT - 1) * (self.u + 1))
            pe.matmul(psum[:, self.bank, 0:self.n], ones[:, :], self.sum[:, :], start=True, stop=True)\
              .then_inc(n_summed, 1)

    dve_step = sem("dve_step")
    steps = {"dve": 0}

    def link(dve, ins):
        steps["dve"] += 1
        ins.then_inc(dve_step, 1)
        dve.wait_ge(dve_step, steps["dve"])

    sb_q = at("sb_q", 144, [P, 4, S])
    sb_k = at("sb_k", 152, [P, 4, S])
    sb_v = at("sb_v", 160, [P, TB, S])
    x_landed = [sem(f"x_landed{g}") for g in range(4)]
    norm1 = Norm("norm1", res, "mix", 170, hi=x_hi, lo=x_lo)
    CONSTS = [("ident", ident), ("neg_tri", neg_tri), ("before", before), ("cos64", cos64), ("sin64", sin64),
              ("cos32", cos32), ("sin32", sin32), ("cols", cols)]
    N_CONSTS = 16 * len(CONSTS)
    fills = sem("fills")
    with nc.Block() as block:
        @block.sync
        def _(sp):
            for g in range(4):
                sp.dma_start(res[:, 2 * g:2 * g + 2, :], d["x"][:, 2 * g:2 * g + 2, :]).then_inc(x_landed[g], 16)
            for name, tile in CONSTS:
                sp.dma_start(tile[:, :], d[name]).then_inc(consts_landed, 16)
            for c in range(4):
                load_chunk(sp, c)
            for name in ("sb_q", "sb_k", "sb_v"):
                dense_sync(sp, name)

        @block.gpsimd
        def _(pool):
            pool.memset(ones[:, :], 1.0).then_inc(fills, 1)
            pool.memset(neg_ones[:, :], -1.0).then_inc(fills, 1)
            for c in range(RING):
                split_lo(pool, c)
            for name in ("sb_q", "sb_k", "sb_v"):
                dense_pool(pool, name)

        @block.vector
        def _(dve):
            dve.wait_ge(consts_landed, N_CONSTS)
            norm1.vector(dve, lambda e, kt: [e.wait_ge(x_landed[g], 16) for g in range(4)])

        @block.scalar
        def _(act):
            act.wait_ge(consts_landed, N_CONSTS)
            act.sem_inc(bank_free, 4)
            norm1.act(act, lambda e, kt: e.wait_ge(x_landed[kt // 2], 16))
            for c in range(RING):
                split_hi(act, c, 0)
            dense_act(act, "sb_q", lambda e, i, j, bank: e.activation(
                sb_q[:, j, :], psum[:, bank, :], ACT.Copy, scale=HD ** -0.5).then_inc(bank_free, 1))
            dense_act(act, "sb_k", lambda e, i, j, bank: e.activation(
                sb_k[:, j, :], psum[:, bank, :], ACT.Copy).then_inc(bank_free, 1))
            dense_act(act, "sb_v", lambda e, i, j, bank: e.activation(
                sb_v[:, j % 4, 256 * (j // 4):256 * (j // 4) + 256], psum[:, bank, 0:256], ACT.Copy)
                .then_inc(bank_free, 1))

        @block.tensor
        def _(pe):
            pe.wait_ge(fills, 2)
            norm1.pe(pe)
            norm1.wait_split(pe)
            dense_pe(pe, "sb_q", x_hi, x_lo, drain=False)
            dense_pe(pe, "sb_k", x_hi, x_lo, drain=False)
            dense_pe(pe, "sb_v", x_hi, x_lo, token_major=True, drain=False)

    za = [at(f"sb_log{b}", 168 + 5 * b, [P, SPAN]) for b in range(2)]
    zw = [at(f"sb_weight{b}", 178 + 5 * b, [P, SPAN]) for b in range(2)]
    Z = [flat[:, 1536 * b:1536 * b + SPAN] for b in range(2)]
    z_done, a_done, e_done, ln_done, l_done, lm_done, c_done, w_done, wm_done, y_done, y_high, y_low = (
        sem("sb_" + n) for n in ("scores", "abs", "exp", "ln", "softplus", "masked", "logs", "weights",
                                 "weights_masked", "values", "high", "low"))

    def span(j):
        n = S - P * j
        return SEG[n], n

    with nc.Block() as block:
        @block.tensor
        def _(pe):
            pe.wait_ge(bank_free, FIRST_TILE["gate_sb"] + 4)

            def scores(h):
                r = HD * (h % 2)
                if h >= 2:
                    pe.wait_ge(w_done, h - 1)
                for j in range(TB):
                    o, n = span(j)
                    mm = pe.matmul(Z[h % 2][:, o:o + n], sb_k[r:r + HD, h // 2, j * P:(j + 1) * P],
                                   sb_q[r:r + HD, h // 2, j * P:S], start=(j != 3), stop=True, skip_group_check=True)
                mm.then_inc(z_done, 1)

            def logs(h):
                pe.wait_ge(lm_done, h + 1)
                for j in range(TB):
                    o, n = span(j)
                    mm = pe.matmul(Z[h % 2][:, o:o + n], neg_tri[:, :], za[h % 2][:, o:o + n],
                                   start=False, stop=True, skip_group_check=True)
                    for j2 in range(j + 1, TB):
                        o2, n2 = span(j2)
                        mm = pe.matmul(Z[h % 2][:, o + n - n2:o + n], neg_ones[:, :], za[h % 2][:, o2:o2 + n2],
                                       start=False, stop=True, skip_group_check=True)
                mm.then_inc(c_done, 1)

            def values(h):
                r = HD * (h % 2)
                pe.wait_ge(wm_done, h + 1)
                if h >= 4:
                    pe.wait_ge(y_low, (h - 4) // 2 + 1)
                for j in range(TB):
                    o, n = span(j)
                    mm = pe.matmul(psum[r:r + HD, 6 + h // 2 % 2, S - n:S], sb_v[:, j, h * HD:(h + 1) * HD],
                                   zw[h % 2][:, o:o + n], start=(j == 0), stop=(j == TB - 1), skip_group_check=True)
                mm.then_inc(y_done, 1)

            scores(0)
            for h in range(HEADS):
                if h + 1 < HEADS:
                    scores(h + 1)
                logs(h)
                if h >= 1:
                    values(h - 1)
            values(HEADS - 1)

        @block.vector
        def _(dve):
            def softplus(h):
                dve.wait_ge(ln_done, h + 1)
                dve.scalar_tensor_tensor(out=za[h % 2][:, :], in0=Z[h % 2], scalar=0.0, in1=za[h % 2][:, :],
                                         op0=ALU.max, op1=ALU.add).then_inc(l_done, 1)

            def low(p):
                dve.wait_ge(y_high, p + 1)
                dve.tensor_tensor(y_lo[:, p, :], psum[:, 6 + p % 2, :], y_hi[:, p, :].bitcast(F32), ALU.subtract)\
                   .then_inc(y_low, 1)
            for h in range(HEADS):
                softplus(h)
                if h >= 3 and h % 2 == 1:
                    low(h // 2 - 1)
            low(3)

        @block.scalar
        def _(act):
            def log1p(h):
                act.wait_ge(z_done, h + 1)
                if h >= 2:
                    act.wait_ge(c_done, h - 1)
                act.activation(za[h % 2][:, :], Z[h % 2], ACT.Abs).then_inc(a_done, 1)
                act.wait_ge(a_done, h + 1)
                act.activation(za[h % 2][:, :], za[h % 2][:, :], ACT.Exp, scale=-1.0).then_inc(e_done, 1)
                act.wait_ge(e_done, h + 1)
                act.activation(za[h % 2][:, :], za[h % 2][:, :], ACT.Ln, bias=1.0).then_inc(ln_done, 1)

            def weights(h):
                act.wait_ge(c_done, h + 1)
                if h >= 2:
                    act.wait_ge(y_done, h - 1)
                act.activation(zw[h % 2][:, :], Z[h % 2], ACT.Exp).then_inc(w_done, 1)

            def high(p):
                act.wait_ge(y_done, 2 * p + 2)
                act.activation(y_hi[:, p, :], psum[:, 6 + p % 2, :], ACT.Copy).then_inc(y_high, 1)
            log1p(0)
            for h in range(HEADS):
                if h + 1 < HEADS:
                    log1p(h + 1)
                weights(h)
                if h >= 3 and h % 2 == 1:
                    high(h // 2 - 1)
            high(3)

        @block.gpsimd
        def _(pool):
            def mask(buf, done):
                for j in range(TB):
                    o, _ = span(j)
                    ins = pool.affine_select(out=buf[:, o:o + P], in_=buf[:, o:o + P], compare_op=ALU.is_gt, fill=0.0,
                                             base=0, pattern=[[1, P]], channel_multiplier=-1)
                ins.then_inc(done, 1)
            for h in range(HEADS):
                pool.wait_ge(l_done, h + 1)
                mask(za[h % 2], lm_done)
                pool.wait_ge(w_done, h + 1)
                mask(zw[h % 2], wm_done)


    gate = at("gate", 144, [P, KT, S])
    mix = at("mix", 190, [P, KT, S])
    ret_q = at("ret_q", 144, [P, 4, S])
    ret_k = at("ret_k", 152, [P, 4, S])
    ret_v = at("ret_v", 160, [P, TB, D])

    class Rotary:

        def __init__(self, tag, temps_kb):
            self.t = [[at(f"{tag}_t{b}{n}", temps_kb[b] + 2 * n, [P, S]) for n in range(4)] for b in range(2)]
            self.rotated = sem(f"{tag}_rotated")
            self.pairs = {"dve": 0, "pool": 0}

        def vector(self, dve, name, pairs):
            for q in range(pairs):
                u = self.pairs["dve"]
                self.pairs["dve"] += 1
                t = self.t[u % 2]
                t0 = FIRST_TILE[name] + 2 * q
                a, b = psum[:, t0 % 4, :], psum[:, (t0 + 1) % 4, :]
                dve.wait_ge(tile_done, t0 + 2)
                if u >= 2:
                    dve.wait_ge(self.rotated, 2 * (u - 1))
                dve.tensor_tensor(t[0][:, :], a, cos64[:, :], ALU.mult)
                dve.tensor_tensor(t[3][:, :], a, sin64[:, :], ALU.mult).then_inc(bank_free, 1)
                dve.tensor_tensor(t[1][:, :], b, sin64[:, :], ALU.mult)
                dve.tensor_tensor(t[2][:, :], b, cos64[:, :], ALU.mult).then_inc(bank_free, 1)

        def pool(self, pool, name, out, q):
            u = self.pairs["pool"]
            self.pairs["pool"] += 1
            t = self.t[u % 2]
            pool.wait_ge(bank_free, FIRST_TILE[name] + 2 * q + 2 + 4)
            pool.tensor_tensor(out[:, 2 * q, :], t[0][:, :], t[1][:, :], ALU.subtract).then_inc(self.rotated, 1)
            pool.tensor_tensor(out[:, 2 * q + 1, :], t[2][:, :], t[3][:, :], ALU.add).then_inc(self.rotated, 1)

    rot1 = Rotary("rot1", (88, 104))
    with nc.Block() as block:
        names = ("gate_sb", "sb_out", "ret_q", "ret_k", "ret_v")

        @block.sync
        def _(sp):
            for name in names:
                dense_sync(sp, name)

        @block.gpsimd
        def _(pool):
            for name in names:
                rope_to = {"ret_q": ret_q, "ret_k": ret_k}.get(name)
                dense_pool(pool, name, after=rope_to and (lambda e, i, b: rot1.pool(e, name, rope_to, b)))

        @block.scalar
        def _(act):
            dense_act(act, "gate_sb", lambda e, i, j, bank: e.activation(
                gate[:, bass.ds(4 * i + j, 1), :], psum[:, bank:bank + 1, :], ACT.Sigmoid,
                bias=cols[:, bass.ds(4 * i + j + COLS["bgate"], 1)]).then_inc(bank_free, 1))
            for name in ("sb_out", "ret_q", "ret_k"):
                dense_act(act, name)
            dense_act(act, "ret_v", lambda e, i, j, bank: e.activation(
                ret_v[:, j % 4, bass.ds(512 * i + 256 * (j // 4), 256)], psum[:, bank, 0:256], ACT.Copy)
                .then_inc(bank_free, 1))

        @block.vector
        def _(dve):
            def gated(e, i, j, bank):
                e.wait_ge(tile_done, FIRST_TILE["sb_out"] + j + 1)
                e.tensor_tensor(mix[:, j, :], psum[:, bank, :], gate[:, j, :], ALU.mult).then_inc(bank_free, 1)
            dve.wait_ge(bank_free, FIRST_TILE["sb_out"] + 4)
            dense_vector(dve, "sb_out", gated)
            rot1.vector(dve, "ret_q", 2)
            rot1.vector(dve, "ret_k", 2)

        @block.tensor
        def _(pe):
            dense_pe(pe, "gate_sb", x_hi, x_lo)
            dense_pe(pe, "sb_out", y_hi, y_lo, kts=4)
            dense_pe(pe, "ret_q", x_hi, x_lo)
            dense_pe(pe, "ret_k", x_hi, x_lo)
            dense_pe(pe, "ret_v", x_hi, x_lo, token_major=True)

    prod = [at(f"ret_prod{b}", 176 + 5 * b, [P, SPAN]) for b in range(2)]
    dec = [at(f"decay{b}", 186 + 2 * b, [P, S]) for b in range(2)]
    ret_y = at("ret_y", 80, [P, KT, S])
    rq = [[at(f"ret_{n}{b}", 96 + 2 * k + 8 * b, [P, S]) for b in range(2)] for k, n in enumerate(("sq", "rms", "rstd"))]
    r_landed = [sem(f"decay_landed{b}") for b in range(2)]
    rs_done, rp_done, rv_done, rc_done, rsq_done, rm_done, rr_done, ri_done, ry_done = (
        sem("ret_" + n) for n in ("scores", "decayed", "values", "copied", "squared", "summed", "rooted", "inverted",
                                  "normed"))
    with nc.Block() as block:
        @block.sync
        def _(sp):
            for h in range(HEADS):
                if h >= 2:
                    sp.wait_ge(rp_done, h - 1)
                sp.dma_start(dec[h % 2][:, :], d["decay"][h]).then_inc(r_landed[h % 2], 16)

        @block.tensor
        def _(pe):
            def scores(h):
                r, g = 32 * (h % 4), 2 * (h // 4)
                if h >= 2:
                    pe.wait_ge(rp_done, h - 1)
                for j in range(TB):
                    o, n = span(j)
                    for half in range(2):
                        mm = pe.matmul(Z[h % 2][:, o:o + n], ret_k[r:r + 32, g + half, j * P:(j + 1) * P],
                                       ret_q[r:r + 32, g + half, j * P:S], start=(half == 0 and j != 3), stop=True,
                                       skip_group_check=True)
                mm.then_inc(rs_done, 1)

            def values(h):
                pe.wait_ge(rp_done, h + 1)
                if h >= 2:
                    pe.wait_ge(rr_done, h - 1)
                for j in range(TB):
                    o, n = span(j)
                    mm = pe.matmul(psum[:, 6 + h % 2, S - n:S], ret_v[:, j, h * RV:(h + 1) * RV],
                                   prod[h % 2][:, o:o + n], start=(j == 0), stop=(j == TB - 1), skip_group_check=True)
                mm.then_inc(rv_done, 1)

            def mean_square(h):
                pe.wait_ge(rsq_done, h + 1)
                pe.matmul(psum[:, 6 + h % 2, :], ones[:, :], rq[0][h % 2][:, :], start=True, stop=True)\
                  .then_inc(rm_done, 1)
            scores(0)
            for h in range(HEADS):
                if h + 1 < HEADS:
                    scores(h + 1)
                values(h)
                if h >= 1:
                    mean_square(h - 1)
            mean_square(HEADS - 1)

        @block.vector
        def _(dve):
            def decayed(h):
                dve.wait_ge(rs_done, h + 1)
                dve.wait_ge(r_landed[h % 2], 16 * (h // 2 + 1))
                if h >= 2:
                    dve.wait_ge(rv_done, h - 1)
                for j in range(TB):
                    o, n = span(j)
                    ins = dve.tensor_tensor(prod[h % 2][:, o:o + n], Z[h % 2][:, o:o + n], dec[h % 2][:, 0:n], ALU.mult)
                ins.then_inc(rp_done, 1)

            def norm(h):
                dve.wait_ge(rr_done, h + 1)
                dve.reciprocal(rq[2][h % 2][:, :], rq[1][h % 2][:, :]).then_inc(ri_done, 1)
                dve.wait_ge(ri_done, h + 1)
                dve.scalar_tensor_tensor(out=ret_y[:, h, :], in0=ret_y[:, h, :], scalar=col("ret", h),
                                         in1=rq[2][h % 2][:, :], op0=ALU.mult, op1=ALU.mult).then_inc(ry_done, 1)
            for h in range(HEADS):
                decayed(h)
                if h >= 2:
                    norm(h - 2)
            norm(HEADS - 2)
            norm(HEADS - 1)

        @block.scalar
        def _(act):
            for h in range(HEADS + 1):
                if h < HEADS:
                    act.wait_ge(rv_done, h + 1)
                    act.activation(ret_y[:, h, :], psum[:, 6 + h % 2, :], ACT.Copy).then_inc(rc_done, 1)
                    if h >= 2:
                        act.wait_ge(rm_done, h - 1)
                    act.activation(rq[0][h % 2][:, :], psum[:, 6 + h % 2, :], ACT.Square).then_inc(rsq_done, 1)
                if h >= 1:
                    g = h - 1
                    act.wait_ge(rm_done, g + 1)
                    if g >= 2:
                        act.wait_ge(ri_done, g - 1)
                    act.activation(rq[1][g % 2][:, :], psum[:, 6 + g % 2, :], ACT.Sqrt, scale=1.0 / RV, bias=col("eps"))\
                       .then_inc(rr_done, 1)

    g_tmp = [at(f"g_tmp{b}", 144 + 2 * b, [P, S]) for b in range(4)]
    gate2 = at("gate2", 160, [P, KT, S])
    m_tmp = [at(f"m_tmp{b}", 152 + 2 * b, [P, S]) for b in range(4)]
    g_mul, g_hi, g_lo, m_add, m_hi, m_lo = (
        sem("mix_" + n) for n in ("gated", "gated_high", "gated_low", "sum", "high", "low"))
    norm2 = Norm("norm2", res, "ffn", 176, out=at("hn", 144, [P, KT, S]))
    hn = norm2.out
    with nc.Block() as block:
        names = ("ret_g", "gate_ret", "ret_out", "out")

        @block.sync
        def _(sp):
            for name in names:
                dense_sync(sp, name)

        @block.gpsimd
        def _(pool):
            for name in names:
                dense_pool(pool, name)

        @block.scalar
        def _(act):
            t0, c0 = FIRST_TILE["ret_g"], FIRST_CHUNK["ret_g"]

            def high(t):
                act.wait_ge(g_mul, t + 1)
                act.activation(y_hi[:, t, :], g_tmp[t % 4][:, :], ACT.Copy).then_inc(g_hi, 1)
            for t in range(KT):
                act.wait_ge(tile_done, t0 + t + 1)
                if t >= 4:
                    act.wait_ge(g_lo, t - 3)
                act.activation(g_tmp[t % 4][:, :], psum[:, (t0 + t) % 4, :], ACT.Silu).then_inc(bank_free, 1)
                if t % 2 == 1:
                    split_hi(act, c0 + 2 + t // 2, t0 + t + 1)
                if t >= 1:
                    high(t - 1)
            high(KT - 1)
            dense_act(act, "gate_ret", lambda e, i, j, bank: e.activation(
                gate2[:, bass.ds(4 * i + j, 1), :], psum[:, bank:bank + 1, :], ACT.Sigmoid,
                bias=cols[:, bass.ds(4 * i + j + COLS["bgate"] + KT, 1)]).then_inc(bank_free, 1))
            t0, c0 = FIRST_TILE["ret_out"], FIRST_CHUNK["ret_out"]
            for t in range(KT):
                act.wait_ge(m_add, t + 1)
                act.activation(x_hi[:, t, :], mix[:, t, :], ACT.Copy).then_inc(m_hi, 1)
                if t % 2 == 1:
                    split_hi(act, c0 + 2 + t // 2, t0 + t + 1)
            dense_act(act, "out")
            norm2.act(act, lambda e, kt: e.wait_ge(bank_free, FIRST_TILE["out"] + kt + 5))

        @block.vector
        def _(dve):
            t0 = FIRST_TILE["ret_g"]

            def gated_low(t):
                dve.wait_ge(g_hi, t + 1)
                dve.tensor_tensor(y_lo[:, t, :], g_tmp[t % 4][:, :], y_hi[:, t, :].bitcast(F32), ALU.subtract)\
                   .then_inc(g_lo, 1)
            for t in range(KT):
                dve.wait_ge(bank_free, t0 + t + 5)
                dve.tensor_tensor(g_tmp[t % 4][:, :], g_tmp[t % 4][:, :], ret_y[:, t, :], ALU.mult).then_inc(g_mul, 1)
                if t >= 1:
                    gated_low(t - 1)
            gated_low(KT - 1)
            t0 = FIRST_TILE["ret_out"]
            dve.wait_ge(bank_free, t0 + 4)

            def mix_low(t):
                dve.wait_ge(m_hi, t + 1)
                dve.tensor_tensor(x_lo[:, t, :], mix[:, t, :], x_hi[:, t, :].bitcast(F32), ALU.subtract).then_inc(m_lo, 1)
            for t in range(KT):
                dve.wait_ge(tile_done, t0 + t + 1)
                if t >= 4:
                    dve.wait_ge(m_add, t - 3)
                dve.tensor_tensor(m_tmp[t % 4][:, :], psum[:, (t0 + t) % 4, :], gate2[:, t, :], ALU.mult)\
                   .then_inc(bank_free, 1)
                dve.wait_ge(bank_free, t0 + t + 5)
                dve.tensor_tensor(mix[:, t, :], mix[:, t, :], m_tmp[t % 4][:, :], ALU.add).then_inc(m_add, 1)
                if t >= 1:
                    mix_low(t - 1)
            mix_low(KT - 1)
            t0 = FIRST_TILE["out"]
            for t in range(KT):
                dve.wait_ge(tile_done, t0 + t + 1)
                dve.tensor_tensor(res[:, t, :], res[:, t, :], psum[:, (t0 + t) % 4, :], ALU.add).then_inc(bank_free, 1)
            dve.wait_ge(bank_free, t0 + KT + 4)
            norm2.vector(dve, lambda e, kt: None)

        @block.tensor
        def _(pe):
            dense_pe(pe, "ret_g", x_hi, x_lo)
            dense_pe(pe, "gate_ret", x_hi, x_lo, drain=False)
            pe.wait_ge(g_lo, KT)
            dense_pe(pe, "ret_out", y_hi, y_lo)
            pe.wait_ge(m_lo, KT)
            dense_pe(pe, "out", x_hi, x_lo)
            norm2.pe(pe)


    LISTS = NE * TB + 2
    hn_rows = nc.dram_tensor("hn_rows", [S, D], F32).ap()
    slots = nc.dram_tensor("slots", [P * LISTS, 1], I32).ap()
    expert_rows = nc.dram_tensor("expert_rows", [2 * S + P, D], F32).ap()
    list_rows = at("list_rows", 139, [P, LISTS], I32)
    list_tokens = at("list_tokens", 139.28125, [P, LISTS], I32)
    row_col = [at(f"row_col{b}", 139.5625 + b / 32, [P, 1], I32) for b in range(2)]
    token_col = [at(f"token_col{b}", 139.625 + b / 32, [P, 1], I32) for b in range(2)]
    rounds_i = at("rounds_i", 139.6875, [P, 1], I32)
    gates2 = at("expert_gates", 139.75, [P, 2, TB])
    hn_tok = [at(f"hn_tok{b}", 160 + 4 * b, [P, D]) for b in range(2)]
    w_router = at("w_router", 168, [P, KT, NR])
    _small = [170.0]

    def small(name, shape, dt=F32):
        t = at("r_" + name, _small[0], shape, dt)
        _small[0] += (int(np.prod(shape[1:])) * 4 + 31) // 32 * 32 / 1024
        return t
    b_router, ranks, dest = small("bias", [P, NR]), small("ranks", [P, 36]), small("dest", [P, 2, TB], I32)
    lg, gmax, gdif, gexp, gsum, pg = (small(n, [P, TB] + s) for n, s in (
        ("logits", [NR]), ("gmax", []), ("gdif", [NG]), ("gexp", [NG]), ("gsum", []), ("pgroup", [])))
    geq, gord, gtop, goh, gpen = (small(n, [P, TB] + s) for n, s in (
        ("geq", [NG]), ("gord", [NG]), ("gtop", []), ("gone", [NG]), ("gpen", [NG])))
    ml, eeq, eord, etop = (small(n, [P, TB] + s) for n, s in (("masked", [NE]), ("eeq", [NE]), ("eord", [NE]), ("etop", [])))
    best = small("best", [P, 2, TB])
    eoh = small("eone", [P, 2, TB, NE])
    both = small("both", [P, TB, NE])
    edif, eexp, eden, einv = (small(n, [P, TB]) for n in ("edif", "eexp", "eden", "einv"))
    pick = small("pick", [P, 2, TB, NE])
    rank, eid, window, w1, slot_f = (small(n, [P, 2, TB]) for n in ("rank", "eid", "window", "w1", "slot_f"))
    slot_i = small("slot_i", [P, 2, TB], I32)
    cmax, rounds = small("cmax", [P, 1]), small("rounds", [P, 1])
    empty = small("empty", [P, LISTS], I32)
    r_in, lg_done, tr_done, tr_read, hn_stored, gdif_done, gexp_done, edif_done, eexp_done, both_done, rank_done, \
        slot_done, slots_zero, slots_full, list_landed = (sem("route_" + n) for n in (
            "in", "logits", "transposed", "rows_read", "rows_stored", "gdif", "gexp", "edif", "eexp", "both", "ranks",
            "slots", "zero", "full", "landed"))

    hn_half = [sem(f"route_rows_stored{b}") for b in range(2)]

    def wide(ap, shape, axis):
        return ap.unsqueeze(axis).to_broadcast(shape)

    with nc.Block() as block:
        @block.sync
        def _(sp):
            for t, n in ((w_router, "w_router"), (b_router, "b_router"), (ranks, "ranks"), (dest, "dest"), (empty, "empty")):
                sp.dma_start(t[tuple([slice(None)] * len(t.shape))], d[n]).then_inc(r_in, 16)
            sp.wait_ge(r_in, 80)
            sp.dma_start(slots.rearrange("(p l) o -> p (l o)", p=P), empty[:, :]).then_inc(slots_zero, 16)
            for q in range(TB):
                sp.wait_ge(tr_read, 2 * (q + 1))
                sp.dma_start(hn_rows[q * P:(q + 1) * P, :], hn_tok[q % 2][:, :])\
                  .then_inc(hn_half[q] if q < 2 else hn_stored, 16)
            sp.wait_ge(slots_full, 16 * 2 * TB)
            sp.dma_start(list_rows[:, :], slots.rearrange("(p l) o -> p (l o)", p=P)).then_inc(list_landed, 16)

        @block.tensor
        def _(pe):
            pe.wait_ge(r_in, 80)
            for q in range(TB):
                for kt in range(KT):
                    mm = pe.matmul(psum[:, q, 0:NR], hn[:, kt, q * P:(q + 1) * P], w_router[:, kt, :],
                                   start=(kt == 0), stop=(kt == KT - 1))
            mm.then_inc(lg_done, 1)
            for q in range(TB):
                for half in range(2):
                    if q >= 1:
                        pe.wait_ge(tr_read, 2 * q - 1 + half)
                    for k in range(4):
                        mm = pe.transpose(psum[:, 4 + half, k * P:(k + 1) * P],
                                          hn[:, 4 * half + k, q * P:(q + 1) * P], ident[:, :])
                    mm.then_inc(tr_done, 1)
            pe.wait_ge(both_done, 1)
            for q in range(TB):
                for q2 in range(q + 1):
                    mm = pe.matmul(psum[:, 6, q * NE:(q + 1) * NE], before[:, :] if q2 == q else ones[:, :],
                                   both[:, q2, :], start=(q == 0), stop=(q2 == q), skip_group_check=True)
            for q in range(TB):
                mm = pe.matmul(psum[:, 7, 0:NE], ones[:, :], both[:, q, :], start=(q == 0), stop=(q == TB - 1))
            mm.then_inc(rank_done, 1)

        @block.scalar
        def _(act):
            def row(n):
                q, half = n // 2, n % 2
                act.wait_ge(tr_done, n + 1)
                if q >= 2:
                    act.wait_ge(hn_half[q % 2], 16)
                act.activation(hn_tok[q % 2][:, half * 512:(half + 1) * 512], psum[:, 4 + half, :], ACT.Copy)\
                   .then_inc(tr_read, 1)
            for n in range(4):
                row(n)
            act.wait_ge(gdif_done, 1)
            act.activation(gexp[:, :, :], gdif[:, :, :], ACT.Exp).then_inc(gexp_done, 1)
            act.wait_ge(edif_done, 1)
            act.activation(eexp[:, :], edif[:, :], ACT.Exp).then_inc(eexp_done, 1)
            for n in range(4, 8):
                row(n)

        @block.vector
        def _(dve):
            def first_best(values, top, eq, order, otop, one, nth, n):
                link(dve, dve.tensor_reduce(top, values, AX.X, ALU.max))
                link(dve, dve.tensor_tensor(eq[:, :, :], values, wide(top, [P, TB, n], 2), ALU.is_equal))
                link(dve, dve.tensor_tensor(order[:, :, :], eq[:, :, :], wide(nth, [P, TB, n], 1), ALU.mult))
                link(dve, dve.tensor_reduce(otop[:, :], order[:, :, :], AX.X, ALU.max))
                link(dve, dve.tensor_tensor(one, order[:, :, :], wide(otop[:, :], [P, TB, n], 2), ALU.is_equal))

            dve.wait_ge(lg_done, 1)
            dve.wait_ge(r_in, 80)
            link(dve, dve.tensor_tensor(lg[:, :, :], psum[:, 0:TB, 0:NR], wide(b_router[:, :], [P, TB, NR], 1), ALU.add))
            gl, el = lg[:, :, 0:NG], lg[:, :, NG:NR].rearrange("p q (g e) -> p q g e", g=NG)
            first_best(gl, gmax[:, :], geq, gord, gtop, goh[:, :, :], ranks[:, 0:NG], NG)
            dve.tensor_tensor(gdif[:, :, :], gl, wide(gmax[:, :], [P, TB, NG], 2), ALU.subtract).then_inc(gdif_done, 1)
            link(dve, dve.tensor_scalar(gpen[:, :, :], goh[:, :, :], BIG, -BIG, ALU.mult, ALU.add))
            ml4 = ml[:, :, :].rearrange("p q (g e) -> p q g e", g=NG)
            for q in range(TB):
                dve.tensor_tensor(ml4[:, q], el[:, q], wide(goh[:, q, :], [P, NG, 4], 2), ALU.mult)
            link(dve, dve.engine_nop())
            for q in range(TB):
                ins = dve.tensor_tensor(ml4[:, q], ml4[:, q], wide(gpen[:, q, :], [P, NG, 4], 2), ALU.add)
            link(dve, ins)
            first_best(ml[:, :, :], best[:, 0, :], eeq, eord, etop, eoh[:, 0], ranks[:, NG:NG + NE], NE)
            link(dve, dve.scalar_tensor_tensor(out=ml[:, :, :], in0=eoh[:, 0], scalar=-2 * BIG, in1=ml[:, :, :],
                                               op0=ALU.mult, op1=ALU.add))
            first_best(ml[:, :, :], best[:, 1, :], eeq, eord, etop, eoh[:, 1], ranks[:, NG:NG + NE], NE)
            dve.tensor_tensor(edif[:, :], best[:, 1, :], best[:, 0, :], ALU.subtract).then_inc(edif_done, 1)
            dve.tensor_tensor(both[:, :, :], eoh[:, 0], eoh[:, 1], ALU.add).then_inc(both_done, 1)
            dve.wait_ge(gexp_done, 1)
            link(dve, dve.tensor_reduce(gsum[:, :], gexp[:, :, :], AX.X, ALU.add))
            link(dve, dve.reciprocal(pg[:, :], gsum[:, :]))
            dve.wait_ge(eexp_done, 1)
            link(dve, dve.tensor_scalar(eden[:, :], eexp[:, :], 1.0, None, ALU.add))
            link(dve, dve.reciprocal(einv[:, :], eden[:, :]))
            link(dve, dve.tensor_tensor(gates2[:, 0, :], einv[:, :], pg[:, :], ALU.mult))
            link(dve, dve.tensor_tensor(gates2[:, 1, :], gates2[:, 0, :], eexp[:, :], ALU.mult))
            for k in range(2):
                ins = dve.tensor_tensor(pick[:, k], eoh[:, k], wide(ranks[:, NG + NE:NG + 2 * NE], [P, TB, NE], 1), ALU.mult)
            link(dve, ins)
            for k in range(2):
                ins = dve.tensor_reduce(eid[:, k, :], pick[:, k], AX.X, ALU.add)
            link(dve, ins)
            dve.wait_ge(rank_done, 1)
            for k in range(2):
                ins = dve.tensor_tensor(pick[:, k], psum[:, 6, 0:TB * NE].rearrange("p (q e) -> p q e", e=NE),
                                        eoh[:, k], ALU.mult)
            link(dve, ins)
            for k in range(2):
                ins = dve.tensor_reduce(rank[:, k, :], pick[:, k], AX.X, ALU.add)
            link(dve, ins)
            link(dve, dve.tensor_scalar(w1[:, :, :], rank[:, :, :], float(P), None, ALU.is_ge))
            for n in (2, 3):
                src, dst = (w1, window) if n == 2 else (window, w1)
                link(dve, dve.scalar_tensor_tensor(out=dst[:, :, :], in0=rank[:, :, :], scalar=float(n * P),
                                                   in1=src[:, :, :], op0=ALU.is_ge, op1=ALU.add))
            link(dve, dve.tensor_scalar(slot_f[:, :, :], rank[:, :, :], float(LISTS), None, ALU.mult))
            link(dve, dve.scalar_tensor_tensor(out=slot_f[:, :, :], in0=w1[:, :, :], scalar=float(NE - P * LISTS),
                                               in1=slot_f[:, :, :], op0=ALU.mult, op1=ALU.add))
            link(dve, dve.tensor_tensor(slot_f[:, :, :], slot_f[:, :, :], eid[:, :, :], ALU.add))
            dve.tensor_copy(slot_i[:, :, :], slot_f[:, :, :]).then_inc(slot_done, 1)
            link(dve, dve.tensor_reduce(cmax[:, :], psum[:, 7, 0:NE], AX.X, ALU.max))
            link(dve, dve.tensor_scalar(rounds[:, :], cmax[:, :], float(P + 1), 1.0, ALU.is_ge, ALU.add))
            for n in (2, 3):
                link(dve, dve.scalar_tensor_tensor(out=rounds[:, :], in0=cmax[:, :], scalar=float(n * P + 1),
                                                   in1=rounds[:, :], op0=ALU.is_ge, op1=ALU.add))
            link(dve, dve.tensor_copy(rounds_i[:, :], rounds[:, :]))
            dve.wait_ge(list_landed, 16)
            dve.tensor_scalar(list_tokens[:, :], list_rows[:, :], S - 1, None, ALU.bitwise_and)

        @block.gpsimd
        def _(pool):
            pool.wait_ge(slots_zero, 16)
            pool.wait_ge(slot_done, 1)
            for k in range(2):
                for q in range(TB):
                    pool.indirect_dma_start(
                        out=slots, out_offset=bass.IndirectOffsetOnAxis(ap=slot_i[:, k, q:q + 1].bitcast(U32), axis=0),
                        in_=dest[:, k, q:q + 1], in_offset=None).then_inc(slots_full, 16)
            pool.wait_ge(slots_full, 16 * 2 * TB)

    ring = [at(f"moe_w{s}", (48 + 8 * s) if s < 8 else (144 + 8 * (s - 8)), [P, CHUNK_COLS]) for s in range(MOE_RING)]
    xg = [at(f"moe_x{b}", 176 + 4 * b, [P, D]) for b in range(2)]
    xt = [at(f"moe_xt{b}", 184 + 4 * b, [P, KT, P]) for b in range(2)]
    hid = [at(f"moe_h{b}", 140 + 2 * b, [P, FF]) for b in range(2)]
    hidt = [at(f"moe_ht{b}", 192 + 2 * b, [P, FF // P, P]) for b in range(2)]
    yo = [at(f"moe_y{b}", 196 + 4 * b, [P, D]) for b in range(2)]
    moe_landed = [sem(f"moe_landed{s}") for s in range(MOE_RING)]
    xg_landed = [sem(f"moe_x_landed{b}") for b in range(2)]
    y_stored = [sem(f"moe_y_stored{b}") for b in range(2)]
    tr = [sem(f"moe_x_transposed{b}") for b in range(2)]
    tr_ev = [sem(f"moe_x_read{b}") for b in range(2)]
    moe_used, col_done, pool_seen, y_free, silu_done, h_ready, ht_done, ht_read, yy_done, yy_read, credits = (
        sem("moe_" + n) for n in ("used", "column", "seen", "y_free", "silu", "hidden", "hidden_t", "hidden_t_read", "down",
                                  "down_read", "credits"))

    def rounds_of(eng):
        return eng.value_load(rounds_i[0:1, 0:1], min_val=1, max_val=TB)

    def expert_loop(eng, body):
        n_rounds = rounds_of(eng)
        with eng.Fori(0, n_rounds) as r:
            with eng.Fori(0, PAIRS) as i:
                body(r * PAIRS + i, i, r)
        return n_rounds

    with nc.Block() as block:
        @block.sync
        def _(sp):
            sp.wait_ge(credits, 1)

            def body(n, i, r):
                for s in range(MOE_RING):
                    sp.wait_ge(moe_used, MOE_RING * n + s + 1)
                    sp.dma_start(ring[s][:, :], d["w_moe"][bass.ds(i, 1), s].rearrange("a p n -> p (a n)"))\
                      .then_inc(moe_landed[s], 16)
            expert_loop(sp, body)

        @block.gpsimd
        def _(pool):
            def gather(n, b):
                pool.tensor_copy(token_col[b][:, :], list_tokens[:, bass.ds(2 * n + b, 1)]).then_inc(col_done, 1)
                pool.wait_ge(col_done, 4 * n + b + 1)
                pool.sem_inc(pool_seen, 1)
                pool.indirect_dma_start(
                    out=xg[b][:, :], out_offset=None, in_=hn_rows,
                    in_offset=bass.IndirectOffsetOnAxis(ap=token_col[b][:, :].bitcast(U32), axis=0))\
                    .then_inc(xg_landed[b], 16)

            def body(n, i, r):
                for b in range(2):
                    pool.wait_ge(tr[1], 2 * n + b + 1)
                    pool.sem_inc(pool_seen, 1)
                    pool.tensor_copy(row_col[b][:, :], list_rows[:, bass.ds(2 * n + b, 1)]).then_inc(col_done, 1)
                for b in range(2):
                    gather(n + 1, b)
                for b in range(2):
                    pool.wait_ge(yy_read, 4 * n + 2 * b + 4)
                    pool.sem_inc(pool_seen, 1)
                    pool.indirect_dma_start(
                        out=expert_rows, in_=yo[b][:, :], in_offset=None,
                        out_offset=bass.IndirectOffsetOnAxis(ap=row_col[b][:, :].bitcast(U32), axis=0))\
                        .then_inc(y_stored[b], 16)
                    pool.wait_ge(y_stored[b], 16 * n + 16)
                    pool.sem_inc(y_free, 1)
            for b in range(2):
                gather(0, b)
            n_rounds = expert_loop(pool, body)
            for b in range(2):
                pool.wait_ge(xg_landed[b], n_rounds * (16 * PAIRS) + 16)
                pool.sem_inc(pool_seen, 1)

        @block.tensor
        def _(pe):
            pe.sem_inc(moe_used, MOE_RING)
            pe.sem_inc(ht_read, 1)
            pe.sem_inc(yy_read, 2)
            pe.sem_inc(y_free, 2)
            pe.sem_inc(credits, 1)

            def body(n, i, r):
                for b in range(2):
                    pe.wait_ge(xg_landed[b], 16 * n + 16)
                    for half in range(2):
                        if b == 0 and half == 0:
                            pe.wait_ge(ht_read, 2 * n + 1)
                        if b == 1:
                            pe.wait_ge(tr_ev[half], 2 * n + 1)
                        for k in range(4):
                            mm = pe.transpose(psum[:, 6 + half, k * P:(k + 1) * P],
                                              xg[b][:, (4 * half + k) * P:(4 * half + k + 1) * P], ident[:, :])
                        mm.then_inc(tr[half], 1)
                for b in range(2):
                    pe.wait_ge(tr_ev[0], 2 * n + b + 1)
                    pe.wait_ge(tr_ev[1], 2 * n + b + 1)
                    for m in range(2):
                        for kt in range(KT):
                            s = 4 * b + 2 * m + kt // 4
                            if kt % 4 == 0:
                                pe.wait_ge(moe_landed[s], 16 * n + 16)
                            mm = pe.matmul(psum[:, 2 * b + m, :], xt[b][:, kt, :],
                                           ring[s][:, (kt % 4) * FF:(kt % 4 + 1) * FF], start=(kt == 0), stop=(kt == KT - 1))
                            if kt == 3:
                                mm.then_inc(moe_used, 1)
                        mm.then_inc(moe_used, 1)
                for b in range(2):
                    pe.wait_ge(h_ready, 2 * n + b + 1)
                    for k in range(4):
                        mm = pe.transpose(psum[:, 6, k * P:(k + 1) * P], hid[b][:, k * P:(k + 1) * P], ident[:, :])
                    mm.then_inc(ht_done, 1)
                    pe.wait_ge(ht_read, 2 * n + b + 2)
                    pe.wait_ge(moe_landed[8 + 2 * b], 16 * n + 16)
                    pe.wait_ge(moe_landed[9 + 2 * b], 16 * n + 16)
                    for half in range(2):
                        pe.wait_ge(yy_read, 4 * n + 2 * b + half + 1)
                        for k in range(4):
                            mm = pe.matmul(psum[:, 4 + half, :], hidt[b][:, k, :],
                                           ring[8 + 2 * b + k // 2][:, (k % 2) * D + half * 512:(k % 2) * D + half * 512 + 512],
                                           start=(k == 0), stop=(k == 3))
                        if half == 0:
                            mm.then_inc(yy_done, 1)
                        else:
                            mm.then_inc(moe_used, 2)
            expert_loop(pe, body)

        @block.scalar
        def _(act):
            def body(n, i, r):
                for b in range(2):
                    act.wait_ge(tr[0], 2 * n + b + 1)
                    act.activation(xt[b][:, 0:4, :].rearrange("p k n -> p (k n)"), psum[:, 6, :], ACT.Copy)\
                       .then_inc(tr_ev[0], 1)
                for b in range(2):
                    act.wait_ge(moe_used, MOE_RING * (n + 1) + 4 * b + 4)
                    act.activation(hid[b][:, :], psum[:, 2 * b, :], ACT.Silu).then_inc(silu_done, 1)
                for b in range(2):
                    for half in range(2):
                        if half == 0:
                            act.wait_ge(y_free, 2 * n + b + 1)
                            act.wait_ge(yy_done, 2 * n + b + 1)
                        else:
                            act.wait_ge(moe_used, MOE_RING * (n + 1) + 2 * b + 10)
                        act.activation(yo[b][:, half * 512:half * 512 + 512], psum[:, 4 + half, :], ACT.Copy)\
                           .then_inc(yy_read, 1)
            expert_loop(act, body)

        @block.vector
        def _(dve):
            def body(n, i, r):
                for b in range(2):
                    dve.wait_ge(tr[1], 2 * n + b + 1)
                    dve.tensor_copy(xt[b][:, 4:8, :].rearrange("p k n -> p (k n)"), psum[:, 7, :]).then_inc(tr_ev[1], 1)
                for b in range(2):
                    dve.wait_ge(silu_done, 2 * n + b + 1)
                    dve.tensor_tensor(hid[b][:, :], hid[b][:, :], psum[:, 2 * b + 1, :], ALU.mult).then_inc(h_ready, 1)
                for b in range(2):
                    dve.wait_ge(ht_done, 2 * n + b + 1)
                    dve.tensor_copy(hidt[b][:, :, :].rearrange("p k n -> p (k n)"), psum[:, 6, :]).then_inc(ht_read, 1)
            expert_loop(dve, body)

    yrow = [[at(f"yrow{k}{q}", 144 + 4 * (4 * k + q), [P, D]) for q in range(TB)] for k in range(2)]
    ysum = at("ysum", 176, [P, TB, D])
    yrows_landed = [sem(f"yrows_landed{q}") for q in range(TB)]
    ys1, ys2, yt_done, yt_added = (sem("moe_sum_" + n) for n in ("first", "both", "transposed", "added"))
    norm_end1 = Norm("norm_end1", res, "end1", 144, out=res)
    norm3 = Norm("norm3", res, "mix2", 154, hi=x_hi, lo=x_lo, bank=5)
    with nc.Block() as block:
        @block.sync
        def _(sp):
            for q in range(TB):
                for k in range(2):
                    sp.dma_start(yrow[k][q][:, :], expert_rows[k * S + q * P:k * S + (q + 1) * P, :])\
                      .then_inc(yrows_landed[q], 16)

        @block.vector
        def _(dve):
            def add(n):
                q, half = n // 2, n % 2
                dve.wait_ge(yt_done, n + 1)
                r4 = res[:, 4 * half:4 * half + 4, q * P:(q + 1) * P]
                dve.tensor_tensor(r4, r4, psum[:, 1 + n % 4, :].rearrange("p (k n) -> p k n", n=P), ALU.add)\
                   .then_inc(yt_added, 1)
            for q in range(TB):
                dve.wait_ge(yrows_landed[q], 32)
                dve.tensor_scalar(ysum[:, q, :], yrow[0][q][:, :], gates2[:, 0, q:q + 1], None, ALU.mult).then_inc(ys1, 1)
                dve.wait_ge(ys1, q + 1)
                dve.scalar_tensor_tensor(out=ysum[:, q, :], in0=yrow[1][q][:, :], scalar=gates2[:, 1, q:q + 1],
                                         in1=ysum[:, q, :], op0=ALU.mult, op1=ALU.add).then_inc(ys2, 1)
                if q >= 1:
                    add(2 * q - 2)
                    add(2 * q - 1)
            add(6)
            add(7)
            dve.wait_ge(yt_added, 8)
            norm_end1.vector(dve, lambda e, kt: None)
            norm3.vector(dve, lambda e, kt: None)

        @block.scalar
        def _(act):
            norm_end1.act(act, lambda e, kt: e.wait_ge(yt_added, 8))
            norm3.act(act, lambda e, kt: norm_end1.wait_scaled(e, kt + 1))

        @block.tensor
        def _(pe):
            for n in range(2 * TB):
                q, half = n // 2, n % 2
                pe.wait_ge(ys2, q + 1)
                if n >= 4:
                    pe.wait_ge(yt_added, n - 3)
                for k in range(4):
                    mm = pe.transpose(psum[:, 1 + n % 4, k * P:(k + 1) * P],
                                      ysum[:, q, (4 * half + k) * P:(4 * half + k + 1) * P], ident[:, :])
                mm.then_inc(yt_done, 1)
            norm_end1.pe(pe)
            norm3.pe(pe)


    qn = at("q_nope", 144, [P, 4, S])
    q_lat = at("q_lat", 152, [P, HEADS, S])
    q_r = at("q_rope", 168, [P, 2, S])
    k_r = at("k_rope", 172, [P, S])
    c_kv = at("c_kv", 174, [P, S])
    c_tok = at("c_tok", 176, [P, TB, P])
    bias = at("kept_bias", 178, [P, SPAN])
    q_b = at("q_b", 183, [P, 4, S])
    k_b = at("k_b", 191, [P, 4, S])
    v_b = at("v_b", 199, [P, TB, S])
    w_eff = at("w_eff", 207, [P, TB, HEADS])
    top8 = at("top8", 207.25, [P, 8])
    q_i = at("q_idx", 80, [P, 4, S])
    k_i = at("k_idx", 88, [P, 2, S])
    w_uk = at("w_uk", 92, [P, 4, P])
    relu = [at(f"relu{b}", 140 + 2 * b, [P, S]) for b in range(2)]
    kv_sq, kv_rms, kv_rstd = (at(f"kv_{n}", 152 + 2 * i, [P, S]) for i, n in enumerate(("sq", "rms", "rstd")))
    rot2 = Rotary("rot2", (96, 104))
    uk_landed, causal_landed, kv_squared, kv_summed, kv_rooted, kv_inverted, kv_normed, ct_done, ct_read, ql_done, \
        ql_read, li_done, li_relu, li_added, li_masked = (sem("proj_" + n) for n in (
            "w_uk", "causal", "kv_squared", "kv_summed", "kv_rooted", "kv_inverted", "kv_normed", "latents_t",
            "latents_t_read", "q_lat", "q_lat_read", "index", "index_relu", "index_added", "index_masked"))
    INDEX = [(qt, h, SEG[P * (qt + 1)], P * (qt + 1)) for qt in range(1, TB) for h in range(HEADS)]
    with nc.Block() as block:
        names = ("q_idx", "k_idx", "ckv_wi", "q_nope", "q_rope", "k_rope", "q_b", "k_b", "v_b")

        @block.sync
        def _(sp):
            sp.dma_start(w_uk[:, :, :], d["w_uk"]).then_inc(uk_landed, 16)
            o = SEG[P]
            sp.dma_start(bias[:, o:o + P], d["causal"][:, o:o + P]).then_inc(causal_landed, 16)
            for name in names:
                dense_sync(sp, name)

        @block.gpsimd
        def _(pool):
            def rope32(e, name, out):
                u = rot2.pairs["pool"]
                rot2.pairs["pool"] += 1
                e.wait_ge(bank_free, FIRST_TILE[name] + 2 + 4)
                e.tensor_tensor(out, rot2.t[u % 2][0][:, :], rot2.t[u % 2][1][:, :], ALU.add).then_inc(rot2.rotated, 2)

            dense_pool(pool, "q_idx", after=lambda e, i, b: rot2.pool(e, "q_idx", q_i, b))
            dense_pool(pool, "k_idx", after=lambda e, i, b: rot2.pool(e, "k_idx", k_i, b))
            dense_pool(pool, "ckv_wi")
            for qt in range(1, TB):
                o = SEG[P * (qt + 1)] + P * qt
                pool.wait_ge(li_added, HEADS * qt)
                pool.affine_select(out=bias[:, o:o + P], in_=bias[:, o:o + P], compare_op=ALU.is_ge, fill=-BIG,
                                   base=0, pattern=[[-1, P]], channel_multiplier=1).then_inc(li_masked, 1)
            dense_pool(pool, "q_nope")

            def q_rope(e, i, b):
                u = rot2.pairs["pool"]
                rot2.pairs["pool"] += 1
                e.wait_ge(bank_free, FIRST_TILE["q_rope"] + 2 * b + 2 + 4)
                e.tensor_tensor(q_r[:, b, :], rot2.t[u % 2][0][:, :], rot2.t[u % 2][1][:, :], ALU.add)\
                 .then_inc(rot2.rotated, 2)
            dense_pool(pool, "q_rope", after=q_rope)
            dense_pool(pool, "k_rope", after=lambda e, i, b: rope32(e, "k_rope", k_r[:, :]))
            dense_pool(pool, "q_b", after=lambda e, i, b: rot2.pool(e, "q_b", q_b, b))
            dense_pool(pool, "k_b", after=lambda e, i, b: rot2.pool(e, "k_b", k_b, b))
            dense_pool(pool, "v_b")

        @block.scalar
        def _(act):
            dense_act(act, "q_idx")
            dense_act(act, "k_idx")
            t0 = FIRST_TILE["ckv_wi"]
            act.wait_ge(tile_done, t0 + 1)
            act.activation(c_kv[:, :], psum[:, t0 % 4, :], ACT.Copy)
            act.activation(kv_sq[:, :], psum[:, t0 % 4, :], ACT.Square).then_inc(bank_free, 1)
            act.wait_ge(tile_done, t0 + 2)
            act.activation(w_eff[:, :, :].rearrange("p q h -> p (q h)"), psum[:, (t0 + 1) % 4, 0:TB * HEADS], ACT.Copy,
                           scale=HEADS ** -0.5 * HD ** -0.5).then_inc(bank_free, 1)
            split_hi(act, FIRST_CHUNK["ckv_wi"] + 2, t0 + 2)
            act.wait_ge(kv_summed, 1)
            act.activation(kv_rms[:, :], psum[:, 4, :], ACT.Sqrt, scale=1.0 / P, bias=col("eps")).then_inc(kv_rooted, 1)
            for u in range(len(INDEX)):
                n = INDEX[u][3]
                act.wait_ge(li_done, u + 1)
                if u >= 2:
                    act.wait_ge(li_added, u - 1)
                act.activation(relu[u % 2][:, 0:n], psum[:, 4 + u % 4, 0:n], ACT.Relu).then_inc(li_relu, 1)
            dense_act(act, "q_nope", lambda e, i, j, bank: e.activation(
                qn[:, j, :], psum[:, bank, :], ACT.Copy).then_inc(bank_free, 1))
            act.wait_ge(ct_done, 1)
            act.activation(c_tok[:, :, :].rearrange("p q c -> p (q c)"), psum[:, 7, :], ACT.Copy).then_inc(ct_read, 1)
            for h in range(HEADS):
                act.wait_ge(ql_done, h + 1)
                act.activation(q_lat[:, h, :], psum[:, 4 + h % 4, :], ACT.Copy).then_inc(ql_read, 1)
            for name in ("q_rope", "k_rope", "q_b", "k_b"):
                dense_act(act, name)
            dense_act(act, "v_b", lambda e, i, j, bank: e.activation(
                v_b[:, j % 4, 256 * (j // 4):256 * (j // 4) + 256], psum[:, bank, 0:256], ACT.Copy).then_inc(bank_free, 1))

        @block.vector
        def _(dve):
            rot2.vector(dve, "q_idx", 2)
            rot2.vector(dve, "k_idx", 1)
            dve.wait_ge(kv_rooted, 1)
            dve.reciprocal(kv_rstd[:, :], kv_rms[:, :]).then_inc(kv_inverted, 1)
            dve.wait_ge(kv_inverted, 1)
            dve.scalar_tensor_tensor(out=c_kv[:, :], in0=c_kv[:, :], scalar=col("kv"), in1=kv_rstd[:, :],
                                     op0=ALU.mult, op1=ALU.mult).then_inc(kv_normed, 1)
            dve.wait_ge(bank_free, FIRST_TILE["ckv_wi"] + 2 + 4)
            for u, (qt, h, o, n) in enumerate(INDEX):
                dve.wait_ge(li_relu, u + 1)
                if h == 0:
                    dve.tensor_scalar(bias[:, o:o + n], relu[u % 2][:, 0:n], w_eff[:, qt, h:h + 1], None, ALU.mult)\
                       .then_inc(li_added, 1)
                else:
                    dve.wait_ge(li_added, u)
                    dve.scalar_tensor_tensor(out=bias[:, o:o + n], in0=relu[u % 2][:, 0:n],
                                             scalar=w_eff[:, qt, h:h + 1], in1=bias[:, o:o + n],
                                             op0=ALU.mult, op1=ALU.add).then_inc(li_added, 1)

            def keep_eight(qt):
                o, n = SEG[P * (qt + 1)], P * (qt + 1)
                link(dve, dve.max(top8[:, :], bias[:, o:o + n]))
                link(dve, dve.match_replace(bias[:, o:o + n], top8[:, :], bias[:, o:o + n], -3e38))

            def rope32(name, pairs):
                for q in range(pairs):
                    u = rot2.pairs["dve"]
                    rot2.pairs["dve"] += 1
                    t0 = FIRST_TILE[name] + 2 * q
                    dve.wait_ge(tile_done, t0 + 2)
                    if u >= 2:
                        dve.wait_ge(rot2.rotated, 2 * (u - 1))
                    dve.tensor_tensor(rot2.t[u % 2][0][:, :], psum[:, t0 % 4, :], cos32[:, :], ALU.mult)\
                       .then_inc(bank_free, 1)
                    dve.tensor_tensor(rot2.t[u % 2][1][:, :], psum[:, (t0 + 1) % 4, :], sin32[:, :], ALU.mult)\
                       .then_inc(bank_free, 1)
            rounds8 = [qt for qt in range(1, TB) for _ in range(TOPK // 8)]
            turns8 = [lambda: rope32("q_rope", 2), lambda: rope32("k_rope", 1), lambda: rot2.vector(dve, "q_b", 2),
                      lambda: rot2.vector(dve, "k_b", 2)]
            dve.wait_ge(li_masked, TB - 1)
            done = 0
            for k, turn in enumerate(turns8):
                upto = len(rounds8) * (k + 1) // 5
                for qt in rounds8[done:upto]:
                    keep_eight(qt)
                done = upto
                turn()
            for qt in rounds8[done:]:
                keep_eight(qt)
            dve.tensor_scalar(bias[:, 0:SEG[P]], bias[:, 0:SEG[P]], -2e38, -BIG, ALU.is_gt, ALU.mult)
            o = SEG[2 * P]
            dve.tensor_scalar(bias[:, o:o + 2 * P], bias[:, o:o + 2 * P], -2e38, -BIG, ALU.is_gt, ALU.mult)

        @block.tensor
        def _(pe):
            dense_pe(pe, "q_idx", x_hi, x_lo)
            dense_pe(pe, "k_idx", x_hi, x_lo)
            c0, t0 = FIRST_CHUNK["ckv_wi"], FIRST_TILE["ckv_wi"]
            wh = w_hi[c0 % RING][:, :].rearrange("p (m k n) -> p m k n", k=KT, n=P)
            wl = w_lo[c0 % RING][:, :].rearrange("p (m k n) -> p m k n", k=KT, n=P)
            pe.wait_ge(lo_ready, c0 + 1)
            pe.wait_ge(bank_free, t0 + 4)
            for kt in range(KT):
                mm = three_pass(pe, psum[:, t0 % 4, :], wh[:, 0, kt, :], wl[:, 0, kt, :], x_hi[:, kt, :], x_lo[:, kt, :],
                                kt == 0, kt == KT - 1)
            mm.then_inc(tile_done, 1)
            for q in range(TB):
                for kt in range(KT):
                    tok = slice(q * P, (q + 1) * P)
                    out = psum[:, (t0 + 1) % 4, q * HEADS:(q + 1) * HEADS]
                    pe.matmul(out, x_hi[:, kt, tok], wh[:, 1, kt, 0:HEADS], start=(q == 0 and kt == 0), stop=False,
                              skip_group_check=True)
                    pe.matmul(out, x_hi[:, kt, tok], wl[:, 1, kt, 0:HEADS], start=False, stop=False,
                              skip_group_check=True)
                    mm = pe.matmul(out, x_lo[:, kt, tok], wh[:, 1, kt, 0:HEADS], start=False, stop=(kt == KT - 1),
                                   skip_group_check=True)
            mm.then_inc(tile_done, 1)
            pe.wait_ge(bank_free, t0 + 1 + 4)
            pe.matmul(psum[:, 4, :], ones[:, :], kv_sq[:, :], start=True, stop=True).then_inc(kv_summed, 1)
            pe.wait_ge(rot2.rotated, 2 * 3)
            pe.wait_ge(kv_rooted, 1)
            for u, (qt, h, o, n) in enumerate(INDEX):
                r, g = 32 * (h % 4), 2 * (h // 4)
                if u >= 4:
                    pe.wait_ge(li_relu, u - 3)
                for half in range(2):
                    mm = pe.matmul(psum[:, 4 + u % 4, 0:n], q_i[r:r + 32, g + half, qt * P:(qt + 1) * P],
                                   k_i[r:r + 32, half, 0:n], start=(half == 0), stop=(half == 1))
                mm.then_inc(li_done, 1)
            dense_pe(pe, "q_nope", x_hi, x_lo)
            pe.wait_ge(li_relu, len(INDEX))
            pe.wait_ge(kv_normed, 1)
            for q in range(TB):
                mm = pe.transpose(psum[:, 7, q * P:(q + 1) * P], c_kv[:, q * P:(q + 1) * P], ident[:, :])
            mm.then_inc(ct_done, 1)
            pe.wait_ge(uk_landed, 16)
            pe.wait_ge(bank_free, FIRST_TILE["q_nope"] + 4 + 4)
            for h in range(HEADS):
                r = HD * (h % 2)
                if h == 3:
                    pe.wait_ge(ct_read, 1)
                if h >= 4:
                    pe.wait_ge(ql_read, h - 3)
                pe.matmul(psum[:, 4 + h % 4, :], w_uk[r:r + HD, h // 2, :], qn[r:r + HD, h // 2, :], start=True, stop=True)\
                  .then_inc(ql_done, 1)
            for name in ("q_rope", "k_rope", "q_b", "k_b"):
                dense_pe(pe, name, x_hi, x_lo)
            dense_pe(pe, "v_b", x_hi, x_lo, token_major=True)

    A_HEADS = 2 * HEADS
    score = [at(f"score{b}", 48 + 5 * b, [P, SPAN]) for b in range(2)]
    prob_t = [at(f"prob_t{b}", 58 + 5 * b, [P, SPAN]) for b in range(2)]
    dil_bias = at("dil_bias", 68, [P, SPAN])
    o_lat = [at(f"o_lat{b}", 73 + 2 * b, [P, S]) for b in range(2)]
    smax, snmax, ssum, sinv = ([at(f"{n}{b}", 77 + (4 * i + b) / 32, [P, TB]) for b in range(2)]
                               for i, n in enumerate(("smax", "snmax", "ssum", "sinv")))
    w_uv = at("w_uv", 144, [P, HEADS, HD])
    a_in, s_done, s_read, s_exp, s_norm, t_done, t_read, ol_done, ol_read, av_done, av_high, av_low = (
        sem("att_" + n) for n in ("in", "scores", "scores_read", "exp", "normed", "probs_t", "probs_t_read", "latents",
                                  "latents_read", "values", "values_high", "values_low"))
    with nc.Block() as block:
        @block.sync
        def _(sp):
            sp.dma_start(w_uv[:, :, :], d["w_uv"]).then_inc(a_in, 16)
            sp.dma_start(dil_bias[:, :], d["dil_bias"]).then_inc(a_in, 16)

        @block.tensor
        def _(pe):
            def scores(h):
                if h >= 2:
                    pe.wait_ge(t_read, h - 1)
                for qt in reversed(range(TB)):
                    n = P * (qt + 1)
                    o = SEG[n]
                    out, q = Z[h % 2][:, o:o + n], slice(qt * P, (qt + 1) * P)
                    if h < HEADS:
                        r = 32 * (h % 4)
                        parts = [(q_lat[:, h, q], c_kv[:, 0:n]), (q_r[r:r + 32, h // 4, q], k_r[r:r + 32, 0:n])]
                    else:
                        r, g = 32 * (h % 4), 2 * (h % HEADS // 4)
                        parts = [(q_b[r:r + 32, g + half, q], k_b[r:r + 32, g + half, 0:n]) for half in range(2)]
                    for k, (lhs, rhs) in enumerate(parts):
                        mm = pe.matmul(out, lhs, rhs, start=(k == 0 and qt != 0), stop=(k == 1), skip_group_check=True)
                mm.then_inc(s_done, 1)

            def transposes(h):
                pe.wait_ge(s_norm, h + 1)
                for j in range(TB):
                    o, n = span(j)
                    for qt in range(j, TB):
                        src = SEG[P * (qt + 1)] + P * j
                        dst = o + P * (qt - j)
                        mm = pe.transpose(Z[h % 2][:, dst:dst + P], score[h % 2][:, src:src + P], ident[:, :])
                mm.then_inc(t_done, 1)

            def values(h):
                r = HD * (h % 2)
                pe.wait_ge(t_read, h + 1)
                if h < HEADS:
                    if h >= 1:
                        pe.wait_ge(ol_read, h)
                    out = psum[:, 6, :]
                else:
                    out = psum[r:r + HD, 7, :]
                    if h % 2 == 0:
                        pe.wait_ge(av_low, h // 2)
                for j in range(TB):
                    o, n = span(j)
                    lhs = c_tok[:, j, :] if h < HEADS else v_b[:, j, (h % HEADS) * HD:(h % HEADS + 1) * HD]
                    mm = pe.matmul(out[:, S - n:S], lhs, prob_t[h % 2][:, o:o + n], start=(j == 0), stop=(j == TB - 1),
                                   skip_group_check=True)
                mm.then_inc(ol_done if h < HEADS else av_done, 1)

            def from_latents(h):
                r = HD * (h % 2)
                pe.wait_ge(ol_read, h + 1)
                if h % 2 == 0 and h >= 2:
                    pe.wait_ge(av_low, h // 2)
                pe.matmul(psum[r:r + HD, 7, :], w_uv[:, h, :], o_lat[h % 2][:, :], start=True, stop=True)\
                  .then_inc(av_done, 1)
            pe.wait_ge(bank_free, FIRST_TILE["out2"] + 4)
            pe.wait_ge(a_in, 32)
            scores(0)
            for h in range(A_HEADS + 1):
                if h + 1 < A_HEADS:
                    scores(h + 1)
                if h >= 1:
                    values(h - 1)
                if h < A_HEADS:
                    transposes(h)
                if 1 <= h <= HEADS:
                    from_latents(h - 1)

        @block.vector
        def _(dve):
            def low(p):
                dve.wait_ge(av_high, p + 1)
                dve.tensor_tensor(y_lo[:, p, :], psum[:, 7, :], y_hi[:, p, :].bitcast(F32), ALU.subtract)\
                   .then_inc(av_low, 1)

            def softmax(h):
                b = h % 2
                scale = (HD + 32) ** -0.5 if h < HEADS else HD ** -0.5
                dve.wait_ge(s_done, h + 1)
                if h >= 2:
                    dve.wait_ge(t_done, h - 1)
                if h == HEADS:
                    dve.wait_ge(a_in, 32)
                link(dve, dve.tensor_tensor(score[b][:, :], Z[b], (bias if h < HEADS else dil_bias)[:, :], ALU.add))
                for qt in range(TB):
                    n = P * (qt + 1)
                    ins = dve.tensor_reduce(smax[b][:, qt:qt + 1], score[b][:, SEG[n]:SEG[n] + n], AX.X, ALU.max)
                link(dve, ins)
                dve.tensor_scalar(snmax[b][:, :], smax[b][:, :], -scale, None, ALU.mult).then_inc(s_read, 1)

            def normalise(h):
                b = h % 2
                dve.wait_ge(s_exp, h + 1)
                link(dve, dve.reciprocal(sinv[b][:, :], ssum[b][:, :]))
                for qt in range(TB):
                    n = P * (qt + 1)
                    ins = dve.tensor_scalar(score[b][:, SEG[n]:SEG[n] + n], score[b][:, SEG[n]:SEG[n] + n],
                                            sinv[b][:, qt:qt + 1], None, ALU.mult)
                ins.then_inc(s_norm, 1)
            softmax(0)
            for h in range(A_HEADS):
                if h >= 3 and h % 2 == 1:
                    low(h // 2 - 1)
                normalise(h)
                if h + 1 < A_HEADS:
                    softmax(h + 1)
            low(A_HEADS // 2 - 1)

        @block.scalar
        def _(act):
            def high(p):
                act.wait_ge(av_done, 2 * p + 2)
                act.activation(y_hi[:, p, :], psum[:, 7, :], ACT.Copy).then_inc(av_high, 1)

            def exp(h):
                b = h % 2
                scale = (HD + 32) ** -0.5 if h < HEADS else HD ** -0.5
                act.wait_ge(s_read, h + 1)
                for qt in range(TB):
                    n = P * (qt + 1)
                    ins = act.activation(score[b][:, SEG[n]:SEG[n] + n], score[b][:, SEG[n]:SEG[n] + n], ACT.Exp,
                                         bias=snmax[b][:, qt:qt + 1], scale=scale, accum_out=ssum[b][:, qt:qt + 1])
                ins.then_inc(s_exp, 1)

            def copy_t(h):
                act.wait_ge(t_done, h + 1)
                if h >= 2:
                    act.wait_ge(ol_done, min(h - 1, HEADS))
                if h - 2 >= HEADS:
                    act.wait_ge(av_done, h - 1)
                act.activation(prob_t[h % 2][:, :], Z[h % 2], ACT.Copy).then_inc(t_read, 1)

            def copy_latents(h):
                act.wait_ge(ol_done, h + 1)
                if h >= 2:
                    act.wait_ge(av_done, h - 1)
                act.activation(o_lat[h % 2][:, :], psum[:, 6, :], ACT.Copy).then_inc(ol_read, 1)
            exp(0)
            for h in range(A_HEADS):
                if h >= 3 and h % 2 == 1:
                    high(h // 2 - 1)
                if 1 <= h <= HEADS:
                    copy_latents(h - 1)
                copy_t(h)
                if h + 1 < A_HEADS:
                    exp(h + 1)
            high(A_HEADS // 2 - 1)


    m_high = at("mem_hi", 144, [P, KT, MEM], FR)
    m_low = at("mem_lo", 152, [P, KT, MEM], FR)
    mem = at("mem", 176, [P, KT, MEM])
    norm_mem = Norm("norm_mem", mem, "mem", 184, n_tok=MEM, hi=m_high, lo=m_low, bank=5)
    norm_cross = Norm("norm_cross", res, "cross", 160, hi=x_hi, lo=x_lo, bank=4)
    norm_mlp = Norm("norm_mlp", res, "mlp", 160, hi=x_hi, lo=x_lo, bank=4)
    qc = at("q_cross", 160, [P, KT, S])
    kc = at("k_cross", 176, [P, KT, MEM])
    vc = at("v_cross", 184, [P, MEM // P, D])
    cs = [at(f"cross_score{b}", 144 + 4 * b, [P, TB, MEM]) for b in range(2)]
    ct = [at(f"cross_prob_t{b}", 152 + 4 * b, [P, MEM // P, S]) for b in range(2)]
    cmx, cnm, csm, cin = ([at(f"{n}{b}", 192 + (4 * i + b) / 32, [P, TB]) for b in range(2)]
                          for i, n in enumerate(("cmax", "cnmax", "csum", "cinv")))
    mem_landed, cs_done, cs_max, cs_exp, cs_norm, ct_done2, ct_read2, cv_done, cv_high, cv_low = (
        sem("cross_" + n) for n in ("mem", "scores", "max", "exp", "normed", "probs_t", "probs_t_read", "values",
                                    "values_high", "values_low"))

    def add_residual(dve, name):
        t0 = FIRST_TILE[name]
        for t in range(KT):
            dve.wait_ge(tile_done, t0 + t + 1)
            dve.tensor_tensor(res[:, t, :], res[:, t, :], psum[:, (t0 + t) % 4, :], ALU.add).then_inc(bank_free, 1)

    with nc.Block() as block:
        names = ("out2", "k_mem", "v_mem", "q_cross", "o_cross")

        @block.sync
        def _(sp):
            sp.dma_start(mem[:, :, :], d["mem"]).then_inc(mem_landed, 16)
            for name in names:
                dense_sync(sp, name)

        @block.gpsimd
        def _(pool):
            for name in names:
                dense_pool(pool, name)

        @block.scalar
        def _(act):
            norm_mem.act(act, lambda e, kt: e.wait_ge(mem_landed, 16))
            dense_act(act, "out2")
            norm_cross.act(act, lambda e, kt: e.wait_ge(bank_free, FIRST_TILE["out2"] + kt + 5))
            dense_act(act, "k_mem", lambda e, i, j, bank: e.activation(
                kc[:, bass.ds(4 * i + j, 1), :], psum[:, bank:bank + 1, 0:MEM], ACT.Copy).then_inc(bank_free, 1))
            dense_act(act, "v_mem", lambda e, i, j, bank: e.activation(
                vc[:, j % 2, bass.ds(512 * i + 256 * (j // 2), 256)], psum[:, bank, 0:256], ACT.Copy)
                .then_inc(bank_free, 1))
            dense_act(act, "q_cross", lambda e, i, j, bank: e.activation(
                qc[:, bass.ds(4 * i + j, 1), :], psum[:, bank:bank + 1, :], ACT.Copy).then_inc(bank_free, 1))

            def exp(h):
                act.wait_ge(cs_max, h + 1)
                for q in range(TB):
                    ins = act.activation(cs[h % 2][:, q, :], flat[:, 1024 * (h % 2) + 256 * q:1024 * (h % 2) + 256 * (q + 1)],
                                         ACT.Exp, bias=cnm[h % 2][:, q:q + 1], scale=CH_DIM ** -0.5,
                                         accum_out=csm[h % 2][:, q:q + 1])
                ins.then_inc(cs_exp, 1)

            def copy_t(h):
                act.wait_ge(ct_done2, h + 1)
                if h >= 2:
                    act.wait_ge(cv_done, 2 * (h - 1))
                act.activation(ct[h % 2][:, :, :].rearrange("p m n -> p (m n)"), flat[:, 2048:3072], ACT.Copy)\
                   .then_inc(ct_read2, 1)

            def high(t):
                act.wait_ge(cv_done, t + 1)
                act.activation(y_hi[:, t, :], psum[:, 6 + t % 2, :], ACT.Copy).then_inc(cv_high, 1)
            exp(0)
            for h in range(CH_HEADS):
                if h + 1 < CH_HEADS:
                    exp(h + 1)
                copy_t(h)
                high(2 * h)
                high(2 * h + 1)
            dense_act(act, "o_cross")
            norm_mlp.act(act, lambda e, kt: e.wait_ge(bank_free, FIRST_TILE["o_cross"] + kt + 5))

        @block.vector
        def _(dve):
            norm_mem.vector(dve, lambda e, kt: None)
            add_residual(dve, "out2")
            dve.wait_ge(bank_free, FIRST_TILE["out2"] + KT + 4)
            norm_cross.vector(dve, lambda e, kt: None)

            def top(h):
                b = h % 2
                dve.wait_ge(cs_done, h + 1)
                link(dve, dve.tensor_reduce(cmx[b][:, :], flat[:, 1024 * b:1024 * b + 1024]
                                            .rearrange("p (q n) -> p q n", n=MEM), AX.X, ALU.max))
                dve.tensor_scalar(cnm[b][:, :], cmx[b][:, :], -CH_DIM ** -0.5, None, ALU.mult).then_inc(cs_max, 1)

            def normalise(h):
                b = h % 2
                dve.wait_ge(cs_exp, h + 1)
                link(dve, dve.reciprocal(cin[b][:, :], csm[b][:, :]))
                dve.tensor_tensor(cs[b][:, :, :], cs[b][:, :, :], wide(cin[b][:, :], [P, TB, MEM], 2), ALU.mult)\
                   .then_inc(cs_norm, 1)

            def low(t):
                dve.wait_ge(cv_high, t + 1)
                dve.tensor_tensor(y_lo[:, t, :], psum[:, 6 + t % 2, :], y_hi[:, t, :].bitcast(F32), ALU.subtract)\
                   .then_inc(cv_low, 1)
            top(0)
            for h in range(CH_HEADS):
                if h + 1 < CH_HEADS:
                    top(h + 1)
                normalise(h)
                if h >= 1:
                    low(2 * h - 2)
                    low(2 * h - 1)
            low(KT - 2)
            low(KT - 1)
            add_residual(dve, "o_cross")
            dve.wait_ge(bank_free, FIRST_TILE["o_cross"] + KT + 4)
            norm_mlp.vector(dve, lambda e, kt: None)

        @block.tensor
        def _(pe):
            dense_pe(pe, "out2", y_hi, y_lo, between=lambda: norm_mem.pe(pe))
            norm_mem.wait_split(pe)
            dense_pe(pe, "k_mem", m_high, m_low, n_tok=MEM, between=lambda: norm_cross.pe(pe))
            dense_pe(pe, "v_mem", m_high, m_low, token_major=True)
            norm_cross.wait_split(pe)
            dense_pe(pe, "q_cross", x_hi, x_lo)
            pe.wait_ge(bank_free, FIRST_TILE["o_cross"] + 4)

            def scores(h):
                b = h % 2
                if h >= 2:
                    pe.wait_ge(cs_exp, h - 1)
                for q in range(TB):
                    for half in range(2):
                        mm = pe.matmul(flat[:, 1024 * b + 256 * q:1024 * b + 256 * (q + 1)],
                                       qc[:, 2 * h + half, q * P:(q + 1) * P], kc[:, 2 * h + half, :],
                                       start=(half == 0 and q % 2 == 0), stop=(half == 1), skip_group_check=True)
                mm.then_inc(cs_done, 1)

            def transposes(h):
                pe.wait_ge(cs_norm, h + 1)
                if h >= 1:
                    pe.wait_ge(ct_read2, h)
                for m in range(MEM // P):
                    for q in range(TB):
                        mm = pe.transpose(psum[:, 4 + m, q * P:(q + 1) * P], cs[h % 2][:, q, m * P:(m + 1) * P], ident[:, :])
                mm.then_inc(ct_done2, 1)

            def values(h):
                pe.wait_ge(ct_read2, h + 1)
                for half in range(2):
                    if h >= 1:
                        pe.wait_ge(cv_low, 2 * h - 1 + half)
                    for m in range(MEM // P):
                        o = CH_DIM * h + P * half
                        mm = pe.matmul(psum[:, 6 + half, :], vc[:, m, o:o + P], ct[h % 2][:, m, :], start=(m == 0),
                                       stop=(m == 1))
                    mm.then_inc(cv_done, 1)
            scores(0)
            for h in range(CH_HEADS):
                if h + 1 < CH_HEADS:
                    scores(h + 1)
                transposes(h)
                values(h)
            pe.wait_ge(cv_low, KT)
            dense_pe(pe, "o_cross", y_hi, y_lo)
            norm_mlp.pe(pe)

    G = 4
    f_hi = [y_hi, at("f_hi", 144, [P, KT, S], FR)]
    f_lo = [y_lo, at("f_lo", 160, [P, KT, S], FR)]
    f_relu = [at(f"f_relu{b}", 176 + 2 * b, [P, S]) for b in range(4)]
    f_sq = [at(f"f_sq{b}", 196 + 2 * b, [P, S]) for b in range(2)]
    norm_end2 = Norm("norm_end2", res, "final", 184, out=res, bank=4)
    f_squared, f_high, f_low, stored = sem("mlp_squared"), sem("mlp_high"), sem("mlp_low"), sem("stored")
    ORDER = [n for n, _ in LAYERS[-2 * G:]]
    LAST = ORDER[-1]
    with nc.Block() as block:
        @block.sync
        def _(sp):
            for name in ORDER:
                dense_sync(sp, name)
            for k in range(4):
                norm_end2.wait_scaled(sp, 2 * (k + 1))
                sp.dma_start(d["out"][:, 2 * k:2 * k + 2, :], res[:, 2 * k:2 * k + 2, :]).then_inc(stored, 16)
            sp.wait_ge(stored, 64)

        @block.gpsimd
        def _(pool):
            for name in ORDER[:-1]:
                dense_pool(pool, name)
            for b in range(RING):
                split_lo(pool, FIRST_CHUNK[LAST] + 2 + b)

        @block.scalar
        def _(act):
            for name in ORDER:
                t0, c0, g = FIRST_TILE[name], FIRST_CHUNK[name], int(name[-1])
                if name[:2] == "up":
                    for t in range(KT):
                        act.wait_ge(tile_done, t0 + t + 1)
                        if KT * g + t >= 4:
                            act.wait_ge(f_squared, KT * g + t - 3)
                        act.activation(f_relu[t % 4][:, :], psum[:, (t0 + t) % 4, :], ACT.Relu).then_inc(bank_free, 1)
                        act.wait_ge(bank_free, t0 + t + 5)
                        act.activation(f_hi[g % 2][:, t, :], f_relu[t % 4][:, :], ACT.Square).then_inc(f_high, 1)
                        if t % 2 == 1:
                            split_hi(act, c0 + 2 + t // 2, t0 + t + 1)
                elif name != LAST:
                    dense_act(act, name)
                else:
                    for b in range(RING):
                        split_hi(act, c0 + 2 + b, t0 + 2 * (b + 1))
            norm_end2.act(act, lambda e, kt: e.wait_ge(bank_free, FIRST_TILE[LAST] + kt + 5))

        @block.vector
        def _(dve):
            def low(g, t):
                dve.wait_ge(f_high, KT * g + t + 1)
                dve.wait_ge(f_squared, KT * g + t + 1)
                dve.tensor_tensor(f_lo[g % 2][:, t, :], f_sq[t % 2][:, :], f_hi[g % 2][:, t, :].bitcast(F32),
                                  ALU.subtract).then_inc(f_low, 1)
            for name in ORDER:
                t0, g = FIRST_TILE[name], int(name[-1])
                if name[:2] == "up":
                    for t in range(KT):
                        dve.wait_ge(bank_free, t0 + t + 5)
                        if KT * g + t >= 2:
                            dve.wait_ge(f_low, KT * g + t - 1)
                        dve.tensor_tensor(f_sq[t % 2][:, :], f_relu[t % 4][:, :], f_relu[t % 4][:, :], ALU.mult)\
                           .then_inc(f_squared, 1)
                        if t >= 1:
                            low(g, t - 1)
                    low(g, KT - 1)
                else:
                    add_residual(dve, name)
            dve.wait_ge(bank_free, FIRST_TILE[LAST] + KT + 4)
            norm_end2.vector(dve, lambda e, kt: None)

        @block.tensor
        def _(pe):
            norm_mlp.wait_split(pe)
            for name in ORDER:
                g = int(name[-1])
                if name[:2] == "up":
                    dense_pe(pe, name, x_hi, x_lo)
                else:
                    pe.wait_ge(f_low, KT * (g + 1))
                    dense_pe(pe, name, f_hi[g % 2], f_lo[g % 2])
            norm_end2.pe(pe)


def _chunks(w, kts=KT):
    k, n = w.shape
    per = CHUNK_COLS // (kts * P)
    w = w.reshape(kts, P, n // (per * P), per, P)
    return np.ascontiguousarray(w.transpose(2, 1, 3, 0, 4)).reshape(-1, P, CHUNK_COLS)


def _halves(width, heads, first):
    c = np.arange(width * heads).reshape(heads, 2, width // 2) + first * width
    return [c[:, 0].ravel(), c[:, 1].ravel()]


def _pad(w, n):
    return np.concatenate([w, np.zeros((w.shape[0], n - w.shape[1]), w.dtype)], axis=1)


def _cols(g):
    return np.asarray(g).reshape(-1, P).T


def _layout(v):
    a = {k: np.asarray(x) for k, x in v.items()}
    w_in, w_in2 = a["w_in"][0], a["w_in_2"][0]
    rope_half = [np.concatenate(_halves(HD, 4, 0)), np.concatenate(_halves(HD, 4, 4))]
    rh = np.concatenate(rope_half)
    o = np.cumsum([0, 512, 512, 512, 512, 512, 1024, 1024])
    wg, wd, wu = a["w_gate"][0], a["w_down_2"][0], a["w_up_2"][0]
    o2 = np.cumsum([0, 512, 256, 128, 32, 512, 64, 8, 512, 512, 512])
    r = np.arange(256).reshape(8, 32)
    swapped = np.concatenate([r[:, 16:], r[:, :16]], axis=1)
    qr = np.concatenate([r[:4].ravel(), swapped[:4].ravel(), r[4:].ravel(), swapped[4:].ravel()])
    kr = np.concatenate([np.tile(r[0], 4), np.tile(swapped[0], 4)])
    ki = np.concatenate([np.tile(np.arange(32), 4), np.tile(np.arange(32, 64), 4)])
    wkv = a["w_kv_cross_2"][0]
    parts = {
        "sb_q": w_in[:, o[0]:o[1]], "sb_k": w_in[:, o[1]:o[2]], "sb_v": w_in[:, o[2]:o[3]],
        "gate_sb": wg[:, :D], "sb_out": a["w_sb_out"][0],
        "ret_q": w_in[:, o[3] + rh], "ret_k": w_in[:, o[4] + rh], "ret_v": w_in[:, o[5]:o[6]],
        "ret_g": w_in[:, o[6]:o[7]], "gate_ret": wg[:, D:], "ret_out": a["w_ret_out"][0], "out": a["w_out"][0],
        "q_nope": w_in2[:, o2[0]:o2[1]], "q_rope": w_in2[:, o2[1] + qr], "k_rope": w_in2[:, o2[3] + kr],
        "ckv_wi": _pad(np.concatenate([w_in2[:, o2[2]:o2[3]], w_in2[:, o2[6]:o2[7]]], axis=1), 256),
        "q_idx": w_in2[:, o2[4] + rh], "k_idx": w_in2[:, o2[5] + ki],
        "q_b": w_in2[:, o2[7] + rh], "k_b": w_in2[:, o2[8] + rh], "v_b": w_in2[:, o2[9]:o2[10]],
        "out2": a["w_out_2"][0], "q_cross": a["w_q_cross_2"][0], "k_mem": wkv[:, :D], "v_mem": wkv[:, D:],
        "o_cross": a["w_o_cross_2"][0],
    }
    for g in range(4):
        parts[f"up{g}"] = wu[:, g * D:(g + 1) * D]
        parts[f"down{g}"] = wd[g * D:(g + 1) * D, :]
    w_dense = np.concatenate([_chunks(parts[n], 4 if n == "sb_out" else KT) for n, _ in LAYERS])
    assert w_dense.shape[0] == N_CHUNKS

    def expert(w, k, n):
        return w[0].reshape(NE, 2, k // 256, P, n).transpose(0, 1, 3, 2, 4).reshape(NE, 2, P, CHUNK_COLS)
    ge, ue = expert(a["w_exp_gate"], D, FF), expert(a["w_exp_up"], D, FF)
    de = expert(a["w_exp_down"], FF, D)
    gu = np.concatenate([ge, ue], axis=1).reshape(PAIRS, 8, P, CHUNK_COLS)
    w_moe = np.concatenate([gu, de.reshape(PAIRS, 4, P, CHUNK_COLS)], axis=1)

    f32 = np.float32
    params = np.concatenate([_cols(a["norm_mix_g"]), _cols(a["b_gate"]), _cols(a["ret_norm_g"]), _cols(a["norm_ffn_g"]),
                             _cols(a["norm_final_g"]),
                             _cols(a["norm_mix_g_2"]), _cols(a["kv_norm_g_2"]), _cols(a["norm_cross_g_2"]),
                             _cols(a["norm_mem_g_2"]), _cols(a["norm_mlp_g_2"]), _cols(a["norm_final_g_2"]),
                             np.full((P, 1), EPS, f32)], axis=1)
    pos = np.arange(S, dtype=f32)

    def angle(n):
        inv = np.power(f32(10000.0), -np.arange(n, dtype=f32) / f32(n)).astype(f32)
        return (pos[None, :] * inv[np.arange(P) % n][:, None]).astype(f32).astype(np.float64)
    sign = np.where(np.arange(P) % 32 < 16, -1.0, 1.0)[:, None]
    i = np.arange(P)
    log_gamma = np.log(1.0 - 2.0 ** (-5.0 - np.arange(HEADS)))
    cc = np.arange(S)
    dist = np.abs(cc[None, :] - i[:, None])
    seen = cc[None, :] // 64 >= i[:, None] // 64
    decay = np.exp(log_gamma[:, None, None] * dist) * seen * HD ** -0.5
    rel = (np.arange(S)[:, None] - np.arange(S)[None, :])
    count = ((rel >= 0) & (rel <= 128)).astype(float) + ((rel >= 0) & (rel % 4 == 0)) + ((rel >= 0) & (rel % 16 == 0))
    dil = np.where(count > 0, np.log(np.maximum(count, 1)) * HD ** 0.5, -BIG)
    dil_bias = np.zeros((P, SPAN))
    causal = np.zeros((P, SPAN))
    for q in range(TB):
        n = P * (q + 1)
        dil_bias[:, SEG[n]:SEG[n] + n] = dil[q * P:(q + 1) * P, :n]
        causal[:, SEG[n]:SEG[n] + n] = np.where(rel[q * P:(q + 1) * P, :n] >= 0, 0, -BIG)
    wuk, wuv = a["w_uk_2"][0], a["w_uv_2"][0]
    small = np.concatenate([a["w_group_router"][0], a["w_expert_router"][0]], axis=1)
    return {
        "x": np.ascontiguousarray(a["x"][0].T.reshape(KT, P, S).transpose(1, 0, 2)),
        "mem": np.ascontiguousarray(a["mem_2"][0].T.reshape(KT, P, MEM).transpose(1, 0, 2)),
        "w_dense": w_dense, "w_moe": w_moe, "cols": np.ascontiguousarray(params),
        "w_router": np.ascontiguousarray(small.reshape(KT, P, NR).transpose(1, 0, 2)),
        "b_router": np.ascontiguousarray(np.broadcast_to(
            np.concatenate([a["b_group_router"][0], a["b_expert_router"][0]])[None, :], (P, NR))),
        "w_uk": np.ascontiguousarray(wuk.reshape(4, P, P).transpose(1, 0, 2)),
        "w_uv": np.ascontiguousarray(wuv.transpose(1, 0, 2)),
        "ident": np.eye(P, dtype=f32), "neg_tri": -(i[:, None] >= i[None, :]).astype(f32),
        "before": (i[:, None] < i[None, :]).astype(f32),
        "cos64": np.cos(angle(FREQ)).astype(f32), "sin64": np.sin(angle(FREQ)).astype(f32),
        "cos32": np.cos(angle(FREQ_R)).astype(f32), "sin32": (sign * np.sin(angle(FREQ_R))).astype(f32),
        "decay": decay.astype(f32), "dil_bias": dil_bias.astype(f32), "causal": causal.astype(f32),
        "ranks": np.broadcast_to(np.concatenate([4.0 - np.arange(4), 16.0 - np.arange(16), np.arange(16)]),
                                 (P, 36)).astype(f32),
        "dest": (np.arange(2)[None, :, None] * S + np.arange(TB)[None, None, :] * P + i[:, None, None]).astype(np.int32),
        "empty": np.broadcast_to(2 * S + i[:, None], (P, NE * TB + 2)).astype(np.int32),
    }


def kernel(**inputs):
    import concourse.bacc as _bacc
    from concourse.bass_utils import run_bass_kernel_spmd as _run

    nc = _bacc.Bacc("TRN2", target_bir_lowering=False, num_devices=1)
    arrays, d = {}, {}
    for name, a in _layout(inputs).items():
        arrays[f"in_{name}"] = a
        d[name] = nc.dram_tensor(f"in_{name}", a.shape, mybir.dt.from_np(a.dtype), kind="ExternalInput").ap()
    d["out"] = nc.dram_tensor("out", [P, KT, S], F32, kind="ExternalOutput").ap()
    build(nc, d)
    r = _run(nc, [arrays], core_ids=[0])
    got = r.results[0]["out"]
    return got.transpose(1, 0, 2).reshape(D, S).T[None]
```

```python
import numpy as np

import concourse.bass as bass
from concourse import mybir

F32 = mybir.dt.float32
FR = mybir.dt.float32r
I32 = mybir.dt.int32
U32 = mybir.dt.uint32
ACT = mybir.ActivationFunctionType
ALU = mybir.AluOpType
AX = mybir.AxisListType

P = 128
D = 1024
S = 512
KT = D // P
TB = S // P
HEADS = 8
HD = 64
RV = 128
NG, NE = 4, 16
NR = NG + NE
FF = 512
MEM = 256
CH_HEADS, CH_DIM = 4, 256
TOPK = min(256, S // 4)
FREQ = HD // 2
FREQ_R = 16
EPS = 1e-6
BIG = 1e30
CHUNK_COLS = 2048
RING = 2
MOE_RING = 12
MOE_AHEAD = 4
PAIRS = NE // 2

SEG = {512: 0, 384: 512, 128: 896, 256: 1024}
SPAN = 1280

COLS = {}
_at = 0
for _name, _n in [("mix", KT), ("bgate", 2 * KT), ("ret", KT), ("ffn", KT), ("end1", KT), ("mix2", KT), ("kv", 1),
                  ("cross", KT), ("mem", KT), ("mlp", KT), ("final", KT), ("eps", 1)]:
    COLS[_name] = _at
    _at += _n
N_COLS = _at

LAYERS = [("sb_q", 2), ("sb_k", 2), ("sb_v", 2), ("gate_sb", 4), ("sb_out", 2),
          ("ret_q", 2), ("ret_k", 2), ("ret_v", 4), ("ret_g", 4), ("gate_ret", 4), ("ret_out", 4), ("out", 4),
          ("k_mem", 4), ("v_mem", 4),
          ("q_idx", 2), ("k_idx", 1), ("ckv_wi", 1), ("q_nope", 2), ("q_rope", 2), ("k_rope", 1),
          ("q_b", 2), ("k_b", 2), ("v_b", 2), ("out2", 4), ("q_cross", 4),
          ("o_cross", 4), ("up0", 4), ("up1", 4), ("down0", 4), ("up2", 4), ("down1", 4), ("up3", 4), ("down2", 4),
          ("down3", 4)]
TILES_OF = {"sb_v": 8, "sb_out": 8, "ret_v": 16, "v_b": 8, "v_mem": 8}
FIRST_CHUNK, FIRST_TILE = {}, {}
_c = _t = 0
for _name, _n in LAYERS:
    FIRST_CHUNK[_name], FIRST_TILE[_name] = _c, _t
    _c += _n
    _t += TILES_OF.get(_name, 2 * _n)
N_CHUNKS = _c
N_OF = dict(LAYERS)


def build(nc, d):
    BASE = 16512

    def at(name, kb, shape, dt=F32):
        return nc.alloc_sbuf_tensor_at(name, shape, dt, offset=BASE + int(kb * 1024))

    def sem(name):
        return nc.alloc_semaphore(name)

    raw = [at(f"raw{b}", 8 * b, [P, CHUNK_COLS]) for b in range(RING)]
    w_hi = [at(f"w_hi{b}", 16 + 8 * b, [P, CHUNK_COLS], FR) for b in range(RING)]
    w_lo = [at(f"w_lo{b}", 32 + 8 * b, [P, CHUNK_COLS], FR) for b in range(RING)]
    x_hi = at("x_hi", 48, [P, KT, S], FR)
    x_lo = at("x_lo", 64, [P, KT, S], FR)
    y_hi = at("y_hi", 80, [P, KT, S], FR)
    y_lo = at("y_lo", 96, [P, KT, S], FR)
    res = at("res", 112, [P, KT, S])
    ident = at("ident", 128, [P, P])
    neg_tri = at("neg_tri", 128.5, [P, P])
    neg_ones = at("neg_ones", 129, [P, P])
    ones = at("ones", 129.5, [P, P])
    before = at("before", 130, [P, P])
    cos64 = at("cos64", 130.5, [P, S])
    sin64 = at("sin64", 132.5, [P, S])
    cos32 = at("cos32", 134.5, [P, S])
    sin32 = at("sin32", 136.5, [P, S])
    cols = at("cols", 138.5, [P, N_COLS])

    def col(name, i=0):
        return cols[:, COLS[name] + i:COLS[name] + i + 1]

    psum = nc.alloc_psum_tensor("psum", [P, 8, 512], F32)
    flat = psum[:, :, :].rearrange("p b n -> p (b n)")

    raw_landed = [sem(f"raw_landed{b}") for b in range(RING)]
    hi_ready = sem("hi_ready")
    lo_ready = sem("lo_ready")
    tile_done = sem("tile_done")
    bank_free = sem("bank_free")
    consts_landed = sem("consts_landed")

    def load_chunk(sp, c, i=0):
        if isinstance(c, int) and c >= N_CHUNKS:
            return
        if c >= RING:
            sp.wait_ge(lo_ready, c - 1 + RING * i)
        sp.dma_start(raw[c % RING][:, :], d["w_dense"][c + RING * i]).then_inc(raw_landed[c % RING], 16)

    def split_hi(act, c, tiles_before, i=0, ti=0):
        if c >= N_CHUNKS:
            return
        if c >= RING:
            act.wait_ge(tile_done, tiles_before + ti)
        act.wait_ge(raw_landed[c % RING], 16 * (c // RING + 1) + 16 * i)
        act.activation(w_hi[c % RING][:, :], raw[c % RING][:, :], ACT.Copy).then_inc(hi_ready, 1)

    def split_lo(pool, c, i=0):
        if c >= N_CHUNKS:
            return
        pool.wait_ge(hi_ready, c + 1 + RING * i)
        pool.tensor_tensor(w_lo[c % RING][:, :], raw[c % RING][:, :], w_hi[c % RING][:, :].bitcast(F32),
                           ALU.subtract).then_inc(lo_ready, 1)

    def loop(eng, n, body):
        if n == 1:
            body(0)
        else:
            with eng.Fori(0, n) as i:
                body(i)

    def turns(name):
        n = N_OF[name]
        return (n // 2, 2) if n % 2 == 0 else (1, 1)

    def per_chunk(name):
        return TILES_OF.get(name, 2 * N_OF[name]) // N_OF[name]

    def dense_sync(sp, name, after=None):
        n, k = turns(name)
        c0 = FIRST_CHUNK[name]

        def body(i):
            for b in range(k):
                load_chunk(sp, c0 + 4 + b, i)
                if after:
                    after(b)
        loop(sp, n, body)

    def dense_pool(pool, name, after=None, between=None):
        n, k = turns(name)
        c0 = FIRST_CHUNK[name]

        def body(i):
            for b in range(k):
                if after:
                    after(pool, i, b)
                split_lo(pool, c0 + 2 + b, i)
        if between:
            body(0)
            between()
            body(1)
        else:
            loop(pool, n, body)

    def dense_act(act, name, evac=None, between=None):
        n, k = turns(name)
        c0, t0, per = FIRST_CHUNK[name], FIRST_TILE[name], per_chunk(name)
        if evac and t0:
            act.wait_ge(bank_free, t0 + 4)

        def body(i):
            for b in range(k):
                for m in range(per if evac else 0):
                    j = per * b + m
                    act.wait_ge(tile_done, t0 + 1 + j + k * per * i)
                    act.wait_ge(consts_landed, N_CONSTS)
                    evac(act, i, j, (t0 + j) % 4)
                split_hi(act, c0 + 2 + b, t0 + per * (b + 1), i, k * per * i)
        if between:
            body(0)
            between()
            body(1)
        else:
            loop(act, n, body)

    def dense_vector(dve, name, evac):
        n, k = turns(name)
        t0, per = FIRST_TILE[name], per_chunk(name)
        assert n == 1 or (k * per) % 4 == 0
        dve.wait_ge(bank_free, t0 + 4)

        def body(i):
            for j in range(k * per):
                evac(dve, i, j, (t0 + j) % 4)
        loop(dve, n, body)

    def three_pass(pe, out, lh, ll, rh, rl, first, last):
        pe.matmul(out, lh, rh, start=first, stop=False)
        pe.matmul(out, lh, rl, start=False, stop=False)
        return pe.matmul(out, ll, rh, start=False, stop=last)

    def dense_pe(pe, name, ah, al, n_tok=S, kts=KT, token_major=False, between=None,
                 norm=None):
        n, k = turns(name)
        c0, t0, per = FIRST_CHUNK[name], FIRST_TILE[name], per_chunk(name)

        def body(i):
            for b in range(k):
                slot = (c0 + b) % RING
                wh = w_hi[slot][:, :].rearrange("p (m k n) -> p m k n", k=kts, n=P)
                wl = w_lo[slot][:, :].rearrange("p (m k n) -> p m k n", k=kts, n=P)
                pe.wait_ge(lo_ready, c0 + b + 1 + k * i)
                for m in range(per):
                    j = per * b + m
                    bank = (t0 + j) % 4
                    pe.wait_ge(bank_free, t0 + j + 1 + k * per * i)
                    for kt in range(kts):
                        if norm and j == 0:
                            norm.wait_split(pe, kt + 1)
                        if token_major:
                            mm = three_pass(pe, psum[:, bank, 0:2 * P], ah[:, kt, m * P:(m + 1) * P],
                                            al[:, kt, m * P:(m + 1) * P], wh[:, :, kt, :], wl[:, :, kt, :],
                                            kt == 0, kt == kts - 1)
                        else:
                            mm = three_pass(pe, psum[:, bank, 0:n_tok], wh[:, m, kt, :], wl[:, m, kt, :],
                                            ah[:, kt, 0:n_tok], al[:, kt, 0:n_tok], kt == 0, kt == kts - 1)
                    mm.then_inc(tile_done, 1)
        if between:
            body(0)
            between()
            body(1)
        else:
            loop(pe, n, body)

    warm = at("warm", 207.5, [P, 1])
    n_squared, n_added, n_summed, n_rooted, n_inverted, n_scaled, n_high, n_low = (
        sem("norm_" + x) for x in ("squared", "added", "summed", "rooted", "inverted", "scaled", "high", "low"))
    norms = {"sums": 0, "all": 0, "split": 0}

    class Norm:

        def __init__(self, tag, x, gain, temps_kb, n_tok=S, hi=None, lo=None, out=None, bank=0,
                     rstd_kb=None, y_kb=None, sums=True):
            self.x, self.gain, self.n, self.hi, self.lo, self.out, self.bank = x, gain, n_tok, hi, lo, out, bank
            self.u, self.a, self.s = norms["sums"], norms["all"], KT * norms["split"]
            norms["sums"] += sums
            norms["all"] += 1
            norms["split"] += hi is not None
            w = n_tok * 4 / 1024
            if sums:
                self.sq = [at(f"{tag}_sq{b}", temps_kb + w * b, [P, n_tok]) for b in range(2)]
                self.sum = at(f"{tag}_sum", temps_kb + 2 * w, [P, n_tok])
                self.rms = at(f"{tag}_rms", temps_kb + 3 * w, [P, n_tok])
                self.rstd = at(f"{tag}_rstd", temps_kb + 4 * w if rstd_kb is None else rstd_kb, [P, n_tok])
            if hi is not None:
                y_kb = temps_kb + 5 * w if y_kb is None else y_kb
                self.y = [at(f"{tag}_y{b}", y_kb + w * b, [P, n_tok]) for b in range(3)]

        def gain_of(self, kt):
            return col(self.gain, kt) if isinstance(self.gain, str) else self.gain[:, kt:kt + 1]

        def wait_scaled(self, eng, n):
            eng.wait_ge(n_scaled, KT * self.a + n)

        def wait_split(self, eng, n=KT):
            eng.wait_ge(n_low, self.s + n)

        def act(self, act, arrived):
            self.act_sum(act, arrived)
            self.act_split(act)

        def vector(self, dve, arrived):
            self.vector_sum(dve, arrived)
            self.vector_split(dve)

        def act_sum(self, act, arrived, meanwhile=None, root=True):
            if root:
                self.warm_up(act)
            for kt in range(KT):
                arrived(act, kt)
                self.square(act, kt)
            if meanwhile:
                meanwhile()
            if root:
                self.act_root(act)

        def warm_up(self, act):
            act.activation(warm[:, :], col("eps"), ACT.Sqrt)

        def square(self, act, kt):
            if kt >= 2:
                act.wait_ge(n_added, (KT - 1) * self.u + kt - 1)
            act.activation(self.sq[kt % 2][:, :], self.x[:, kt, :], ACT.Square).then_inc(n_squared, 1)

        def act_root(self, act):
            act.wait_ge(n_summed, self.u + 1)
            act.activation(self.rms[:, :], psum[:, self.bank, 0:self.n], ACT.Sqrt, scale=1.0 / D, bias=col("eps"))\
               .then_inc(n_rooted, 1)

        def act_split(self, act):
            if self.hi is not None:
                for kt in range(KT):
                    act.wait_ge(n_scaled, KT * self.a + kt + 1)
                    act.activation(self.hi[:, kt, :], self.y[kt % 3][:, :], ACT.Copy).then_inc(n_high, 1)

        def vector_sum(self, dve, arrived, invert=True):
            arrived(dve, KT - 1)
            for kt in range(1, KT):
                self.add_square(dve, kt)
            if invert:
                self.vector_invert(dve)

        def add_square(self, dve, kt):
            dve.wait_ge(n_squared, KT * self.u + kt + 1)
            if kt == 1:
                a, b = self.sq
            else:
                a, b = self.sum, self.sq[kt % 2]
                dve.wait_ge(n_added, (KT - 1) * self.u + kt - 1)
            dve.tensor_tensor(self.sum[:, :], a[:, :], b[:, :], ALU.add).then_inc(n_added, 1)

        def vector_invert(self, dve):
            dve.wait_ge(n_rooted, self.u + 1)
            dve.reciprocal(self.rstd[:, :], self.rms[:, :]).then_inc(n_inverted, 1)

        def vector_split(self, dve, ready=None):
            if ready:
                ready()
            else:
                dve.wait_ge(n_inverted, self.u + 1)

            def low(kt):
                dve.wait_ge(n_high, self.s + kt + 1)
                dve.tensor_tensor(self.lo[:, kt, :], self.y[kt % 3][:, :], self.hi[:, kt, :].bitcast(F32),
                                  ALU.subtract).then_inc(n_low, 1)
            for kt in range(KT):
                if self.hi is not None and kt >= 3:
                    dve.wait_ge(n_low, self.s + kt - 2)
                y = self.y[kt % 3][:, :] if self.hi is not None else self.out[:, kt, :]
                dve.scalar_tensor_tensor(out=y, in0=self.x[:, kt, :], scalar=self.gain_of(kt), in1=self.rstd[:, :],
                                         op0=ALU.mult, op1=ALU.mult).then_inc(n_scaled, 1)
                if self.hi is not None and kt >= 1:
                    low(kt - 1)
            if self.hi is not None:
                low(KT - 1)

        def pe(self, pe):
            pe.wait_ge(n_added, (KT - 1) * (self.u + 1))
            pe.matmul(psum[:, self.bank, 0:self.n], ones[:, :], self.sum[:, :], start=True, stop=True)\
              .then_inc(n_summed, 1)

    dve_step = sem("dve_step")
    steps = {"dve": 0}

    def link(dve, ins):
        steps["dve"] += 1
        ins.then_inc(dve_step, 1)
        dve.wait_ge(dve_step, steps["dve"])

    def add_residual(dve, name, norm=None):
        t0 = FIRST_TILE[name]
        dve.wait_ge(bank_free, t0 + 4)
        for t in range(KT):
            dve.wait_ge(tile_done, t0 + t + 1)
            dve.tensor_tensor(res[:, t, :], res[:, t, :], psum[:, (t0 + t) % 4, :], ALU.add).then_inc(bank_free, 1)
            if norm and t >= 2:
                norm.add_square(dve, t - 1)
        if norm:
            norm.add_square(dve, KT - 1)
            norm.vector_invert(dve)

    def residual_act(act, name, norm):
        c0, t0 = FIRST_CHUNK[name], FIRST_TILE[name]
        norm.warm_up(act)
        for t in range(KT):
            if t % 2 == 1:
                split_hi(act, c0 + 2 + t // 2, t0 + t + 1)
            act.wait_ge(bank_free, t0 + t + 5)
            norm.square(act, t)
        norm.act_root(act)

    sb_q = at("sb_q", 144, [P, 4, S])
    sb_k = at("sb_k", 152, [P, 4, S])
    sb_v = at("sb_v", 160, [P, TB, S])
    x_landed = [sem(f"x_landed{g}") for g in range(4)]
    norm1 = Norm("norm1", res, "mix", 170, hi=x_hi, lo=x_lo)
    CONSTS = [("ident", ident), ("neg_tri", neg_tri), ("before", before), ("cos64", cos64), ("sin64", sin64),
              ("cos32", cos32), ("sin32", sin32)]
    cols_landed = sem("cols_landed")
    N_CONSTS = 16 * len(CONSTS)
    fills = sem("fills")
    with nc.Block() as block:
        @block.sync
        def _(sp):
            sp.dma_start(cols[:, :], d["cols"]).then_inc(cols_landed, 16)
            for g in range(4):
                sp.dma_start(res[:, 2 * g:2 * g + 2, :], d["x"][:, 2 * g:2 * g + 2, :]).then_inc(x_landed[g], 16)
            load_chunk(sp, 0)
            load_chunk(sp, 1)
            for name, tile in CONSTS:
                sp.dma_start(tile[:, :], d[name]).then_inc(consts_landed, 16)
            load_chunk(sp, 2)
            load_chunk(sp, 3)
            for name in ("sb_q", "sb_k", "sb_v"):
                dense_sync(sp, name)

        @block.gpsimd
        def _(pool):
            pool.memset(ones[:, :], 1.0).then_inc(fills, 1)
            pool.memset(neg_ones[:, :], -1.0).then_inc(fills, 1)
            for c in range(RING):
                split_lo(pool, c)
            for name in ("sb_q", "sb_k", "sb_v"):
                dense_pool(pool, name)

        @block.vector
        def _(dve):
            dve.wait_ge(cols_landed, 16)
            norm1.vector(dve, lambda e, kt: [e.wait_ge(x_landed[g], 16) for g in range(4)])

        @block.scalar
        def _(act):
            act.wait_ge(cols_landed, 16)
            act.sem_inc(bank_free, 4)
            norm1.act_sum(act, lambda e, kt: e.wait_ge(x_landed[kt // 2], 16), lambda: split_hi(act, 0, 0))
            norm1.act_split(act)
            split_hi(act, 1, 0)
            dense_act(act, "sb_q", lambda e, i, j, bank: e.activation(
                sb_q[:, j, :], psum[:, bank, :], ACT.Copy, scale=HD ** -0.5).then_inc(bank_free, 1))
            dense_act(act, "sb_k", lambda e, i, j, bank: e.activation(
                sb_k[:, j, :], psum[:, bank, :], ACT.Copy).then_inc(bank_free, 1))
            dense_act(act, "sb_v", lambda e, i, j, bank: e.activation(
                sb_v[:, j % 4, 256 * (j // 4):256 * (j // 4) + 256], psum[:, bank, 0:256], ACT.Copy)
                .then_inc(bank_free, 1))

        @block.tensor
        def _(pe):
            pe.wait_ge(fills, 2)
            norm1.pe(pe)
            dense_pe(pe, "sb_q", x_hi, x_lo, norm=norm1)
            dense_pe(pe, "sb_k", x_hi, x_lo)
            dense_pe(pe, "sb_v", x_hi, x_lo, token_major=True)

    za = [at(f"sb_log{b}", 168 + 5 * b, [P, SPAN]) for b in range(2)]
    zw = [at(f"sb_weight{b}", 178 + 5 * b, [P, SPAN]) for b in range(2)]
    Z = [flat[:, 1536 * b:1536 * b + SPAN] for b in range(2)]
    z_done, log1p_steps, l_done, lm_done, c_done, w_done, wm_done, y_done, y_high, y_low = (
        sem("sb_" + n) for n in ("scores", "log1p_steps", "softplus", "masked", "logs", "weights",
                                 "weights_masked", "values", "high", "low"))

    def span(j):
        n = S - P * j
        return SEG[n], n

    with nc.Block() as block:
        @block.tensor
        def _(pe):
            pe.wait_ge(bank_free, FIRST_TILE["gate_sb"] + 4)

            def scores(h):
                r = HD * (h % 2)
                if h >= 2:
                    pe.wait_ge(w_done, h - 1)
                for j in range(TB):
                    o, n = span(j)
                    mm = pe.matmul(Z[h % 2][:, o:o + n], sb_k[r:r + HD, h // 2, j * P:(j + 1) * P],
                                   sb_q[r:r + HD, h // 2, j * P:S], start=(j != 3), stop=True, skip_group_check=True)
                mm.then_inc(z_done, 1)

            def logs(h):
                pe.wait_ge(lm_done, h + 1)
                for j in range(TB):
                    o, n = span(j)
                    mm = pe.matmul(Z[h % 2][:, o:o + n], neg_tri[:, :], za[h % 2][:, o:o + n],
                                   start=False, stop=True, skip_group_check=True)
                    for j2 in range(j + 1, TB):
                        o2, n2 = span(j2)
                        mm = pe.matmul(Z[h % 2][:, o + n - n2:o + n], neg_ones[:, :], za[h % 2][:, o2:o2 + n2],
                                       start=False, stop=True, skip_group_check=True)
                mm.then_inc(c_done, 1)

            def values(h):
                r = HD * (h % 2)
                pe.wait_ge(wm_done, h + 1)
                if h >= 4:
                    pe.wait_ge(y_low, (h - 4) // 2 + 1)
                for j in range(TB):
                    o, n = span(j)
                    mm = pe.matmul(psum[r:r + HD, 6 + h // 2 % 2, S - n:S], sb_v[:, j, h * HD:(h + 1) * HD],
                                   zw[h % 2][:, o:o + n], start=(j == 0), stop=(j == TB - 1), skip_group_check=True)
                mm.then_inc(y_done, 1)

            scores(0)
            for h in range(HEADS):
                if h + 1 < HEADS:
                    scores(h + 1)
                logs(h)
                if h >= 1:
                    values(h - 1)
            values(HEADS - 1)

        @block.vector
        def _(dve):
            def softplus(h):
                dve.wait_ge(log1p_steps, 3 * h + 3)
                dve.scalar_tensor_tensor(out=za[h % 2][:, :], in0=Z[h % 2], scalar=0.0, in1=za[h % 2][:, :],
                                         op0=ALU.max, op1=ALU.add).then_inc(l_done, 1)

            def low(p):
                dve.wait_ge(y_high, p + 1)
                dve.tensor_tensor(y_lo[:, p, :], psum[:, 6 + p % 2, :], y_hi[:, p, :].bitcast(F32), ALU.subtract)\
                   .then_inc(y_low, 1)
            for h in range(HEADS):
                softplus(h)
                if h >= 3 and h % 2 == 1:
                    low(h // 2 - 1)
            low(3)

        @block.scalar
        def _(act):
            def log1p(h):
                act.wait_ge(z_done, h + 1)
                if h >= 2:
                    act.wait_ge(c_done, h - 1)
                act.activation(za[h % 2][:, :], Z[h % 2], ACT.Abs).then_inc(log1p_steps, 1)
                act.wait_ge(log1p_steps, 3 * h + 1)
                act.activation(za[h % 2][:, :], za[h % 2][:, :], ACT.Exp, scale=-1.0).then_inc(log1p_steps, 1)
                act.wait_ge(log1p_steps, 3 * h + 2)
                act.activation(za[h % 2][:, :], za[h % 2][:, :], ACT.Ln, bias=1.0).then_inc(log1p_steps, 1)

            def weights(h):
                act.wait_ge(c_done, h + 1)
                if h >= 2:
                    act.wait_ge(y_done, h - 1)
                act.activation(zw[h % 2][:, :], Z[h % 2], ACT.Exp).then_inc(w_done, 1)

            def high(p):
                act.wait_ge(y_done, 2 * p + 2)
                act.activation(y_hi[:, p, :], psum[:, 6 + p % 2, :], ACT.Copy).then_inc(y_high, 1)
            act.preload_act_table_set("natural_log_exp_and_others")
            log1p(0)
            for h in range(HEADS):
                if h + 1 < HEADS:
                    log1p(h + 1)
                weights(h)
                if h >= 3 and h % 2 == 1:
                    high(h // 2 - 1)
            high(3)

        @block.gpsimd
        def _(pool):
            def mask(buf, done):
                for j in range(TB):
                    o, _ = span(j)
                    ins = pool.affine_select(out=buf[:, o:o + P], in_=buf[:, o:o + P], compare_op=ALU.is_gt, fill=0.0,
                                             base=0, pattern=[[1, P]], channel_multiplier=-1)
                ins.then_inc(done, 1)
            for h in range(HEADS):
                pool.wait_ge(l_done, h + 1)
                mask(za[h % 2], lm_done)
                pool.wait_ge(w_done, h + 1)
                mask(zw[h % 2], wm_done)


    gate = at("gate", 144, [P, KT, S])
    mix = at("mix", 190, [P, KT, S])
    ret_q = at("ret_q", 144, [P, 4, S])
    ret_k = at("ret_k", 152, [P, 4, S])
    ret_v = at("ret_v", 160, [P, TB, D])

    rotated, moved = sem("rotated"), [sem(f"rotated_moved{b}") for b in range(2)]
    rot_counts = {"rotated": 0, "moved": [0, 0]}

    class Rotary:

        def __init__(self, tag, temps_kb, layers):
            self.t = [[at(f"{tag}_t{b}{n}", temps_kb[b] + 2 * n, [P, S]) for n in range(4)] for b in range(2)]
            self.first, self.added, self.free, n = {}, [], [], rot_counts
            for name, pairs, moves in layers:
                self.first[name] = len(self.added)
                for _ in range(pairs):
                    b = len(self.added) % 2
                    n["rotated"] += 2
                    self.added.append(n["rotated"])
                    n["moved"][b] += 16 * moves
                    self.free.append((moved[b], n["moved"][b]) if moves else (rotated, self.added[-1]))

        def wait(self, eng, name, q):
            u = self.first[name] + q
            for v in (u - 1, u):
                eng.wait_ge(*self.free[v])

        def vector(self, dve, name, pairs, narrow=False):
            dve.wait_ge(bank_free, FIRST_TILE[name] + 4)
            for q in range(pairs):
                u = self.first[name] + q
                t = self.t[u % 2]
                t0 = FIRST_TILE[name] + 2 * q
                a, b = psum[:, t0 % 4, :], psum[:, (t0 + 1) % 4, :]
                dve.wait_ge(tile_done, t0 + 2)
                if u >= 2:
                    dve.wait_ge(*self.free[u - 2])
                if narrow:
                    dve.tensor_tensor(t[0][:, :], a, cos32[:, :], ALU.mult).then_inc(bank_free, 1)
                    dve.tensor_tensor(t[1][:, :], b, sin32[:, :], ALU.mult).then_inc(bank_free, 1)
                else:
                    dve.tensor_tensor(t[0][:, :], a, cos64[:, :], ALU.mult)
                    dve.tensor_tensor(t[3][:, :], a, sin64[:, :], ALU.mult).then_inc(bank_free, 1)
                    dve.tensor_tensor(t[1][:, :], b, sin64[:, :], ALU.mult)
                    dve.tensor_tensor(t[2][:, :], b, cos64[:, :], ALU.mult).then_inc(bank_free, 1)

        def pool(self, pool, name, q, narrow=False, narrow_out=None):
            t = self.t[(self.first[name] + q) % 2]
            pool.wait_ge(bank_free, FIRST_TILE[name] + 2 * q + 2 + 4)
            if narrow:
                narrow_out = t[0][:, :] if narrow_out is None else narrow_out
                pool.tensor_tensor(narrow_out, t[0][:, :], t[1][:, :], ALU.add).then_inc(rotated, 2)
            else:
                pool.tensor_tensor(t[0][:, :], t[0][:, :], t[1][:, :], ALU.subtract).then_inc(rotated, 1)
                pool.tensor_tensor(t[2][:, :], t[2][:, :], t[3][:, :], ALU.add).then_inc(rotated, 1)

        def move_narrow(self, sp, name, out, q):
            u = self.first[name] + q
            sp.wait_ge(rotated, self.added[u])
            for h in range(4):
                r = HD * (1 - h % 2)
                sp.dma_start(out[r:r + 32, 4 * q + h, :], self.t[u % 2][0][32 * h:32 * h + 32, :])\
                  .then_inc(moved[u % 2], 16)

        def move(self, sp, name, out, q, heads=4):
            u = self.first[name] + q
            sp.wait_ge(rotated, self.added[u])
            for h in range(heads):
                for half in range(2):
                    r = HD * (h % 2) + 32 * half
                    sp.dma_start(out[r:r + 32, 2 * q + h // 2, :], self.t[u % 2][2 * half][32 * h:32 * h + 32, :])\
                      .then_inc(moved[u % 2], 16)

    rot1 = Rotary("rot1", (88, 104), [("ret_q", 2, 8), ("ret_k", 2, 8)])
    names3 = ("gate_sb", "sb_out", "ret_q", "ret_k", "ret_v")

    def gate_sync(sp):
        for name in names3:
            to = {"ret_q": ret_q, "ret_k": ret_k}.get(name)
            dense_sync(sp, name, after=to and (lambda b: rot1.move(sp, name, to, b)))

    def gate_gpsimd(pool):
        for name in names3:
            dense_pool(pool, name, after=(lambda e, i, b: rot1.pool(e, name, b)) if name in rot1.first else None)

    def gate_scalar(act):
        dense_act(act, "gate_sb", lambda e, i, j, bank: e.activation(
            gate[:, bass.ds(4 * i + j, 1), :], psum[:, bank:bank + 1, :], ACT.Sigmoid,
            bias=cols[:, bass.ds(4 * i + j + COLS["bgate"], 1)]).then_inc(bank_free, 1))
        for name in ("sb_out", "ret_q", "ret_k"):
            dense_act(act, name)
        dense_act(act, "ret_v", lambda e, i, j, bank: e.activation(
            ret_v[:, j % 4, bass.ds(512 * i + 256 * (j // 4), 256)], psum[:, bank, 0:256], ACT.Copy)
            .then_inc(bank_free, 1))

    def gate_vector(dve):
        def gated(e, i, j, bank):
            e.wait_ge(tile_done, FIRST_TILE["sb_out"] + j + 1)
            e.tensor_tensor(mix[:, j, :], psum[:, bank, :], gate[:, j, :], ALU.mult).then_inc(bank_free, 1)
        dve.wait_ge(bank_free, FIRST_TILE["sb_out"] + 4)
        dense_vector(dve, "sb_out", gated)
        rot1.vector(dve, "ret_q", 2)
        rot1.vector(dve, "ret_k", 2)

    def gate_tensor(pe):
        dense_pe(pe, "gate_sb", x_hi, x_lo)
        dense_pe(pe, "sb_out", y_hi, y_lo, kts=4)
        dense_pe(pe, "ret_q", x_hi, x_lo)
        dense_pe(pe, "ret_k", x_hi, x_lo)
        dense_pe(pe, "ret_v", x_hi, x_lo, token_major=True)
    prod = [at(f"ret_prod{b}", 176 + 5 * b, [P, SPAN]) for b in range(2)]
    dec = [at(f"decay{b}", 186 + 2 * b, [P, S]) for b in range(2)]
    ret_y = at("ret_y", 80, [P, KT, S])
    rq = [[at(f"ret_{n}{b}", 96 + 2 * k + 8 * b, [P, S]) for b in range(2)] for k, n in enumerate(("sq", "rms", "rstd"))]
    r_landed = [sem(f"decay_landed{b}") for b in range(2)]
    rs_done, rp_done, rv_done, rc_done, rsq_done, rm_done, rr_done, ri_done, ry_done = (
        sem("ret_" + n) for n in ("scores", "decayed", "values", "copied", "squared", "summed", "rooted", "inverted",
                                  "normed"))
    def retention_first_decays(sp):
        for h in range(2):
            sp.dma_start(dec[h][:, :], d["decay"][h]).then_inc(r_landed[h], 16)

    def retention_sync(sp):
        for h in range(2, HEADS):
            sp.wait_ge(rp_done, h - 1)
            sp.dma_start(dec[h % 2][:, :], d["decay"][h]).then_inc(r_landed[h % 2], 16)

    def retention_tensor(pe):
        rot1.wait(pe, "ret_k", 1)
        pe.wait_ge(bank_free, FIRST_TILE["ret_g"] + 4)
        def scores(h):
            r = HD * (h % 2)
            if h >= 2:
                pe.wait_ge(rp_done, h - 1)
            for j in range(TB):
                o, n = span(j)
                mm = pe.matmul(Z[h % 2][:, o:o + n], ret_k[r:r + HD, h // 2, j * P:(j + 1) * P],
                               ret_q[r:r + HD, h // 2, j * P:S], start=(j != 3), stop=True, skip_group_check=True)
            mm.then_inc(rs_done, 1)

        def values(h):
            pe.wait_ge(rp_done, h + 1)
            if h >= 2:
                pe.wait_ge(rr_done, h - 1)
            for j in range(TB):
                o, n = span(j)
                mm = pe.matmul(psum[:, 6 + h % 2, S - n:S], ret_v[:, j, h * RV:(h + 1) * RV],
                               prod[h % 2][:, o:o + n], start=(j == 0), stop=(j == TB - 1), skip_group_check=True)
            mm.then_inc(rv_done, 1)

        def mean_square(h):
            pe.wait_ge(rsq_done, h + 1)
            pe.matmul(psum[:, 6 + h % 2, :], ones[:, :], rq[0][h % 2][:, :], start=True, stop=True)\
              .then_inc(rm_done, 1)
        scores(0)
        for h in range(HEADS):
            if h + 1 < HEADS:
                scores(h + 1)
            values(h)
            if h >= 1:
                mean_square(h - 1)
        mean_square(HEADS - 1)

    def retention_vector(dve):
        def decayed(h):
            dve.wait_ge(rs_done, h + 1)
            dve.wait_ge(r_landed[h % 2], 16 * (h // 2 + 1))
            if h >= 2:
                dve.wait_ge(rv_done, h - 1)
            for j in range(TB):
                o, n = span(j)
                ins = dve.tensor_tensor(prod[h % 2][:, o:o + n], Z[h % 2][:, o:o + n], dec[h % 2][:, 0:n], ALU.mult)
            ins.then_inc(rp_done, 1)

        def norm(h):
            dve.wait_ge(rr_done, h + 1)
            dve.reciprocal(rq[2][h % 2][:, :], rq[1][h % 2][:, :]).then_inc(ri_done, 1)
            dve.wait_ge(ri_done, h + 1)
            dve.scalar_tensor_tensor(out=ret_y[:, h, :], in0=ret_y[:, h, :], scalar=col("ret", h),
                                     in1=rq[2][h % 2][:, :], op0=ALU.mult, op1=ALU.mult).then_inc(ry_done, 1)
        for h in range(HEADS):
            decayed(h)
            if h >= 2:
                norm(h - 2)
        norm(HEADS - 2)
        norm(HEADS - 1)

    def retention_scalar(act):
        for h in range(HEADS + 1):
            if h < HEADS:
                act.wait_ge(rv_done, h + 1)
                act.activation(ret_y[:, h, :], psum[:, 6 + h % 2, :], ACT.Copy).then_inc(rc_done, 1)
                if h >= 2:
                    act.wait_ge(rm_done, h - 1)
                act.activation(rq[0][h % 2][:, :], psum[:, 6 + h % 2, :], ACT.Square).then_inc(rsq_done, 1)
            if h >= 1:
                g = h - 1
                act.wait_ge(rm_done, g + 1)
                if g >= 2:
                    act.wait_ge(ri_done, g - 1)
                act.activation(rq[1][g % 2][:, :], psum[:, 6 + g % 2, :], ACT.Sqrt, scale=1.0 / RV, bias=col("eps"))\
                   .then_inc(rr_done, 1)

    g_tmp = [at(f"g_tmp{b}", 144 + 2 * b, [P, S]) for b in range(4)]
    gate2 = at("gate2", 160, [P, KT, S])
    m_tmp = [at(f"m_tmp{b}", 152 + 2 * b, [P, S]) for b in range(4)]
    g_mul, g_hi, g_lo, m_add, m_hi, m_lo = (
        sem("mix_" + n) for n in ("gated", "gated_high", "gated_low", "sum", "high", "low"))
    mem = at("mem", 176, [P, KT, MEM])
    mem_landed = sem("mem_landed")
    m_high = at("mem_hi", 96, [P, KT, MEM], FR)
    m_low = at("mem_lo", 104, [P, KT, MEM], FR)
    norm_mem = Norm("norm_mem", mem, "mem", 184, n_tok=MEM, hi=m_high, lo=m_low, bank=7, rstd_kb=140, y_kb=141)
    norm2 = Norm("norm2", res, "ffn", 184, out=at("hn", 144, [P, KT, S]))
    norm_mem.a, norm2.a = norm2.a, norm_mem.a
    hn = norm2.out
    names5 = ("ret_g", "gate_ret", "ret_out", "out")

    def mix_sync(sp):
        sp.wait_ge(rv_done, HEADS)
        sp.dma_start(mem[:, :, :], d["mem"]).then_inc(mem_landed, 16)
        for name in names5:
            dense_sync(sp, name)

    def mix_gpsimd(pool):
        for name in names5:
            dense_pool(pool, name)

    def mix_scalar(act):
        t0, c0 = FIRST_TILE["ret_g"], FIRST_CHUNK["ret_g"]
        norm_mem.act_sum(act, lambda e, kt: e.wait_ge(mem_landed, 16), root=False)

        def high(t):
            act.wait_ge(g_mul, t + 1)
            act.activation(y_hi[:, t, :], g_tmp[t % 4][:, :], ACT.Copy).then_inc(g_hi, 1)
        act.wait_ge(bank_free, t0 + 4)
        for t in range(KT):
            act.wait_ge(tile_done, t0 + t + 1)
            if t >= 4:
                act.wait_ge(g_lo, t - 3)
            act.activation(g_tmp[t % 4][:, :], psum[:, (t0 + t) % 4, :], ACT.Silu).then_inc(bank_free, 1)
            if t % 2 == 1:
                split_hi(act, c0 + 2 + t // 2, t0 + t + 1)
            if t >= 1:
                high(t - 1)
        high(KT - 1)
        dense_act(act, "gate_ret", lambda e, i, j, bank: e.activation(
            gate2[:, bass.ds(4 * i + j, 1), :], psum[:, bank:bank + 1, :], ACT.Sigmoid,
            bias=cols[:, bass.ds(4 * i + j + COLS["bgate"] + KT, 1)]).then_inc(bank_free, 1))
        norm_mem.act_root(act)
        t0, c0 = FIRST_TILE["ret_out"], FIRST_CHUNK["ret_out"]
        for t in range(KT):
            act.wait_ge(m_add, t + 1)
            act.activation(x_hi[:, t, :], mix[:, t, :], ACT.Copy).then_inc(m_hi, 1)
            if t % 2 == 1:
                split_hi(act, c0 + 2 + t // 2, t0 + t + 1)
        residual_act(act, "out", norm2)

    def mix_vector(dve):
        dve.wait_ge(ry_done, HEADS)
        t0 = FIRST_TILE["ret_g"]
        norm_mem.vector_sum(dve, lambda e, kt: None, invert=False)

        def gated_low(t):
            dve.wait_ge(g_hi, t + 1)
            dve.tensor_tensor(y_lo[:, t, :], g_tmp[t % 4][:, :], y_hi[:, t, :].bitcast(F32), ALU.subtract)\
               .then_inc(g_lo, 1)
        for t in range(KT):
            dve.wait_ge(bank_free, t0 + t + 5)
            dve.tensor_tensor(g_tmp[t % 4][:, :], g_tmp[t % 4][:, :], ret_y[:, t, :], ALU.mult).then_inc(g_mul, 1)
            if t >= 1:
                gated_low(t - 1)
        gated_low(KT - 1)
        norm_mem.vector_invert(dve)
        t0 = FIRST_TILE["ret_out"]
        dve.wait_ge(bank_free, t0 + 4)

        def mix_low(t):
            dve.wait_ge(m_hi, t + 1)
            dve.tensor_tensor(x_lo[:, t, :], mix[:, t, :], x_hi[:, t, :].bitcast(F32), ALU.subtract).then_inc(m_lo, 1)
        for t in range(KT):
            dve.wait_ge(tile_done, t0 + t + 1)
            if t >= 4:
                dve.wait_ge(m_add, t - 3)
            dve.tensor_tensor(m_tmp[t % 4][:, :], psum[:, (t0 + t) % 4, :], gate2[:, t, :], ALU.mult)\
               .then_inc(bank_free, 1)
            dve.wait_ge(bank_free, t0 + t + 5)
            dve.tensor_tensor(mix[:, t, :], mix[:, t, :], m_tmp[t % 4][:, :], ALU.add).then_inc(m_add, 1)
            if t >= 1:
                mix_low(t - 1)
        mix_low(KT - 1)
        add_residual(dve, "out", norm2)

    def mix_tensor(pe):
        dense_pe(pe, "ret_g", x_hi, x_lo)
        pe.wait_ge(rr_done, HEADS)
        norm_mem.pe(pe)
        dense_pe(pe, "gate_ret", x_hi, x_lo)
        pe.wait_ge(g_lo, KT)
        dense_pe(pe, "ret_out", y_hi, y_lo)
        pe.wait_ge(m_lo, KT)
        dense_pe(pe, "out", x_hi, x_lo)
        norm2.pe(pe)

    with nc.Block() as block:
        @block.sync
        def _(sp):
            retention_first_decays(sp)
            gate_sync(sp)
            retention_sync(sp)
            mix_sync(sp)

        @block.gpsimd
        def _(pool):
            gate_gpsimd(pool)
            mix_gpsimd(pool)

        @block.scalar
        def _(act):
            gate_scalar(act)
            retention_scalar(act)
            mix_scalar(act)

        @block.vector
        def _(dve):
            gate_vector(dve)
            retention_vector(dve)
            mix_vector(dve)

        @block.tensor
        def _(pe):
            gate_tensor(pe)
            retention_tensor(pe)
            mix_tensor(pe)


    LISTS = NE * TB + 2
    hn_rows = nc.dram_tensor("hn_rows", [S, D], F32).ap()
    slots = nc.dram_tensor("slots", [P * LISTS, 1], I32).ap()
    expert_rows = nc.dram_tensor("expert_rows", [2 * S + P, D], F32).ap()
    list_rows = at("list_rows", 139, [P, LISTS], I32)
    list_tokens = at("list_tokens", 139.28125, [P, LISTS], I32)
    row_col = [at(f"row_col{b}", 139.5625 + b / 32, [P, 1], I32) for b in range(2)]
    token_col = [at(f"token_col{b}", 139.625 + b / 32, [P, 1], I32) for b in range(2)]
    rounds_i = at("rounds_i", 139.6875, [P, 1], I32)
    gates2 = at("expert_gates", 139.75, [P, 2, TB])
    hn_tok = [at(f"hn_tok{b}", 160 + 4 * b, [P, D]) for b in range(2)]
    w_router = at("w_router", 168, [P, KT, NR])
    _small = [170.0]

    def small(name, shape, dt=F32):
        t = at("r_" + name, _small[0], shape, dt)
        _small[0] += (int(np.prod(shape[1:])) * 4 + 31) // 32 * 32 / 1024
        return t
    b_router, ranks, dest = small("bias", [P, NR]), small("ranks", [P, 36]), small("dest", [P, 2, TB], I32)
    lg, gmax, gdif, gexp, gsum, pg = (small(n, [P, TB] + s) for n, s in (
        ("logits", [NR]), ("gmax", []), ("gdif", [NG]), ("gexp", [NG]), ("gsum", []), ("pgroup", [])))
    geq, gord, gtop, goh, gpen = (small(n, [P, TB] + s) for n, s in (
        ("geq", [NG]), ("gord", [NG]), ("gtop", []), ("gone", [NG]), ("gpen", [NG])))
    ml, eeq, eord, etop = (small(n, [P, TB] + s) for n, s in (("masked", [NE]), ("eeq", [NE]), ("eord", [NE]), ("etop", [])))
    best = small("best", [P, 2, TB])
    eoh = small("eone", [P, 2, TB, NE])
    both = small("both", [P, TB, NE])
    edif, eexp, eden, einv = (small(n, [P, TB]) for n in ("edif", "eexp", "eden", "einv"))
    pick = small("pick", [P, 2, TB, NE])
    rank, eid, window, w1, slot_f = (small(n, [P, 2, TB]) for n in ("rank", "eid", "window", "w1", "slot_f"))
    slot_i = small("slot_i", [P, 2, TB], I32)
    cmax, rounds = small("cmax", [P, 1]), small("rounds", [P, 1])
    empty = small("empty", [P, LISTS], I32)
    r_in, lg_done, tr_done, tr_read, hn_stored, gdif_done, gexp_done, edif_done, eexp_done, both_done, rank_done, \
        slot_done, slots_zero, slots_full, list_landed = (sem("route_" + n) for n in (
            "in", "logits", "transposed", "rows_read", "rows_stored", "gdif", "gexp", "edif", "eexp", "both", "ranks",
            "slots", "zero", "full", "landed"))

    hn_half = [sem(f"route_rows_stored{b}") for b in range(2)]

    ring = [at(f"moe_w{s}", (48 + 8 * s) if s < 8 else (144 + 8 * (s - 8)), [P, CHUNK_COLS]) for s in range(MOE_RING)]
    xg = [at(f"moe_x{b}", 176 + 4 * b, [P, D]) for b in range(2)]
    moe_landed = [sem(f"moe_landed{s}") for s in range(MOE_RING // 2)]
    xg_landed = [sem(f"moe_x_landed{b}") for b in range(2)]
    col_done, wait_seen, tokens_ready = sem("moe_column"), sem("moe_wait_seen"), sem("route_tokens")

    def gather(pool, n, b):
        pool.tensor_copy(token_col[b][:, :], list_tokens[:, bass.ds(2 * n + b, 1)]).then_inc(col_done, 1)
        pool.wait_ge(col_done, 4 * n + b + 1)
        pool.sem_inc(wait_seen, 1)
        pool.indirect_dma_start(
            out=xg[b][:, :], out_offset=None, in_=hn_rows,
            in_offset=bass.IndirectOffsetOnAxis(ap=token_col[b][:, :].bitcast(U32), axis=0))\
            .then_inc(xg_landed[b], 16)

    def wide(ap, shape, axis):
        return ap.unsqueeze(axis).to_broadcast(shape)

    kc_out = at("k_mem", 80, [P, KT, MEM])
    vc_out = at("v_mem", 88, [P, MEM // P, D])
    kc_rows = nc.dram_tensor("k_mem_rows", [P, KT, MEM], F32).ap()
    vc_rows = nc.dram_tensor("v_mem_rows", [P, MEM // P, D], F32).ap()
    kv_moved = sem("kv_moved")

    with nc.Block() as block:
        @block.sync
        def _(sp):
            for t, n in ((w_router, "w_router"), (b_router, "b_router"), (ranks, "ranks"), (dest, "dest"), (empty, "empty")):
                sp.dma_start(t[tuple([slice(None)] * len(t.shape))], d[n]).then_inc(r_in, 16)
            sp.wait_ge(r_in, 80)
            sp.dma_start(slots.rearrange("(p l) o -> p (l o)", p=P), empty[:, :]).then_inc(slots_zero, 16)
            dense_sync(sp, "k_mem")
            sp.wait_ge(slots_full, 16 * 2 * TB)
            sp.dma_start(list_rows[:, :], slots.rearrange("(p l) o -> p (l o)", p=P)).then_inc(list_landed, 16)
            for s in range(MOE_AHEAD):
                sp.dma_start(ring[s][:, :], d["w_moe_ahead"][PAIRS - 1, s]).then_inc(moe_landed[s // 2], 16)
            for b in range(RING):
                load_chunk(sp, FIRST_CHUNK["v_mem"] + 4 + b)
            sp.wait_ge(bank_free, FIRST_TILE["v_mem"] + KT + 4)
            sp.dma_start(kc_rows, kc_out[:, :, :]).then_inc(kv_moved, 16)
            sp.dma_start(vc_rows, vc_out[:, :, :]).then_inc(kv_moved, 16)

        @block.tensor
        def _(pe):
            def logits():
                for q in range(TB):
                    for kt in range(KT):
                        if q == 0:
                            norm2.wait_scaled(pe, kt + 1)
                        mm = pe.matmul(psum[:, 6, q * NR:(q + 1) * NR], hn[:, kt, q * P:(q + 1) * P], w_router[:, kt, :],
                                       start=(q == 0 and kt == 0), stop=(kt == KT - 1), skip_group_check=True)
                mm.then_inc(lg_done, 1)

            def rows(q):
                for half in range(2):
                    if q >= 1:
                        pe.wait_ge(tr_read, 2 * q - 1 + half)
                    for k in range(4):
                        mm = pe.transpose(psum[:, 4 + half, k * P:(k + 1) * P],
                                          hn[:, 4 * half + k, q * P:(q + 1) * P], ident[:, :])
                    mm.then_inc(tr_done, 1)

            def ranks_of_tokens():
                pe.wait_ge(both_done, 1)
                for q in range(TB):
                    for q2 in range(q + 1):
                        mm = pe.matmul(psum[:, 6, q * NE:(q + 1) * NE], before[:, :] if q2 == q else ones[:, :],
                                       both[:, q2, :], start=(q == 0), stop=(q2 == q), skip_group_check=True)
                for q in range(TB):
                    mm = pe.matmul(psum[:, 7, 0:NE], ones[:, :], both[:, q, :], start=(q == 0), stop=(q == TB - 1))
                mm.then_inc(rank_done, 1)
            pe.wait_ge(r_in, 80)
            logits()
            rows(0)
            dense_pe(pe, "k_mem", m_high, m_low, n_tok=MEM, norm=norm_mem,
                     between=lambda: [rows(1), ranks_of_tokens(), rows(2)])
            rows(3)
            dense_pe(pe, "v_mem", m_high, m_low, token_major=True)

        @block.scalar
        def _(act):
            def rows(q):
                for half in range(2):
                    act.wait_ge(tr_done, 2 * q + half + 1)
                    if q >= 2:
                        act.wait_ge(hn_half[q % 2], 16)
                    act.activation(hn_tok[q % 2][:, half * 512:(half + 1) * 512], psum[:, 4 + half, :], ACT.Copy)\
                       .then_inc(tr_read, 1)
                act.wait_ge(tr_read, 2 * (q + 1))
                act.dma_start(hn_rows[q * P:(q + 1) * P, :], hn_tok[q % 2][:, :])\
                   .then_inc(hn_half[q] if q < 2 else hn_stored, 16)
            norm_mem.act_split(act)
            rows(0)
            dense_act(act, "k_mem", lambda e, i, j, bank: e.activation(
                kc_out[:, 4 * i + j, :], psum[:, bank, 0:MEM], ACT.Copy).then_inc(bank_free, 1), between=lambda: [rows(1), rows(2)])
            act.wait_ge(gdif_done, 1)
            act.activation(gexp[:, :, :], gdif[:, :, :], ACT.Exp).then_inc(gexp_done, 1)
            act.wait_ge(edif_done, 1)
            act.activation(eexp[:, :], edif[:, :], ACT.Exp).then_inc(eexp_done, 1)
            rows(3)
            dense_act(act, "v_mem", lambda e, i, j, bank: e.activation(
                vc_out[:, j % 2, bass.ds(512 * i + 256 * (j // 2), 256)], psum[:, bank, 0:256], ACT.Copy)
                .then_inc(bank_free, 1))
            act.wait_ge(hn_stored, 32)

        @block.vector
        def _(dve):
            def first_best(values, top, eq, order, otop, one, nth, n):
                link(dve, dve.tensor_reduce(top, values, AX.X, ALU.max))
                link(dve, dve.tensor_tensor(eq[:, :, :], values, wide(top, [P, TB, n], 2), ALU.is_equal))
                link(dve, dve.tensor_tensor(order[:, :, :], eq[:, :, :], wide(nth, [P, TB, n], 1), ALU.mult))
                link(dve, dve.tensor_reduce(otop[:, :], order[:, :, :], AX.X, ALU.max))
                link(dve, dve.tensor_tensor(one, order[:, :, :], wide(otop[:, :], [P, TB, n], 2), ALU.is_equal))

            norm2.vector_split(dve)
            norm_mem.vector_split(dve)
            dve.wait_ge(lg_done, 1)
            dve.wait_ge(r_in, 80)
            link(dve, dve.tensor_tensor(lg[:, :, :], psum[:, 6, 0:TB * NR].rearrange("p (q n) -> p q n", n=NR), wide(b_router[:, :], [P, TB, NR], 1), ALU.add))
            gl, el = lg[:, :, 0:NG], lg[:, :, NG:NR].rearrange("p q (g e) -> p q g e", g=NG)
            first_best(gl, gmax[:, :], geq, gord, gtop, goh[:, :, :], ranks[:, 0:NG], NG)
            dve.tensor_tensor(gdif[:, :, :], gl, wide(gmax[:, :], [P, TB, NG], 2), ALU.subtract).then_inc(gdif_done, 1)
            link(dve, dve.tensor_scalar(gpen[:, :, :], goh[:, :, :], BIG, -BIG, ALU.mult, ALU.add))
            ml4 = ml[:, :, :].rearrange("p q (g e) -> p q g e", g=NG)
            for q in range(TB):
                dve.tensor_tensor(ml4[:, q], el[:, q], wide(goh[:, q, :], [P, NG, 4], 2), ALU.mult)
            link(dve, dve.engine_nop())
            for q in range(TB):
                ins = dve.tensor_tensor(ml4[:, q], ml4[:, q], wide(gpen[:, q, :], [P, NG, 4], 2), ALU.add)
            link(dve, ins)
            first_best(ml[:, :, :], best[:, 0, :], eeq, eord, etop, eoh[:, 0], ranks[:, NG:NG + NE], NE)
            link(dve, dve.scalar_tensor_tensor(out=ml[:, :, :], in0=eoh[:, 0], scalar=-2 * BIG, in1=ml[:, :, :],
                                               op0=ALU.mult, op1=ALU.add))
            first_best(ml[:, :, :], best[:, 1, :], eeq, eord, etop, eoh[:, 1], ranks[:, NG:NG + NE], NE)
            dve.tensor_tensor(edif[:, :], best[:, 1, :], best[:, 0, :], ALU.subtract).then_inc(edif_done, 1)
            dve.tensor_tensor(both[:, :, :], eoh[:, 0], eoh[:, 1], ALU.add).then_inc(both_done, 1)
            for k in range(2):
                ins = dve.tensor_tensor(pick[:, k], eoh[:, k], wide(ranks[:, NG + NE:NG + 2 * NE], [P, TB, NE], 1), ALU.mult)
            link(dve, ins)
            for k in range(2):
                ins = dve.tensor_reduce(eid[:, k, :], pick[:, k], AX.X, ALU.add)
            link(dve, ins)
            dve.wait_ge(rank_done, 1)
            for k in range(2):
                ins = dve.tensor_tensor(pick[:, k], psum[:, 6, 0:TB * NE].rearrange("p (q e) -> p q e", e=NE),
                                        eoh[:, k], ALU.mult)
            link(dve, ins)
            for k in range(2):
                ins = dve.tensor_reduce(rank[:, k, :], pick[:, k], AX.X, ALU.add)
            link(dve, ins)
            link(dve, dve.tensor_scalar(w1[:, :, :], rank[:, :, :], float(P), None, ALU.is_ge))
            for n in (2, 3):
                src, dst = (w1, window) if n == 2 else (window, w1)
                link(dve, dve.scalar_tensor_tensor(out=dst[:, :, :], in0=rank[:, :, :], scalar=float(n * P),
                                                   in1=src[:, :, :], op0=ALU.is_ge, op1=ALU.add))
            link(dve, dve.tensor_scalar(slot_f[:, :, :], rank[:, :, :], float(LISTS), None, ALU.mult))
            link(dve, dve.scalar_tensor_tensor(out=slot_f[:, :, :], in0=w1[:, :, :], scalar=float(NE - P * LISTS),
                                               in1=slot_f[:, :, :], op0=ALU.mult, op1=ALU.add))
            link(dve, dve.tensor_tensor(slot_f[:, :, :], slot_f[:, :, :], eid[:, :, :], ALU.add))
            dve.tensor_copy(slot_i[:, :, :], slot_f[:, :, :]).then_inc(slot_done, 1)
            link(dve, dve.tensor_reduce(cmax[:, :], psum[:, 7, 0:NE], AX.X, ALU.max))
            link(dve, dve.tensor_scalar(rounds[:, :], cmax[:, :], float(P + 1), 1.0, ALU.is_ge, ALU.add))
            for n in (2, 3):
                link(dve, dve.scalar_tensor_tensor(out=rounds[:, :], in0=cmax[:, :], scalar=float(n * P + 1),
                                                   in1=rounds[:, :], op0=ALU.is_ge, op1=ALU.add))
            link(dve, dve.tensor_copy(rounds_i[:, :], rounds[:, :]))
            dve.wait_ge(gexp_done, 1)
            link(dve, dve.tensor_reduce(gsum[:, :], gexp[:, :, :], AX.X, ALU.add))
            link(dve, dve.reciprocal(pg[:, :], gsum[:, :]))
            dve.wait_ge(eexp_done, 1)
            link(dve, dve.tensor_scalar(eden[:, :], eexp[:, :], 1.0, None, ALU.add))
            link(dve, dve.reciprocal(einv[:, :], eden[:, :]))
            link(dve, dve.tensor_tensor(gates2[:, 0, :], einv[:, :], pg[:, :], ALU.mult))
            link(dve, dve.tensor_tensor(gates2[:, 1, :], gates2[:, 0, :], eexp[:, :], ALU.mult))
            dve.wait_ge(list_landed, 16)
            dve.tensor_scalar(list_tokens[:, :], list_rows[:, :], S - 1, None, ALU.bitwise_and)\
               .then_inc(tokens_ready, 1)

        @block.gpsimd
        def _(pool):
            def fill_slots():
                pool.wait_ge(slots_zero, 16)
                pool.wait_ge(slot_done, 1)
                for k in range(2):
                    for q in range(TB):
                        pool.indirect_dma_start(
                            out=slots, out_offset=bass.IndirectOffsetOnAxis(ap=slot_i[:, k, q:q + 1].bitcast(U32), axis=0),
                            in_=dest[:, k, q:q + 1], in_offset=None).then_inc(slots_full, 16)
            dense_pool(pool, "k_mem", between=fill_slots)

            def first_rows():
                pool.wait_ge(tokens_ready, 1)
                for b in range(2):
                    pool.wait_ge(hn_half[b], 16)
                pool.wait_ge(hn_stored, 32)
                for b in range(2):
                    gather(pool, 0, b)
            first_rows()
            for b in range(RING):
                split_lo(pool, FIRST_CHUNK["v_mem"] + 2 + b)

    xt = [at(f"moe_xt{b}", 184 + 4 * b, [P, KT, P]) for b in range(2)]
    hid = [at(f"moe_h{b}", 140 + 2 * b, [P, FF]) for b in range(2)]
    hidt = [at(f"moe_ht{b}", 192 + 2 * b, [P, FF // P, P]) for b in range(2)]
    yo = [at(f"moe_y{b}", 196 + 4 * b, [P, D]) for b in range(2)]
    y_stored = [sem(f"moe_y_stored{b}") for b in range(2)]
    tr = [sem(f"moe_x_transposed{b}") for b in range(2)]
    tr_ev = [sem(f"moe_x_read{b}") for b in range(2)]
    moe_used, y_free, silu_done, h_ready, ht_done, ht_read, yy_done, yy_read, credits = (
        sem("moe_" + n) for n in ("used", "y_free", "silu", "hidden", "hidden_t", "hidden_t_read", "down",
                                  "down_read", "credits"))

    def rounds_of(eng):
        return eng.value_load(rounds_i[0:1, 0:1], min_val=1, max_val=TB)

    def expert_loop(eng, body):
        n_rounds = rounds_of(eng)
        with eng.Fori(0, n_rounds) as r:
            with eng.Fori(0, PAIRS) as i:
                body(r * PAIRS + i, i, r)
        return n_rounds

    with nc.Block() as block:
        @block.sync
        def _(sp):
            sp.wait_ge(kv_moved, 32)
            sp.wait_ge(credits, 1)

            def body(n, i, r):
                for s in range(MOE_AHEAD, MOE_RING):
                    sp.wait_ge(moe_used, MOE_RING * n + s + 1)
                    sp.dma_start(ring[s][:, :], d["w_moe"][bass.ds(i, 1), s - MOE_AHEAD].rearrange("a p n -> p (a n)"))\
                      .then_inc(moe_landed[s // 2], 16)
                for s in range(MOE_AHEAD):
                    sp.wait_ge(moe_used, MOE_RING * n + MOE_RING + s + 1)
                    sp.dma_start(ring[s][:, :], d["w_moe_ahead"][bass.ds(i, 1), s].rearrange("a p n -> p (a n)"))\
                      .then_inc(moe_landed[s // 2], 16)
            n_rounds = expert_loop(sp, body)
            for s in range(MOE_AHEAD // 2):
                sp.wait_ge(moe_landed[s], n_rounds * (32 * PAIRS) + 32)
                sp.sem_inc(wait_seen, 1)

        @block.gpsimd
        def _(pool):
            def body(n, i, r):
                for b in range(2):
                    pool.wait_ge(tr[1], 2 * n + b + 1)
                    pool.sem_inc(wait_seen, 1)
                    pool.tensor_copy(row_col[b][:, :], list_rows[:, bass.ds(2 * n + b, 1)]).then_inc(col_done, 1)
                for b in range(2):
                    gather(pool, n + 1, b)
                for b in range(2):
                    pool.wait_ge(yy_read, 4 * n + 2 * b + 4)
                    pool.sem_inc(wait_seen, 1)
                    pool.indirect_dma_start(
                        out=expert_rows, in_=yo[b][:, :], in_offset=None,
                        out_offset=bass.IndirectOffsetOnAxis(ap=row_col[b][:, :].bitcast(U32), axis=0))\
                        .then_inc(y_stored[b], 16)
                    pool.wait_ge(y_stored[b], 16 * n + 16)
                    pool.sem_inc(y_free, 1)
            n_rounds = expert_loop(pool, body)
            for b in range(2):
                pool.wait_ge(xg_landed[b], n_rounds * (16 * PAIRS) + 16)
                pool.sem_inc(wait_seen, 1)

        @block.tensor
        def _(pe):
            pe.sem_inc(moe_used, MOE_RING)
            pe.sem_inc(ht_read, 1)
            pe.sem_inc(yy_read, 2)
            pe.sem_inc(y_free, 2)
            pe.sem_inc(credits, 1)

            def rows_t(n, b):
                pe.wait_ge(xg_landed[b], 16 * n + 16)
                for half in range(2):
                    if b == 1:
                        pe.wait_ge(tr_ev[half], 2 * n + 1)
                    for k in range(4):
                        mm = pe.transpose(psum[:, 6 + half, k * P:(k + 1) * P],
                                          xg[b][:, (4 * half + k) * P:(4 * half + k + 1) * P], ident[:, :])
                    mm.then_inc(tr[half], 1)

            def project(n, b, m):
                for kt in range(KT):
                    s = 4 * b + 2 * m + kt // 4
                    if kt == 0:
                        pe.wait_ge(moe_landed[s // 2], 32 * n + 32)
                    mm = pe.matmul(psum[:, 2 * b + m, :], xt[b][:, kt, :],
                                   ring[s][:, (kt % 4) * FF:(kt % 4 + 1) * FF], start=(kt == 0), stop=(kt == KT - 1))
                    if kt == 3:
                        mm.then_inc(moe_used, 1)
                mm.then_inc(moe_used, 1)

            def hidden_t(n, b):
                pe.wait_ge(h_ready, 2 * n + b + 1)
                pe.wait_ge(ht_read, 2 * n + b + 1)
                for k in range(4):
                    mm = pe.transpose(psum[:, 6, k * P:(k + 1) * P], hid[b][:, k * P:(k + 1) * P], ident[:, :])
                mm.then_inc(ht_done, 1)

            def down(n, b, half):
                if half == 0:
                    pe.wait_ge(ht_read, 2 * n + b + 2)
                    pe.wait_ge(moe_landed[4 + b], 32 * n + 32)
                pe.wait_ge(yy_read, 4 * n + 2 * b + half + 1)
                for k in range(4):
                    mm = pe.matmul(psum[:, 4 + half, :], hidt[b][:, k, :],
                                   ring[8 + 2 * b + k // 2][:, (k % 2) * D + half * 512:(k % 2) * D + half * 512 + 512],
                                   start=(k == 0), stop=(k == 3))
                if half == 0:
                    mm.then_inc(yy_done, 1)
                else:
                    mm.then_inc(moe_used, 2)

            def body(n, i, r):
                for half in range(2):
                    pe.wait_ge(tr_ev[half], 2 * n + 1)
                project(n, 0, 0)
                project(n, 0, 1)
                for half in range(2):
                    pe.wait_ge(tr_ev[half], 2 * n + 2)
                project(n, 1, 0)
                hidden_t(n, 0)
                project(n, 1, 1)
                down(n, 0, 0)
                hidden_t(n, 1)
                down(n, 0, 1)
                pe.wait_ge(ht_read, 2 * n + 3)
                rows_t(n + 1, 0)
                down(n, 1, 0)
                rows_t(n + 1, 1)
                down(n, 1, 1)
            for b in range(2):
                rows_t(0, b)
            expert_loop(pe, body)

        @block.scalar
        def _(act):
            def rows_t(n, b):
                act.wait_ge(tr[0], 2 * n + b + 1)
                act.activation(xt[b][:, 0:4, :].rearrange("p k n -> p (k n)"), psum[:, 6, :], ACT.Copy)\
                   .then_inc(tr_ev[0], 1)

            def body(n, i, r):
                for b in range(2):
                    act.wait_ge(moe_used, MOE_RING * (n + 1) + 4 * b + 4)
                    act.activation(hid[b][:, :], psum[:, 2 * b, :], ACT.Silu).then_inc(silu_done, 1)
                for b in range(2):
                    for half in range(2):
                        if b == 1:
                            rows_t(n + 1, half)
                        if half == 0:
                            act.wait_ge(y_free, 2 * n + b + 1)
                            act.wait_ge(yy_done, 2 * n + b + 1)
                        else:
                            act.wait_ge(moe_used, MOE_RING * (n + 1) + 2 * b + 10)
                        act.activation(yo[b][:, half * 512:half * 512 + 512], psum[:, 4 + half, :], ACT.Copy)\
                           .then_inc(yy_read, 1)
            for b in range(2):
                rows_t(0, b)
            expert_loop(act, body)

        @block.vector
        def _(dve):
            def rows_t(n, b):
                dve.wait_ge(tr[1], 2 * n + b + 1)
                dve.tensor_copy(xt[b][:, 4:8, :].rearrange("p k n -> p (k n)"), psum[:, 7, :]).then_inc(tr_ev[1], 1)

            def body(n, i, r):
                for b in range(2):
                    dve.wait_ge(silu_done, 2 * n + b + 1)
                    dve.tensor_tensor(hid[b][:, :], hid[b][:, :], psum[:, 2 * b + 1, :], ALU.mult).then_inc(h_ready, 1)
                    dve.wait_ge(ht_done, 2 * n + b + 1)
                    dve.tensor_copy(hidt[b][:, :, :].rearrange("p k n -> p (k n)"), psum[:, 6, :]).then_inc(ht_read, 1)
                for b in range(2):
                    rows_t(n + 1, b)
            for b in range(2):
                rows_t(0, b)
            expert_loop(dve, body)

    yrow = [[at(f"yrow{k}{q}", 144 + 4 * (4 * k + q), [P, D]) for q in range(TB)] for k in range(2)]
    ysum = at("ysum", 176, [P, TB, D])
    yrows_landed = [sem(f"yrows_landed{q}") for q in range(TB)]
    ys1, ys2, yt_done, yt_added = (sem("moe_sum_" + n) for n in ("first", "both", "transposed", "added"))
    hg = [at(f"h_gained{b}", 192 + 4 * b, [P, KT, P]) for b in range(2)]
    esq = [at(f"end_sq{b}", 48 + 4 * b, [P, KT, P]) for b in range(2)]
    r12_inv, esum = (at(f"end_{n}", 56 + 2 * i, [P, S]) for i, n in enumerate(("rms12", "mean")))
    erms = at("end_rms1", 204, [P, S])
    r1 = at("end_rstd1", 140, [P, S])
    r12 = at("end_rstd12", 142, [P, S])
    g12 = at("end_gain12", 206, [P, KT])
    hg_done, esq_done, esum_sq, esum_done, eroot = (
        sem("end_" + n) for n in ("gained", "squared", "squares_summed", "mean", "rooted"))
    norm3 = Norm("norm3", res, g12, 154, hi=x_hi, lo=x_lo, y_kb=164, sums=False)
    norm3.rstd = r12
    with nc.Block() as block:
        @block.sync
        def _(sp):
            for q in range(TB):
                for k in range(2):
                    sp.dma_start(yrow[k][q][:, :], expert_rows[k * S + q * P:k * S + (q + 1) * P, :])\
                      .then_inc(yrows_landed[q], 16)
            for b in range(RING):
                load_chunk(sp, FIRST_CHUNK["v_mem"] + 6 + b)

        @block.vector
        def _(dve):
            def add(n):
                q, half = n // 2, n % 2
                dve.wait_ge(yt_done, n + 1)
                r4 = res[:, 4 * half:4 * half + 4, q * P:(q + 1) * P]
                dve.tensor_tensor(r4, r4, psum[:, 1 + n % 4, :].rearrange("p (k n) -> p k n", n=P), ALU.add)\
                   .then_inc(yt_added, 1)
            g1, g2 = (cols[:, COLS[n]:COLS[n] + KT] for n in ("end1", "mix2"))
            dve.tensor_tensor(g12[:, :], g1, g2, ALU.mult)
            for q in range(TB):
                dve.wait_ge(yrows_landed[q], 32)
                dve.tensor_scalar(ysum[:, q, :], yrow[0][q][:, :], gates2[:, 0, q:q + 1], None, ALU.mult).then_inc(ys1, 1)
                dve.wait_ge(ys1, q + 1)
                dve.scalar_tensor_tensor(out=ysum[:, q, :], in0=yrow[1][q][:, :], scalar=gates2[:, 1, q:q + 1],
                                         in1=ysum[:, q, :], op0=ALU.mult, op1=ALU.add).then_inc(ys2, 1)
                if q >= 1:
                    add(2 * q - 2)
                    add(2 * q - 1)
            add(6)
            add(7)
            dve.wait_ge(esum_sq, 2 * TB)
            link(dve, dve.tensor_scalar(esum[:, :], psum[:, 5, :], EPS / D, EPS * EPS, ALU.mult, ALU.add))
            dve.scalar_tensor_tensor(out=esum[:, :], in0=psum[:, 6, :], scalar=1.0 / D, in1=esum[:, :],
                                     op0=ALU.mult, op1=ALU.add).then_inc(esum_done, 1)
            dve.wait_ge(eroot, 1)
            link(dve, dve.reciprocal(r12[:, :], r12_inv[:, :]))

        @block.gpsimd
        def _(pool):
            for b in range(RING):
                split_lo(pool, FIRST_CHUNK["v_mem"] + 4 + b)
            for q in range(TB):
                pool.wait_ge(yt_added, 2 * q + 2)
                if q >= 2:
                    pool.wait_ge(esq_done, 2 * (q - 1))
                pool.tensor_tensor(hg[q % 2][:, :, :], res[:, :, q * P:(q + 1) * P],
                                   wide(cols[:, COLS["end1"]:COLS["end1"] + KT], [P, KT, P], 2), ALU.mult)\
                    .then_inc(hg_done, 1)

        @block.scalar
        def _(act):
            for q in range(TB):
                act.wait_ge(yt_added, 2 * q + 2)
                if q >= 1:
                    act.wait_ge(esum_sq, 2 * q - 1)
                act.activation(esq[0][:, :, :], res[:, :, q * P:(q + 1) * P], ACT.Square).then_inc(esq_done, 1)
                act.wait_ge(hg_done, q + 1)
                if q >= 1:
                    act.wait_ge(esum_sq, 2 * q)
                act.activation(esq[1][:, :, :], hg[q % 2][:, :, :], ACT.Square).then_inc(esq_done, 1)
            norm3.warm_up(act)
            act.wait_ge(esum_done, 1)
            act.activation(r12_inv[:, :], esum[:, :], ACT.Sqrt).then_inc(eroot, 1)
            act.activation(erms[:, :], psum[:, 5, :], ACT.Sqrt, scale=1.0 / D, bias=col("eps")).then_inc(eroot, 1)

        @block.tensor
        def _(pe):
            def sums(q):
                for m in range(2):
                    pe.wait_ge(esq_done, 2 * q + m + 1)
                    for kt in range(KT):
                        mm = pe.matmul(psum[:, 5 + m, q * P:(q + 1) * P], ones[:, :], esq[m][:, kt, :],
                                       start=(kt == 0 and q == 0), stop=(kt == KT - 1), skip_group_check=True)
                    mm.then_inc(esum_sq, 1)
            for n in range(2 * TB):
                q, half = n // 2, n % 2
                pe.wait_ge(ys2, q + 1)
                if n >= 4:
                    pe.wait_ge(yt_added, n - 3)
                for k in range(4):
                    mm = pe.transpose(psum[:, 1 + n % 4, k * P:(k + 1) * P],
                                      ysum[:, q, (4 * half + k) * P:(4 * half + k + 1) * P], ident[:, :])
                mm.then_inc(yt_done, 1)
                if half and q >= 1:
                    sums(q - 1)
            sums(TB - 1)


    q_a = at("q_sparse", 144, [P, HEADS, S])
    k_a = at("k_sparse", 160, [P, HEADS, S])
    k_r = at("k_rope", 176, [P, S])
    c_kv = at("c_kv", 90, [P, S])
    c_tok = at("c_tok", 94, [P, TB, P])
    bias = at("kept_bias", 178, [P, SPAN])
    q_b = at("q_b", 183, [P, 4, S])
    k_b = at("k_b", 191, [P, 4, S])
    v_b = at("v_b", 199, [P, TB, S])
    w_eff = at("w_eff", 207, [P, TB, HEADS])
    top8 = at("top8", 207.25, [P, 8])
    q_i = at("q_idx", 80, [P, 4, S])
    k_i = at("k_idx", 88, [P, 1, S])
    w_uk = at("w_uk", 92, [P, HEADS, HD])
    relu = [at(f"relu{b}", 140 + 2 * b, [P, S]) for b in range(2)]
    kv_sq, kv_rms, kv_rstd = (at(f"kv_{n}", 183 + 2 * i, [P, S]) for i, n in enumerate(("sq", "rms", "rstd")))
    rot2 = Rotary("rot2", (96, 104), [("q_idx", 2, 8), ("k_idx", 1, 4), ("q_rope", 2, 4), ("k_rope", 1, 0), ("q_b", 2, 8),
                                      ("k_b", 2, 8)])
    proj_in, kv_squared, kv_summed, kv_rooted, kv_inverted, kv_normed, ct_done, ct_read, ql_done, \
        ql_read, li_done, li_relu, li_added, li_masked, x1_done = (sem("proj_" + n) for n in (
            "in", "kv_squared", "kv_summed", "kv_rooted", "kv_inverted", "kv_normed", "latents_t",
            "latents_t_read", "q_lat", "q_lat_read", "index", "index_relu", "index_added", "index_masked", "residual"))
    INDEX = [(qt, h, SEG[P * (qt + 1)], P * (qt + 1)) for qt in range(1, TB) for h in range(HEADS)]
    names = ("q_idx", "k_idx", "ckv_wi", "q_nope", "q_rope", "k_rope", "q_b", "k_b", "v_b")

    def project_sync(sp):
        sp.dma_start(w_uk[:, :, :], d["w_uk"]).then_inc(proj_in, 16)
        o = SEG[P]
        sp.dma_start(bias[:, o:o + P], d["causal"][:, o:o + P]).then_inc(proj_in, 16)
        for name in names:
            to = {"q_idx": q_i, "k_idx": k_i, "q_b": q_b, "k_b": k_b}.get(name)
            if name == "q_rope":
                dense_sync(sp, name, after=lambda b: rot2.move_narrow(sp, name, q_a, b))
            else:
                dense_sync(sp, name, after=to and (lambda b: rot2.move(sp, name, to, b, heads=2 if name == "k_idx" else 4)))

    def project_gpsimd(pool):
        dense_pool(pool, "q_idx", after=lambda e, i, b: rot2.pool(e, "q_idx", b))
        dense_pool(pool, "k_idx", after=lambda e, i, b: rot2.pool(e, "k_idx", b))
        dense_pool(pool, "ckv_wi")
        pool.wait_ge(lo_ready, FIRST_CHUNK["ckv_wi"] + 3)
        n = 2
        for t in (q_a, k_a):
            for rows, odd in ((slice(96, 128), 0), (slice(32, 64), 1)):
                heads = t[rows, :, :].rearrange("p (k c) n -> p k c n", c=2)[:, :, odd]
                pool.memset(heads, 0.0).then_inc(fills, 1)
                n += 1
                pool.wait_ge(fills, n)
        for qt in range(1, TB):
            o = SEG[P * (qt + 1)] + P * qt
            pool.wait_ge(li_added, HEADS * qt)
            pool.affine_select(out=bias[:, o:o + P], in_=bias[:, o:o + P], compare_op=ALU.is_ge, fill=-BIG,
                               base=0, pattern=[[-1, P]], channel_multiplier=1).then_inc(li_masked, 1)
        dense_pool(pool, "q_nope")

        dense_pool(pool, "q_rope", after=lambda e, i, b: rot2.pool(e, "q_rope", b, narrow=True))
        dense_pool(pool, "k_rope", after=lambda e, i, b: rot2.pool(e, "k_rope", b, narrow=True, narrow_out=k_r[:, :]))
        dense_pool(pool, "q_b", after=lambda e, i, b: rot2.pool(e, "q_b", b))
        dense_pool(pool, "k_b", after=lambda e, i, b: rot2.pool(e, "k_b", b))
        dense_pool(pool, "v_b")

    def project_scalar(act):
        norm3.act_split(act)
        dense_act(act, "q_idx")
        dense_act(act, "k_idx")
        t0 = FIRST_TILE["ckv_wi"]
        act.wait_ge(tile_done, t0 + 1)
        act.activation(c_kv[:, :], psum[:, t0 % 4, :], ACT.Copy)
        act.activation(kv_sq[:, :], psum[:, t0 % 4, :], ACT.Square).then_inc(bank_free, 1)
        act.wait_ge(tile_done, t0 + 2)
        act.activation(w_eff[:, :, :].rearrange("p q h -> p (q h)"), psum[:, (t0 + 1) % 4, 0:TB * HEADS], ACT.Copy,
                       scale=HEADS ** -0.5 * HD ** -0.5).then_inc(bank_free, 1)
        split_hi(act, FIRST_CHUNK["ckv_wi"] + 2, t0 + 2)
        act.wait_ge(kv_summed, 1)
        act.activation(kv_rms[:, :], psum[:, 4, :], ACT.Sqrt, scale=1.0 / P, bias=col("eps")).then_inc(kv_rooted, 1)
        for u in range(len(INDEX)):
            n = INDEX[u][3]
            act.wait_ge(li_done, u + 1)
            if u >= 2:
                act.wait_ge(li_added, u - 1)
            act.activation(relu[u % 2][:, 0:n], psum[:, 4 + u % 4, 0:n], ACT.Relu).then_inc(li_relu, 1)
        def q_nope(e, i, j, bank):
            e.activation(q_a[0:HD, 2 * j, :], psum[0:HD, bank, :], ACT.Copy)
            e.activation(q_a[HD:P, 2 * j + 1, :], psum[HD:P, bank, :], ACT.Copy).then_inc(bank_free, 1)
        dense_act(act, "q_nope", q_nope)
        act.wait_ge(ct_done, 1)
        act.activation(c_tok[:, :, :].rearrange("p q c -> p (q c)"), psum[:, 7, :], ACT.Copy).then_inc(ct_read, 1)
        for h in range(HEADS):
            r = HD * (h % 2)
            act.wait_ge(ql_done, h + 1)
            act.activation(k_a[r:r + HD, h, :], psum[r:r + HD, 4 + h % 4, :], ACT.Copy).then_inc(ql_read, 1)
        for name in ("q_rope", "k_rope", "q_b", "k_b"):
            dense_act(act, name)
            if name == "q_b":
                rot2.wait(act, "k_rope", 0)
                for r, odd in ((HD, 0), (0, 1)):
                    for h in range(odd, HEADS, 2):
                        ins = act.activation(k_a[r:r + 32, h, :], k_r[r:r + 32, :], ACT.Copy)
                ins.then_inc(ql_read, 1)
        dense_act(act, "v_b", lambda e, i, j, bank: e.activation(
            v_b[:, j % 4, 256 * (j // 4):256 * (j // 4) + 256], psum[:, bank, 0:256], ACT.Copy).then_inc(bank_free, 1))

    def project_vector(dve):
        norm3.vector_split(dve, ready=lambda: None)
        rot2.vector(dve, "q_idx", 2)
        link(dve, dve.reciprocal(r1[:, :], erms[:, :]))
        for kt in range(KT):
            dve.scalar_tensor_tensor(out=res[:, kt, :], in0=res[:, kt, :], scalar=col("end1", kt), in1=r1[:, :],
                                     op0=ALU.mult, op1=ALU.mult).then_inc(x1_done, 1)
        rot2.vector(dve, "k_idx", 1)
        dve.wait_ge(kv_rooted, 1)
        dve.reciprocal(kv_rstd[:, :], kv_rms[:, :]).then_inc(kv_inverted, 1)
        dve.wait_ge(kv_inverted, 1)
        dve.scalar_tensor_tensor(out=c_kv[:, :], in0=c_kv[:, :], scalar=col("kv"), in1=kv_rstd[:, :],
                                 op0=ALU.mult, op1=ALU.mult).then_inc(kv_normed, 1)
        dve.wait_ge(bank_free, FIRST_TILE["ckv_wi"] + 2 + 4)
        for u, (qt, h, o, n) in enumerate(INDEX):
            dve.wait_ge(li_relu, u + 1)
            if h == 0:
                dve.tensor_scalar(bias[:, o:o + n], relu[u % 2][:, 0:n], w_eff[:, qt, h:h + 1], None, ALU.mult)\
                   .then_inc(li_added, 1)
            else:
                dve.wait_ge(li_added, u)
                dve.scalar_tensor_tensor(out=bias[:, o:o + n], in0=relu[u % 2][:, 0:n],
                                         scalar=w_eff[:, qt, h:h + 1], in1=bias[:, o:o + n],
                                         op0=ALU.mult, op1=ALU.add).then_inc(li_added, 1)

        def keep_eight(qt):
            o, n = SEG[P * (qt + 1)], P * (qt + 1)
            link(dve, dve.max(top8[:, :], bias[:, o:o + n]))
            link(dve, dve.match_replace(bias[:, o:o + n], top8[:, :], bias[:, o:o + n], -3e38))

        rounds8 = [qt for qt in range(1, TB) for _ in range(TOPK // 8)]
        turns8 = [lambda: rot2.vector(dve, "q_rope", 2, True), lambda: rot2.vector(dve, "k_rope", 1, True), lambda: rot2.vector(dve, "q_b", 2),
                  lambda: rot2.vector(dve, "k_b", 2)]
        dve.wait_ge(li_masked, TB - 1)
        done = 0
        for k, turn in enumerate(turns8):
            upto = len(rounds8) * (5, 8, 10, 12)[k] // 12
            for qt in rounds8[done:upto]:
                keep_eight(qt)
            done = upto
            turn()
        for qt in rounds8[done:]:
            keep_eight(qt)
        link(dve, dve.tensor_scalar(bias[:, 0:SEG[P]], bias[:, 0:SEG[P]], -2e38, -BIG, ALU.is_gt, ALU.mult))
        o = SEG[2 * P]
        link(dve, dve.tensor_scalar(bias[:, o:o + 2 * P], bias[:, o:o + 2 * P], -2e38, -BIG, ALU.is_gt, ALU.mult))

    def project_tensor(pe):
        dense_pe(pe, "q_idx", x_hi, x_lo, norm=norm3)
        dense_pe(pe, "k_idx", x_hi, x_lo)
        c0, t0 = FIRST_CHUNK["ckv_wi"], FIRST_TILE["ckv_wi"]
        wh = w_hi[c0 % RING][:, :].rearrange("p (m k n) -> p m k n", k=KT, n=P)
        wl = w_lo[c0 % RING][:, :].rearrange("p (m k n) -> p m k n", k=KT, n=P)
        pe.wait_ge(lo_ready, c0 + 1)
        pe.wait_ge(bank_free, t0 + 4)
        for kt in range(KT):
            mm = three_pass(pe, psum[:, t0 % 4, :], wh[:, 0, kt, :], wl[:, 0, kt, :], x_hi[:, kt, :], x_lo[:, kt, :],
                            kt == 0, kt == KT - 1)
        mm.then_inc(tile_done, 1)
        for q in range(TB):
            for kt in range(KT):
                tok = slice(q * P, (q + 1) * P)
                out = psum[:, (t0 + 1) % 4, q * HEADS:(q + 1) * HEADS]
                pe.matmul(out, x_hi[:, kt, tok], wh[:, 1, kt, 0:HEADS], start=(q == 0 and kt == 0), stop=False,
                          skip_group_check=True)
                pe.matmul(out, x_hi[:, kt, tok], wl[:, 1, kt, 0:HEADS], start=False, stop=False,
                          skip_group_check=True)
                mm = pe.matmul(out, x_lo[:, kt, tok], wh[:, 1, kt, 0:HEADS], start=False, stop=(kt == KT - 1),
                               skip_group_check=True)
        mm.then_inc(tile_done, 1)
        pe.wait_ge(bank_free, t0 + 1 + 4)
        pe.matmul(psum[:, 4, :], ones[:, :], kv_sq[:, :], start=True, stop=True).then_inc(kv_summed, 1)
        rot2.wait(pe, "k_idx", 0)
        pe.wait_ge(kv_rooted, 1)
        pe.wait_ge(x1_done, KT)
        for u, (qt, h, o, n) in enumerate(INDEX):
            r = HD * (h % 2)
            if u >= 4:
                pe.wait_ge(li_relu, u - 3)
            mm = pe.matmul(psum[:, 4 + u % 4, 0:n], q_i[r:r + HD, h // 2, qt * P:(qt + 1) * P],
                           k_i[r:r + HD, 0, 0:n], start=True, stop=True)
            mm.then_inc(li_done, 1)
        dense_pe(pe, "q_nope", x_hi, x_lo)
        pe.wait_ge(li_relu, len(INDEX))
        pe.wait_ge(kv_normed, 1)
        for q in range(TB):
            mm = pe.transpose(psum[:, 7, q * P:(q + 1) * P], c_kv[:, q * P:(q + 1) * P], ident[:, :])
        mm.then_inc(ct_done, 1)
        pe.wait_ge(proj_in, 32)
        pe.wait_ge(bank_free, FIRST_TILE["q_nope"] + 4 + 4)
        for h in range(HEADS):
            r = HD * (h % 2)
            if h == 3:
                pe.wait_ge(ct_read, 1)
            if h >= 4:
                pe.wait_ge(ql_read, h - 3)
            pe.matmul(psum[r:r + HD, 4 + h % 4, :], w_uk[:, h, :], c_kv[:, :], start=True, stop=True)\
              .then_inc(ql_done, 1)
        for name in ("q_rope", "k_rope", "q_b", "k_b"):
            dense_pe(pe, name, x_hi, x_lo)
        dense_pe(pe, "v_b", x_hi, x_lo, token_major=True)

    A_HEADS = 2 * HEADS
    score = [at(f"score{b}", 48 + 5 * b, [P, SPAN]) for b in range(2)]
    prob_t = [at(f"prob_t{b}", 58 + 5 * b, [P, SPAN]) for b in range(2)]
    dil_bias = at("dil_bias", 68, [P, SPAN])
    o_lat = [at(f"o_lat{b}", 73 + 2 * b, [P, S]) for b in range(2)]
    smax, snmax, ssum, sinv = ([at(f"{n}{b}", 77 + (4 * i + b) / 32, [P, TB]) for b in range(2)]
                               for i, n in enumerate(("smax", "snmax", "ssum", "sinv")))
    w_uv = at("w_uv", 92, [P, HEADS, HD])
    a_in, s_done, s_read, s_exp, s_inv, s_norm, s_norm_act, s_norm_pool, t_done, t_read, ol_done, ol_read, av_done, av_high, av_low = (
        sem("att_" + n) for n in ("in", "scores", "scores_read", "exp", "inverted", "normed", "normed_act",
                                  "normed_pool", "probs_t", "probs_t_read", "latents",
                                  "latents_read", "values", "values_high", "values_low"))
    def attend_sync(sp):
        sp.wait_ge(tile_done, FIRST_TILE["out2"])
        sp.dma_start(w_uv[:, :, :], d["w_uv"]).then_inc(a_in, 16)
        sp.dma_start(dil_bias[:, :], d["dil_bias"]).then_inc(a_in, 16)

    def attend_tensor(pe):
        def scores(h):
            for qt in reversed(range(TB)):
                if h >= 2 and qt >= TB - 2:
                    pe.wait_ge(t_read, 2 * (h - 1) - (qt == TB - 1))
                n = P * (qt + 1)
                o = SEG[n]
                out, q = Z[h % 2][:, o:o + n], slice(qt * P, (qt + 1) * P)
                if h < HEADS:
                    lhs, rhs = q_a[:, h, q], k_a[:, h, 0:n]
                else:
                    r, g = HD * (h % 2), h % HEADS // 2
                    lhs, rhs = q_b[r:r + HD, g, q], k_b[r:r + HD, g, 0:n]
                mm = pe.matmul(out, lhs, rhs, start=(qt != 0), stop=True, skip_group_check=True)
            mm.then_inc(s_done, 1)

        def transposes(h):
            for ready in (s_norm, s_norm_act, s_norm_pool):
                pe.wait_ge(ready, h + 1)
            for j in range(TB):
                o, n = span(j)
                for qt in range(j, TB):
                    src = SEG[P * (qt + 1)] + P * j
                    dst = o + P * (qt - j)
                    mm = pe.transpose(Z[h % 2][:, dst:dst + P], score[h % 2][:, src:src + P], ident[:, :])
                if j in (0, TB - 1):
                    mm.then_inc(t_done, 1)

        def values(h):
            r = HD * (h % 2)
            pe.wait_ge(t_read, 2 * h + 1)
            if h < HEADS:
                if h >= 1:
                    pe.wait_ge(ol_read, h)
                out = psum[:, 6, :]
            else:
                out = psum[r:r + HD, 7, :]
                if h % 2 == 0:
                    pe.wait_ge(av_low, h // 2)
            for j in range(TB):
                if j == 1:
                    pe.wait_ge(t_read, 2 * h + 2)
                o, n = span(j)
                lhs = c_tok[:, j, :] if h < HEADS else v_b[:, j, (h % HEADS) * HD:(h % HEADS + 1) * HD]
                mm = pe.matmul(out[:, S - n:S], lhs, prob_t[h % 2][:, o:o + n], start=(j == 0), stop=(j == TB - 1),
                               skip_group_check=True)
            mm.then_inc(ol_done if h < HEADS else av_done, 1)

        def from_latents(h):
            r = HD * (h % 2)
            pe.wait_ge(ol_read, h + 1)
            if h == 0:
                pe.wait_ge(a_in, 32)
            if h % 2 == 0 and h >= 2:
                pe.wait_ge(av_low, h // 2)
            pe.matmul(psum[r:r + HD, 7, :], w_uv[:, h, :], o_lat[h % 2][:, :], start=True, stop=True)\
              .then_inc(av_done, 1)
        pe.wait_ge(bank_free, FIRST_TILE["out2"] + 4)
        pe.wait_ge(ql_read, HEADS + 1)
        pe.wait_ge(fills, 6)
        rot2.wait(pe, "k_b", 1)
        scores(0)
        for h in range(A_HEADS + 1):
            if h + 1 < A_HEADS:
                scores(h + 1)
            if h < A_HEADS:
                transposes(h)
            if 2 <= h <= HEADS + 1:
                from_latents(h - 2)
            if h >= 1:
                values(h - 1)

    def attend_vector(dve):
        def low(p):
            dve.wait_ge(av_high, p + 1)
            dve.tensor_tensor(y_lo[:, p, :], psum[:, 7, :], y_hi[:, p, :].bitcast(F32), ALU.subtract)\
               .then_inc(av_low, 1)

        def softmax(h):
            b = h % 2
            scale = (HD + 32) ** -0.5 if h < HEADS else HD ** -0.5
            dve.wait_ge(s_done, h + 1)
            if h >= 2:
                dve.wait_ge(t_done, 2 * (h - 1))
            if h == 0:
                dve.wait_ge(proj_in, 32)
            if h == HEADS:
                dve.wait_ge(a_in, 32)
            for lo, hi, blocks in ((0, S, (3,)), (S, SPAN, (0, 1, 2))):
                link(dve, dve.tensor_tensor(score[b][:, lo:hi], Z[b][:, lo:hi], (bias if h < HEADS else dil_bias)[:, lo:hi],
                                            ALU.add))
                for qt in blocks:
                    n = P * (qt + 1)
                    ins = dve.tensor_reduce(smax[b][:, qt:qt + 1], score[b][:, SEG[n]:SEG[n] + n], AX.X, ALU.max)
                link(dve, ins)
                dve.tensor_scalar(snmax[b][:, blocks[0]:blocks[-1] + 1], smax[b][:, blocks[0]:blocks[-1] + 1], -scale, None,
                                  ALU.mult).then_inc(s_read, 1)

        def normalise(h):
            b = h % 2
            dve.wait_ge(s_exp, h + 1)
            dve.reciprocal(sinv[b][:, :], ssum[b][:, :]).then_inc(s_inv, 1)
            dve.wait_ge(s_inv, h + 1)
            for qt in range(2):
                n = P * (qt + 1)
                ins = dve.tensor_scalar(score[b][:, SEG[n]:SEG[n] + n], score[b][:, SEG[n]:SEG[n] + n],
                                        sinv[b][:, qt:qt + 1], None, ALU.mult)
            ins.then_inc(s_norm, 1)
        softmax(0)
        for h in range(A_HEADS):
            normalise(h)
            if h >= HEADS + 3 and h % 2 == 1:
                low(h // 2 - 1)
            if h + 1 < A_HEADS:
                softmax(h + 1)
            if 3 <= h < HEADS + 3 and h % 2 == 1:
                low(h // 2 - 1)
        low(A_HEADS // 2 - 1)

    def attend_scalar(act):
        def high(p):
            act.wait_ge(av_done, 2 * p + 2)
            act.activation(y_hi[:, p, :], psum[:, 7, :], ACT.Copy).then_inc(av_high, 1)

        def exp(h):
            b = h % 2
            scale = (HD + 32) ** -0.5 if h < HEADS else HD ** -0.5
            act.wait_ge(s_read, 2 * h + 1)
            for qt in reversed(range(TB)):
                if qt == TB - 2:
                    act.wait_ge(s_read, 2 * h + 2)
                n = P * (qt + 1)
                ins = act.activation(score[b][:, SEG[n]:SEG[n] + n], score[b][:, SEG[n]:SEG[n] + n], ACT.Exp,
                                     bias=snmax[b][:, qt:qt + 1], scale=scale, accum_out=ssum[b][:, qt:qt + 1])
            ins.then_inc(s_exp, 1)

        def normalise(h):
            b, n, o = h % 2, S, SEG[S]
            act.wait_ge(s_inv, h + 1)
            act.activation(score[b][:, o:o + n], score[b][:, o:o + n], ACT.Copy, scale=sinv[b][:, 3:4])\
               .then_inc(s_norm_act, 1)

        def copy_t(h):
            if h >= 2:
                act.wait_ge(ol_done, min(h - 1, HEADS))
            if h - 2 >= HEADS:
                act.wait_ge(av_done, h - 1)
            for part, (lo, hi) in enumerate(((0, S), (S, SPAN))):
                act.wait_ge(t_done, 2 * h + part + 1)
                act.activation(prob_t[h % 2][:, lo:hi], Z[h % 2][:, lo:hi], ACT.Copy).then_inc(t_read, 1)

        def copy_latents(h):
            act.wait_ge(ol_done, h + 1)
            if h >= 2:
                act.wait_ge(av_done, h - 1)
            act.activation(o_lat[h % 2][:, :], psum[:, 6, :], ACT.Copy).then_inc(ol_read, 1)
        exp(0)
        for h in range(A_HEADS):
            normalise(h)
            if h >= HEADS + 3 and h % 2 == 1:
                high(h // 2 - 1)
            copy_t(h)
            if h + 1 < A_HEADS:
                exp(h + 1)
            if 1 <= h <= HEADS:
                copy_latents(h - 1)
            if 3 <= h < HEADS + 3 and h % 2 == 1:
                high(h // 2 - 1)
        high(A_HEADS // 2 - 1)

    def attend_gpsimd(pool):
        for h in range(A_HEADS):
            b, n, o = h % 2, 3 * P, SEG[3 * P]
            pool.wait_ge(s_inv, h + 1)
            pool.tensor_scalar(score[b][:, o:o + n], score[b][:, o:o + n], sinv[b][:, 2:3], None, ALU.mult)\
                .then_inc(s_norm_pool, 1)

    with nc.Block() as block:
        @block.sync
        def _(sp):
            project_sync(sp)
            attend_sync(sp)

        @block.gpsimd
        def _(pool):
            project_gpsimd(pool)
            attend_gpsimd(pool)

        @block.scalar
        def _(act):
            project_scalar(act)
            attend_scalar(act)

        @block.vector
        def _(dve):
            project_vector(dve)
            attend_vector(dve)

        @block.tensor
        def _(pe):
            project_tensor(pe)
            attend_tensor(pe)


    norm_cross = Norm("norm_cross", res, "cross", 160, hi=x_hi, lo=x_lo, bank=4)
    norm_mlp = Norm("norm_mlp", res, "mlp", 160, hi=x_hi, lo=x_lo, bank=4)
    qc = at("q_cross", 160, [P, KT, S])
    kc = at("k_cross", 176, [P, KT, MEM])
    vc = at("v_cross", 184, [P, MEM // P, D])
    cs = [at(f"cross_score{b}", 144 + 4 * b, [P, TB, MEM]) for b in range(2)]
    ct = [at(f"cross_prob_t{b}", 152 + 4 * b, [P, MEM // P, S]) for b in range(2)]
    cmx, cnm, csm, cin = ([at(f"{n}{b}", 192 + (4 * i + b) / 32, [P, TB]) for b in range(2)]
                          for i, n in enumerate(("cmax", "cnmax", "csum", "cinv")))
    cs_done, cs_max, cs_exp, cs_norm, ct_done2, ct_read2, cv_done, cv_high, cv_low = (
        sem("cross_" + n) for n in ("scores", "max", "exp", "normed", "probs_t", "probs_t_read", "values",
                                    "values_high", "values_low"))

    with nc.Block() as block:
        names = ("out2", "q_cross", "o_cross")

        @block.sync
        def _(sp):
            sp.dma_start(kc[:, :, :], kc_rows).then_inc(kv_moved, 16)
            sp.dma_start(vc[:, :, :], vc_rows).then_inc(kv_moved, 16)
            for name in names:
                dense_sync(sp, name)

        @block.gpsimd
        def _(pool):
            for name in names:
                dense_pool(pool, name)

        @block.scalar
        def _(act):
            residual_act(act, "out2", norm_cross)
            norm_cross.act_split(act)
            dense_act(act, "q_cross", lambda e, i, j, bank: e.activation(
                qc[:, bass.ds(4 * i + j, 1), :], psum[:, bank:bank + 1, :], ACT.Copy).then_inc(bank_free, 1))

            def exp(h):
                act.wait_ge(cs_max, h + 1)
                for q in range(TB):
                    ins = act.activation(cs[h % 2][:, q, :], flat[:, 1024 * (h % 2) + 256 * q:1024 * (h % 2) + 256 * (q + 1)],
                                         ACT.Exp, bias=cnm[h % 2][:, q:q + 1], scale=CH_DIM ** -0.5,
                                         accum_out=csm[h % 2][:, q:q + 1])
                ins.then_inc(cs_exp, 1)

            def copy_t(h):
                act.wait_ge(ct_done2, h + 1)
                if h >= 2:
                    act.wait_ge(cv_done, 2 * (h - 1))
                act.activation(ct[h % 2][:, :, :].rearrange("p m n -> p (m n)"), flat[:, 2048:3072], ACT.Copy)\
                   .then_inc(ct_read2, 1)

            def high(t):
                act.wait_ge(cv_done, t + 1)
                act.activation(y_hi[:, t, :], psum[:, 6 + t % 2, :], ACT.Copy).then_inc(cv_high, 1)
            exp(0)
            for h in range(CH_HEADS):
                if h + 1 < CH_HEADS:
                    exp(h + 1)
                copy_t(h)
                high(2 * h)
                high(2 * h + 1)
            residual_act(act, "o_cross", norm_mlp)

        @block.vector
        def _(dve):
            add_residual(dve, "out2", norm_cross)
            norm_cross.vector_split(dve)

            def top(h):
                b = h % 2
                dve.wait_ge(cs_done, h + 1)
                link(dve, dve.tensor_reduce(cmx[b][:, :], flat[:, 1024 * b:1024 * b + 1024]
                                            .rearrange("p (q n) -> p q n", n=MEM), AX.X, ALU.max))
                dve.tensor_scalar(cnm[b][:, :], cmx[b][:, :], -CH_DIM ** -0.5, None, ALU.mult).then_inc(cs_max, 1)

            def normalise(h):
                b = h % 2
                dve.wait_ge(cs_exp, h + 1)
                link(dve, dve.reciprocal(cin[b][:, :], csm[b][:, :]))
                dve.tensor_tensor(cs[b][:, :, :], cs[b][:, :, :], wide(cin[b][:, :], [P, TB, MEM], 2), ALU.mult)\
                   .then_inc(cs_norm, 1)

            def low(t):
                dve.wait_ge(cv_high, t + 1)
                dve.tensor_tensor(y_lo[:, t, :], psum[:, 6 + t % 2, :], y_hi[:, t, :].bitcast(F32), ALU.subtract)\
                   .then_inc(cv_low, 1)
            top(0)
            for h in range(CH_HEADS):
                if h + 1 < CH_HEADS:
                    top(h + 1)
                normalise(h)
                if h >= 1:
                    low(2 * h - 2)
                    low(2 * h - 1)
            low(KT - 2)
            low(KT - 1)
            add_residual(dve, "o_cross", norm_mlp)

        @block.tensor
        def _(pe):
            dense_pe(pe, "out2", y_hi, y_lo)
            norm_cross.pe(pe)
            dense_pe(pe, "q_cross", x_hi, x_lo, norm=norm_cross)
            pe.wait_ge(bank_free, FIRST_TILE["o_cross"] + 4)
            pe.wait_ge(kv_moved, 64)

            def scores(h):
                b = h % 2
                if h >= 2:
                    pe.wait_ge(cs_exp, h - 1)
                for q in range(TB):
                    for half in range(2):
                        mm = pe.matmul(flat[:, 1024 * b + 256 * q:1024 * b + 256 * (q + 1)],
                                       qc[:, 2 * h + half, q * P:(q + 1) * P], kc[:, 2 * h + half, :],
                                       start=(half == 0 and q % 2 == 0), stop=(half == 1), skip_group_check=True)
                mm.then_inc(cs_done, 1)

            def transposes(h):
                pe.wait_ge(cs_norm, h + 1)
                if h >= 1:
                    pe.wait_ge(ct_read2, h)
                for m in range(MEM // P):
                    for q in range(TB):
                        mm = pe.transpose(psum[:, 4 + m, q * P:(q + 1) * P], cs[h % 2][:, q, m * P:(m + 1) * P], ident[:, :])
                mm.then_inc(ct_done2, 1)

            def values(h):
                pe.wait_ge(ct_read2, h + 1)
                for half in range(2):
                    if h >= 1:
                        pe.wait_ge(cv_low, 2 * h - 1 + half)
                    for m in range(MEM // P):
                        o = CH_DIM * h + P * half
                        mm = pe.matmul(psum[:, 6 + half, :], vc[:, m, o:o + P], ct[h % 2][:, m, :], start=(m == 0),
                                       stop=(m == 1))
                    mm.then_inc(cv_done, 1)
            scores(0)
            scores(1)
            for h in range(CH_HEADS):
                transposes(h)
                if h + 2 < CH_HEADS:
                    scores(h + 2)
                values(h)
            pe.wait_ge(cv_low, KT)
            dense_pe(pe, "o_cross", y_hi, y_lo)
            norm_mlp.pe(pe)

    G = 4
    f_hi = [y_hi, at("f_hi", 144, [P, KT, S], FR)]
    f_lo = [y_lo, at("f_lo", 160, [P, KT, S], FR)]
    f_relu = [at(f"f_relu{b}", 176 + 2 * b, [P, S]) for b in range(4)]
    f_sq = [at(f"f_sq{b}", 196 + 2 * b, [P, S]) for b in range(2)]
    norm_end2 = Norm("norm_end2", res, "final", 184, out=res, bank=4)
    f_squared, f_high, f_low, stored = sem("mlp_squared"), sem("mlp_high"), sem("mlp_low"), sem("stored")
    ORDER = [n for n, _ in LAYERS[-2 * G:]]
    LAST = ORDER[-1]
    with nc.Block() as block:
        @block.sync
        def _(sp):
            for name in ORDER:
                dense_sync(sp, name)
            for k in range(4):
                norm_end2.wait_scaled(sp, 2 * (k + 1))
                sp.dma_start(d["out"][:, 2 * k:2 * k + 2, :], res[:, 2 * k:2 * k + 2, :]).then_inc(stored, 16)
            sp.wait_ge(stored, 64)

        @block.gpsimd
        def _(pool):
            for name in ORDER[:-1]:
                dense_pool(pool, name)
            for b in range(RING):
                split_lo(pool, FIRST_CHUNK[LAST] + 2 + b)

        @block.scalar
        def _(act):
            norm_mlp.act_split(act)
            for name in ORDER:
                t0, c0, g = FIRST_TILE[name], FIRST_CHUNK[name], int(name[-1])
                if name[:2] == "up":
                    act.wait_ge(bank_free, t0 + 4)
                    for t in range(KT):
                        act.wait_ge(tile_done, t0 + t + 1)
                        if KT * g + t >= 4:
                            act.wait_ge(f_squared, KT * g + t - 3)
                        act.activation(f_relu[t % 4][:, :], psum[:, (t0 + t) % 4, :], ACT.Relu).then_inc(bank_free, 1)
                        act.wait_ge(bank_free, t0 + t + 5)
                        act.activation(f_hi[g % 2][:, t, :], f_relu[t % 4][:, :], ACT.Square).then_inc(f_high, 1)
                        if t % 2 == 1:
                            split_hi(act, c0 + 2 + t // 2, t0 + t + 1)
                elif name != LAST:
                    dense_act(act, name)
                else:
                    residual_act(act, name, norm_end2)

        @block.vector
        def _(dve):
            def low(g, t):
                dve.wait_ge(f_high, KT * g + t + 1)
                dve.wait_ge(f_squared, KT * g + t + 1)
                dve.tensor_tensor(f_lo[g % 2][:, t, :], f_sq[t % 2][:, :], f_hi[g % 2][:, t, :].bitcast(F32),
                                  ALU.subtract).then_inc(f_low, 1)
            norm_mlp.vector_split(dve)
            for name in ORDER:
                t0, g = FIRST_TILE[name], int(name[-1])
                if name[:2] == "up":
                    for t in range(KT):
                        dve.wait_ge(bank_free, t0 + t + 5)
                        if KT * g + t >= 2:
                            dve.wait_ge(f_low, KT * g + t - 1)
                        dve.tensor_tensor(f_sq[t % 2][:, :], f_relu[t % 4][:, :], f_relu[t % 4][:, :], ALU.mult)\
                           .then_inc(f_squared, 1)
                        if t >= 1:
                            low(g, t - 1)
                    low(g, KT - 1)
                else:
                    add_residual(dve, name, norm_end2 if name == LAST else None)
            norm_end2.vector_split(dve)

        @block.tensor
        def _(pe):
            for name in ORDER:
                g = int(name[-1])
                if name[:2] == "up":
                    dense_pe(pe, name, x_hi, x_lo, norm=norm_mlp if g == 0 else None)
                else:
                    pe.wait_ge(f_low, KT * (g + 1))
                    dense_pe(pe, name, f_hi[g % 2], f_lo[g % 2])
            norm_end2.pe(pe)


def _chunks(w, kts=KT):
    k, n = w.shape
    per = CHUNK_COLS // (kts * P)
    w = w.reshape(kts, P, n // (per * P), per, P)
    return np.ascontiguousarray(w.transpose(2, 1, 3, 0, 4)).reshape(-1, P, CHUNK_COLS)


def _halves(width, heads, first):
    c = np.arange(width * heads).reshape(heads, 2, width // 2) + first * width
    return [c[:, 0].ravel(), c[:, 1].ravel()]


def _pad(w, n):
    return np.concatenate([w, np.zeros((w.shape[0], n - w.shape[1]), w.dtype)], axis=1)


def _cols(g):
    return np.asarray(g).reshape(-1, P).T


def _layout(v):
    a = {k: np.asarray(x) for k, x in v.items()}
    w_in, w_in2 = a["w_in"][0], a["w_in_2"][0]
    rope_half = [np.concatenate(_halves(HD, 4, 0)), np.concatenate(_halves(HD, 4, 4))]
    rh = np.concatenate(rope_half)
    o = np.cumsum([0, 512, 512, 512, 512, 512, 1024, 1024])
    wg, wd, wu = a["w_gate"][0], a["w_down_2"][0], a["w_up_2"][0]
    o2 = np.cumsum([0, 512, 256, 128, 32, 512, 64, 8, 512, 512, 512])
    r = np.arange(256).reshape(8, 32)
    swapped = np.concatenate([r[:, 16:], r[:, :16]], axis=1)
    qr = np.concatenate([r[:4].ravel(), swapped[:4].ravel(), r[4:].ravel(), swapped[4:].ravel()])
    kr = np.concatenate([np.tile(r[0], 4), np.tile(swapped[0], 4)])
    ki = np.concatenate([np.tile(np.arange(32), 4), np.tile(np.arange(32, 64), 4)])
    wkv = a["w_kv_cross_2"][0]
    parts = {
        "sb_q": w_in[:, o[0]:o[1]], "sb_k": w_in[:, o[1]:o[2]], "sb_v": w_in[:, o[2]:o[3]],
        "gate_sb": wg[:, :D], "sb_out": a["w_sb_out"][0],
        "ret_q": w_in[:, o[3] + rh], "ret_k": w_in[:, o[4] + rh], "ret_v": w_in[:, o[5]:o[6]],
        "ret_g": w_in[:, o[6]:o[7]], "gate_ret": wg[:, D:], "ret_out": a["w_ret_out"][0], "out": a["w_out"][0],
        "q_nope": w_in2[:, o2[0]:o2[1]], "q_rope": w_in2[:, o2[1] + qr], "k_rope": w_in2[:, o2[3] + kr],
        "ckv_wi": _pad(np.concatenate([w_in2[:, o2[2]:o2[3]], w_in2[:, o2[6]:o2[7]]], axis=1), 256),
        "q_idx": w_in2[:, o2[4] + rh], "k_idx": w_in2[:, o2[5] + ki],
        "q_b": w_in2[:, o2[7] + rh], "k_b": w_in2[:, o2[8] + rh], "v_b": w_in2[:, o2[9]:o2[10]],
        "out2": a["w_out_2"][0], "q_cross": a["w_q_cross_2"][0], "k_mem": wkv[:, :D], "v_mem": wkv[:, D:],
        "o_cross": a["w_o_cross_2"][0],
    }
    for g in range(4):
        parts[f"up{g}"] = wu[:, g * D:(g + 1) * D]
        parts[f"down{g}"] = wd[g * D:(g + 1) * D, :]
    w_dense = np.concatenate([_chunks(parts[n], 4 if n == "sb_out" else KT) for n, _ in LAYERS])
    assert w_dense.shape[0] == N_CHUNKS

    def expert(w, k, n):
        return w[0].reshape(NE, 2, k // 256, P, n).transpose(0, 1, 3, 2, 4).reshape(NE, 2, P, CHUNK_COLS)
    ge, ue = expert(a["w_exp_gate"], D, FF), expert(a["w_exp_up"], D, FF)
    de = expert(a["w_exp_down"], FF, D)
    gu = np.concatenate([ge, ue], axis=1).reshape(PAIRS, 8, P, CHUNK_COLS)
    w_moe = np.concatenate([gu, de.reshape(PAIRS, 4, P, CHUNK_COLS)], axis=1)

    f32 = np.float32
    params = np.concatenate([_cols(a["norm_mix_g"]), _cols(a["b_gate"]), _cols(a["ret_norm_g"]), _cols(a["norm_ffn_g"]),
                             _cols(a["norm_final_g"]),
                             _cols(a["norm_mix_g_2"]), _cols(a["kv_norm_g_2"]), _cols(a["norm_cross_g_2"]),
                             _cols(a["norm_mem_g_2"]), _cols(a["norm_mlp_g_2"]), _cols(a["norm_final_g_2"]),
                             np.full((P, 1), EPS, f32)], axis=1)
    pos = np.arange(S, dtype=f32)

    def angle(n):
        inv = np.power(f32(10000.0), -np.arange(n, dtype=f32) / f32(n)).astype(f32)
        return (pos[None, :] * inv[np.arange(P) % n][:, None]).astype(f32).astype(np.float64)
    sign = np.where(np.arange(P) % 32 < 16, -1.0, 1.0)[:, None]
    i = np.arange(P)
    log_gamma = np.log(1.0 - 2.0 ** (-5.0 - np.arange(HEADS)))
    cc = np.arange(S)
    dist = np.abs(cc[None, :] - i[:, None])
    seen = cc[None, :] // 64 >= i[:, None] // 64
    decay = np.exp(log_gamma[:, None, None] * dist) * seen * HD ** -0.5
    rel = (np.arange(S)[:, None] - np.arange(S)[None, :])
    count = ((rel >= 0) & (rel <= 128)).astype(float) + ((rel >= 0) & (rel % 4 == 0)) + ((rel >= 0) & (rel % 16 == 0))
    dil = np.where(count > 0, np.log(np.maximum(count, 1)) * HD ** 0.5, -BIG)
    dil_bias = np.zeros((P, SPAN))
    causal = np.zeros((P, SPAN))
    for q in range(TB):
        n = P * (q + 1)
        dil_bias[:, SEG[n]:SEG[n] + n] = dil[q * P:(q + 1) * P, :n]
        causal[:, SEG[n]:SEG[n] + n] = np.where(rel[q * P:(q + 1) * P, :n] >= 0, 0, -BIG)
    wuk, wuv = a["w_uk_2"][0], a["w_uv_2"][0]
    small = np.concatenate([a["w_group_router"][0], a["w_expert_router"][0]], axis=1)
    return {
        "x": np.ascontiguousarray(a["x"][0].T.reshape(KT, P, S).transpose(1, 0, 2)),
        "mem": np.ascontiguousarray(a["mem_2"][0].T.reshape(KT, P, MEM).transpose(1, 0, 2)),
        "w_dense": w_dense, "w_moe": np.ascontiguousarray(w_moe[:, MOE_AHEAD:]),
        "w_moe_ahead": np.roll(w_moe[:, :MOE_AHEAD], -1, axis=0), "cols": np.ascontiguousarray(params),
        "w_router": np.ascontiguousarray(small.reshape(KT, P, NR).transpose(1, 0, 2)),
        "b_router": np.ascontiguousarray(np.broadcast_to(
            np.concatenate([a["b_group_router"][0], a["b_expert_router"][0]])[None, :], (P, NR))),
        "w_uk": np.ascontiguousarray(wuk.transpose(2, 0, 1)),
        "w_uv": np.ascontiguousarray(wuv.transpose(1, 0, 2)),
        "ident": np.eye(P, dtype=f32), "neg_tri": -(i[:, None] >= i[None, :]).astype(f32),
        "before": (i[:, None] < i[None, :]).astype(f32),
        "cos64": np.cos(angle(FREQ)).astype(f32), "sin64": np.sin(angle(FREQ)).astype(f32),
        "cos32": np.cos(angle(FREQ_R)).astype(f32), "sin32": (sign * np.sin(angle(FREQ_R))).astype(f32),
        "decay": decay.astype(f32), "dil_bias": dil_bias.astype(f32), "causal": causal.astype(f32),
        "ranks": np.broadcast_to(np.concatenate([4.0 - np.arange(4), 16.0 - np.arange(16), np.arange(16)]),
                                 (P, 36)).astype(f32),
        "dest": (np.arange(2)[None, :, None] * S + np.arange(TB)[None, None, :] * P + i[:, None, None]).astype(np.int32),
        "empty": np.broadcast_to(2 * S + i[:, None], (P, NE * TB + 2)).astype(np.int32),
    }


def kernel(**inputs):
    import concourse.bacc as _bacc
    from concourse.bass_utils import run_bass_kernel_spmd as _run

    nc = _bacc.Bacc("TRN2", target_bir_lowering=False, num_devices=1)
    arrays, d = {}, {}
    for name, a in _layout(inputs).items():
        arrays[f"in_{name}"] = a
        d[name] = nc.dram_tensor(f"in_{name}", a.shape, mybir.dt.from_np(a.dtype), kind="ExternalInput").ap()
    d["out"] = nc.dram_tensor("out", [P, KT, S], F32, kind="ExternalOutput").ap()
    build(nc, d)
    r = _run(nc, [arrays], core_ids=[0])
    got = r.results[0]["out"]
    return got.transpose(1, 0, 2).reshape(D, S).T[None]
```
